# Optimizing a Trainium2 kernel written in Bass

```python
import jax, jax.numpy as jnp
from jax import lax
import numpy as np

D_MODEL = 2048
BATCH = 1
SEQ = 256
DEPTH = 1
DEC_BATCH = 1
DEC_SEQ = 32
PAST_LEN = 512

CHUNK = 64
N_HEADS = 16
HEAD_DIM = 128
SB_WIDTH = N_HEADS * HEAD_DIM
SB_SCALE = HEAD_DIM ** -0.5
Q_BLOCK = 128
LRU_WIDTH = D_MODEL
LRU_BLOCKS = 16
LRU_BLOCK_W = LRU_WIDTH // LRU_BLOCKS
CONV_W = 4
LRU_C = 8.0
N_GROUPS = 4
EXPERTS_PER_GROUP = 4
N_EXPERTS = N_GROUPS * EXPERTS_PER_GROUP
TOP_K = 2
EXPERT_FF = 512
NORM_EPS = 1e-6
IN_COLS = 3 * SB_WIDTH + 2 * LRU_WIDTH + 2 * D_MODEL

kernel_name = 'sb_rglru_hmoe_stream_step'

def rmsnorm(x, g):
    xf = x.astype(jnp.float32)
    y = xf * lax.rsqrt(jnp.mean(xf * xf, axis=-1, keepdims=True) + NORM_EPS)
    return (y * g.astype(jnp.float32)).astype(x.dtype)

def sb_block(q, k, v, q_start):
    tq, lk = q.shape[1], k.shape[1]
    z = jnp.einsum('bqhd,bkhd->bhqk', q.astype(jnp.float32), k.astype(jnp.float32)) * SB_SCALE
    q_pos = q_start + jnp.arange(tq)[:, None]
    k_pos = jnp.arange(lk)[None, :]
    mask = k_pos < q_pos
    log_keep = jnp.where(mask, jax.nn.log_sigmoid(-z), 0.0)
    log_rest = lax.cumsum(log_keep, axis=3, reverse=True) - log_keep
    weights = jnp.where(mask, jnp.exp(jax.nn.log_sigmoid(z) + log_rest), 0.0)
    return jnp.einsum('bhqk,bkhd->bqhd', weights.astype(v.dtype), v)

def sb_attention(q, k, v, q_offset):
    tq = q.shape[1]
    outs = []
    for b0 in range(0, tq, Q_BLOCK):
        b1 = min(b0 + Q_BLOCK, tq)
        kend = q_offset + b1
        outs.append(sb_block(q[:, b0:b1], k[:, :kend], v[:, :kend], q_offset + b0))
    return jnp.concatenate(outs, axis=1)

def causal_conv(xb, prev, w, b):
    t = xb.shape[1]
    xpad = jnp.concatenate([prev.astype(xb.dtype), xb], axis=1)
    out = b
    for tap in range(CONV_W):
        out = out + xpad[:, tap:tap + t] * w[tap]
    return out, xpad[:, -(CONV_W - 1):]

def _lin_combine(left, right):
    a_l, b_l = left
    a_r, b_r = right
    return a_l * a_r, a_r * b_l + b_r

def rg_lru(xc, h0, wa, ba, wx, bx, lam):
    bn, t, _ = xc.shape
    xf = xc.astype(jnp.float32)
    xblk = xf.reshape(bn, t, LRU_BLOCKS, LRU_BLOCK_W)
    r = jax.nn.sigmoid(jnp.einsum('btnc,ncd->btnd', xblk, wa.astype(jnp.float32)).reshape(bn, t, LRU_WIDTH) + ba.astype(jnp.float32))
    i = jax.nn.sigmoid(jnp.einsum('btnc,ncd->btnd', xblk, wx.astype(jnp.float32)).reshape(bn, t, LRU_WIDTH) + bx.astype(jnp.float32))
    log_a = LRU_C * r * jax.nn.log_sigmoid(lam.astype(jnp.float32))
    a = jnp.exp(log_a)
    u = jnp.sqrt(-jnp.expm1(2.0 * log_a)) * (i * xf)
    u = u.at[:, 0].add(a[:, 0] * h0.astype(jnp.float32))
    _, h = lax.associative_scan(_lin_combine, (a, u), axis=1)
    return h.astype(xc.dtype), h[:, -1].astype(xc.dtype)

def hmoe(h, wg, bg, ws, bs, wu, wd):
    bn, t, d = h.shape
    hf = h.reshape(-1, d)
    g_logits = (hf @ wg).astype(jnp.float32) + bg.astype(jnp.float32)
    g_prob = jax.nn.softmax(g_logits, axis=-1)
    _, g_idx = lax.top_k(g_logits, 1)
    p_g = jnp.take_along_axis(g_prob, g_idx, axis=1)
    sub = jnp.einsum('nd,gde->nge', hf, ws).astype(jnp.float32) + bs.astype(jnp.float32)
    sub_sel = jnp.einsum('nge,ng->ne', sub, jax.nn.one_hot(g_idx[:, 0], N_GROUPS, dtype=jnp.float32))
    e_val, e_idx = lax.top_k(sub_sel, TOP_K)
    e_w = jax.nn.softmax(e_val, axis=-1) * p_g
    e_id = g_idx * EXPERTS_PER_GROUP + e_idx
    combine = jnp.sum(jax.nn.one_hot(e_id, N_EXPERTS, dtype=jnp.float32) * e_w[..., None], axis=1).astype(h.dtype)
    out = jnp.zeros_like(hf)
    for e in range(N_EXPERTS):
        gate, up = jnp.split(hf @ wu[e], 2, axis=-1)
        out = out + combine[:, e:e + 1] * ((jax.nn.silu(gate) * up) @ wd[e])
    return out.reshape(bn, t, d)

def run_trunk(x, past_k, past_v, conv_prev, h_prev, params):
    (norm1_g, w_in, conv_w, conv_b, lru_wa, lru_ba, lru_wx, lru_bx, lru_lambda,
     w_pa, w_pb, w_o, norm2_g, router_group_w, router_group_b, router_sub_w,
     router_sub_b, expert_w_up, expert_w_down, final_norm_g) = params
    bn, t, _ = x.shape
    q_offset = 0 if past_k is None else past_k.shape[2]
    splits = [SB_WIDTH, 2 * SB_WIDTH, 3 * SB_WIDTH, 3 * SB_WIDTH + LRU_WIDTH,
              3 * SB_WIDTH + 2 * LRU_WIDTH, 3 * SB_WIDTH + 2 * LRU_WIDTH + D_MODEL]
    ks, vs, convs, hs = [], [], [], []
    for l in range(DEPTH):
        h = rmsnorm(x, norm1_g[l])
        proj = h @ w_in[l]
        q, k, v, xb, yg, ga, gb = jnp.split(proj, splits, axis=-1)
        q = q.reshape(bn, t, N_HEADS, HEAD_DIM)
        k = k.reshape(bn, t, N_HEADS, HEAD_DIM)
        v = v.reshape(bn, t, N_HEADS, HEAD_DIM)
        if past_k is None:
            k_all, v_all = k, v
        else:
            k_all = jnp.concatenate([past_k[l].astype(k.dtype), k], axis=1)
            v_all = jnp.concatenate([past_v[l].astype(v.dtype), v], axis=1)
        o_a = sb_attention(q, k_all, v_all, q_offset).reshape(bn, t, SB_WIDTH)
        xc, conv_new = causal_conv(xb, conv_prev[l], conv_w[l], conv_b[l])
        h_seq, h_last = rg_lru(xc, h_prev[l], lru_wa[l], lru_ba[l], lru_wx[l], lru_bx[l], lru_lambda[l])
        o_b = jax.nn.gelu(yg) * h_seq
        mixed = jax.nn.sigmoid(ga) * (o_a @ w_pa[l]) + jax.nn.sigmoid(gb) * (o_b @ w_pb[l])
        x = x + mixed @ w_o[l]
        x = x + hmoe(rmsnorm(x, norm2_g[l]), router_group_w[l], router_group_b[l], router_sub_w[l],
                     router_sub_b[l], expert_w_up[l], expert_w_down[l])
        ks.append(k)
        vs.append(v)
        convs.append(conv_new)
        hs.append(h_last)
    return rmsnorm(x, final_norm_g), jnp.stack(ks), jnp.stack(vs), jnp.stack(convs), jnp.stack(hs)

def setup_inputs(seed: int = 0) -> dict:
    key = jax.random.key(seed)
    ks = jax.random.split(key, 26)
    f32 = jnp.float32

    def nrm(k, shape, scale):
        return jax.random.normal(k, shape, f32) * scale

    u = jax.random.uniform(ks[13], (DEPTH, LRU_WIDTH), f32, minval=0.9, maxval=0.999)
    s = u ** (1.0 / LRU_C)
    lam = jnp.log(s) - jnp.log1p(-s)
    return {
        'x_prompt': nrm(ks[0], (BATCH, SEQ, D_MODEL), 1.0),
        'x_sample': nrm(ks[1], (DEC_BATCH, DEC_SEQ, D_MODEL), 1.0),
        'cache_k': nrm(ks[2], (DEPTH, DEC_BATCH, PAST_LEN, N_HEADS, HEAD_DIM), 1.0),
        'cache_v': nrm(ks[3], (DEPTH, DEC_BATCH, PAST_LEN, N_HEADS, HEAD_DIM), 1.0),
        'state_conv': nrm(ks[4], (DEPTH, DEC_BATCH, CONV_W - 1, LRU_WIDTH), 1.0),
        'state_lru': nrm(ks[5], (DEPTH, DEC_BATCH, LRU_WIDTH), 0.5),
        'norm1_g': 1.0 + nrm(ks[6], (DEPTH, D_MODEL), 0.02),
        'w_in': nrm(ks[7], (DEPTH, D_MODEL, IN_COLS), D_MODEL ** -0.5),
        'conv_w': nrm(ks[8], (DEPTH, CONV_W, LRU_WIDTH), CONV_W ** -0.5),
        'conv_b': nrm(ks[9], (DEPTH, LRU_WIDTH), 0.02),
        'lru_wa': nrm(ks[10], (DEPTH, LRU_BLOCKS, LRU_BLOCK_W, LRU_BLOCK_W), LRU_BLOCK_W ** -0.5),
        'lru_ba': nrm(ks[11], (DEPTH, LRU_WIDTH), 0.02),
        'lru_wx': nrm(ks[12], (DEPTH, LRU_BLOCKS, LRU_BLOCK_W, LRU_BLOCK_W), LRU_BLOCK_W ** -0.5),
        'lru_bx': nrm(ks[14], (DEPTH, LRU_WIDTH), 0.02),
        'lru_lambda': lam,
        'w_pa': nrm(ks[15], (DEPTH, SB_WIDTH, D_MODEL), SB_WIDTH ** -0.5),
        'w_pb': nrm(ks[16], (DEPTH, LRU_WIDTH, D_MODEL), LRU_WIDTH ** -0.5),
        'w_o': nrm(ks[17], (DEPTH, D_MODEL, D_MODEL), D_MODEL ** -0.5),
        'norm2_g': 1.0 + nrm(ks[18], (DEPTH, D_MODEL), 0.02),
        'router_group_w': nrm(ks[19], (DEPTH, D_MODEL, N_GROUPS), D_MODEL ** -0.5),
        'router_group_b': nrm(ks[20], (DEPTH, N_GROUPS), 0.01),
        'router_sub_w': nrm(ks[21], (DEPTH, N_GROUPS, D_MODEL, EXPERTS_PER_GROUP), D_MODEL ** -0.5),
        'router_sub_b': nrm(ks[22], (DEPTH, N_GROUPS, EXPERTS_PER_GROUP), 0.01),
        'expert_w_up': nrm(ks[23], (DEPTH, N_EXPERTS, D_MODEL, 2 * EXPERT_FF), D_MODEL ** -0.5),
        'expert_w_down': nrm(ks[24], (DEPTH, N_EXPERTS, EXPERT_FF, D_MODEL), EXPERT_FF ** -0.5),
        'final_norm_g': 1.0 + nrm(ks[25], (D_MODEL,), 0.02),
    }

def reference(x_prompt, x_sample, cache_k, cache_v, state_conv, state_lru, norm1_g, w_in,
              conv_w, conv_b, lru_wa, lru_ba, lru_wx, lru_bx, lru_lambda, w_pa, w_pb, w_o,
              norm2_g, router_group_w, router_group_b, router_sub_w, router_sub_b,
              expert_w_up, expert_w_down, final_norm_g):
    params = (norm1_g, w_in, conv_w, conv_b, lru_wa, lru_ba, lru_wx, lru_bx, lru_lambda,
              w_pa, w_pb, w_o, norm2_g, router_group_w, router_group_b, router_sub_w,
              router_sub_b, expert_w_up, expert_w_down, final_norm_g)
    bp = x_prompt.shape[0]
    zero_conv = jnp.zeros((DEPTH, bp, CONV_W - 1, LRU_WIDTH), x_prompt.dtype)
    zero_lru = jnp.zeros((DEPTH, bp, LRU_WIDTH), x_prompt.dtype)
    y_prompt, prompt_k, prompt_v, prompt_conv, prompt_lru = run_trunk(
        x_prompt, None, None, zero_conv, zero_lru, params)
    y_sample, sample_k, sample_v, sample_conv, sample_lru = run_trunk(
        x_sample, cache_k, cache_v, state_conv, state_lru, params)
    return (y_prompt, y_sample, prompt_k, prompt_v, prompt_conv, prompt_lru,
            sample_k, sample_v, sample_conv, sample_lru)


_drawn_inputs = setup_inputs


def setup_inputs(seed=0):
    import zlib

    import numpy as np

    out = dict(_drawn_inputs(seed))
    spreads = {}
    factors = {'lru_ba': 8.0,
     'lru_bx': 7.929,
     'norm2_g': 3.032,
     'router_sub_b': 8.0,
     'final_norm_g': 2.72}
    for name, (base, spread) in spreads.items():
        noise = np.random.default_rng([zlib.crc32(name.encode()), seed]).standard_normal(out[name].shape)
        drawn = base * np.exp(spread * noise) if base else spread * noise
        out[name] = __import__('jax').numpy.asarray(drawn.astype(out[name].dtype))
    for name, factor in factors.items():
        out[name] = (out[name] * factor).astype(out[name].dtype)
    return out
```

```python
from contextlib import ExitStack

import concourse.bass as bass
from concourse import mybir

F32 = mybir.dt.float32
BF16 = mybir.dt.bfloat16
I32 = mybir.dt.int32
ALU = mybir.AluOpType
ACT = mybir.ActivationFunctionType
AX = mybir.AxisListType

P = 128
D = 2048
KT = D // P
TP, TS = 256, 32
T = TP + TS
FT = 3
ROWS = [P, P, TS]
H = 16
PAST = 512
SCALE = float(P) ** -0.5
CONV = 4
HIST = CONV - 1
XW = HIST + TP + HIST + TS
CW = TP + HIST + TS
S0 = TP + HIST
NG, EPG, FF = 4, 4, 512
NE = NG * EPG
FM = FF // P
CAP = 96
CHUNKS = T // CAP
EPS = 1e-6
LRU_C = 8.0
NEG = -1.0e30
RING = 4
PIECES = 6

T_LRU = 0
T_PB = T_LRU + 2 * KT
T_ATT = T_PB + 2 * KT
T_PA = T_ATT + 3 * H
T_WO = T_PA + 2 * KT
T_END = T_WO + KT
COL = {"q": 0, "k": D, "v": 2 * D, "xb": 3 * D, "y": 4 * D, "ga": 5 * D, "gb": 6 * D}

C_CW, C_CB, C_BA, C_BX, C_N1 = 0, 64, 80, 96, 112
C_LAM, C_H0, C_SC = 0, 16, 32
NP2 = 80


def need(eng, sem, value):
    if isinstance(value, int) and value <= 0:
        return
    eng.wait_ge(sem, value)


class Steps:

    def __init__(self, eng, sem, base=0):
        self.eng, self.sem, self.base, self.n = eng, sem, base, 0

    def step(self, ins):
        self.n += 1
        ins.then_inc(self.sem, 1)

    def settle(self):
        self.eng.wait_ge(self.sem, self.base + self.n)

    def link(self, ins):
        self.step(ins)
        self.settle()


def peeled(eng, n, body):
    body(0)
    with eng.Fori(1, n) as i:
        body(i)


def build(nc, x_prompt, x_sample, cache_k, cache_v, state_conv, state_lru, norm1_g, w_in, conv_w,
          conv_b, lru_wa, lru_ba, lru_wx, lru_bx, lru_lambda, w_pa, w_pb, w_o, norm2_g,
          router_group_w, router_group_b, router_sub_w, router_sub_b, expert_w_up, expert_w_down,
          final_norm_g, y_prompt, y_sample, prompt_k, prompt_v, prompt_conv, prompt_lru,
          sample_k, sample_v, sample_conv, sample_lru):
    ds = bass.ds

    here = [nc.sbuf_base]

    def sb(name, shape, dt=F32):
        size = 2 if dt == BF16 else 4
        for s in shape[1:]:
            size *= s
        here[0] = (here[0] + 31) // 32 * 32
        t = nc.alloc_sbuf_tensor_at(name, shape, dt, offset=here[0])
        here[0] += size
        return t

    ident = sb("ident", [P, P])
    ones = sb("ones", [P, P])
    before = sb("before", [P, P])
    ident16 = sb("ident16", [P, P], BF16)
    mask16 = sb("mask16", [P, P], BF16)
    slots_i = sb("slots_i", [P, T], I32)
    slots = sb("slots", [P, T])
    first4 = sb("first4", [P, 4])
    eps_t = sb("eps_t", [P, 1])
    prm = sb("prm", [P, P])
    prm2 = sb("prm2", [P, NP2])
    ssq = sb("ssq", [P, FT])
    rms = sb("rms", [P, FT])
    rstd = sb("rstd", [P, FT])
    x1 = sb("x1", [P, FT, D])
    xn = sb("xn", [P, FT, D])
    gain = sb("gain", [P, D])
    mark = here[0]

    h = sb("h", [P, KT, T])
    o = sb("o", [P, KT, T])
    under = here[0]
    xpad = sb("xpad", [P, XW])
    xc = sb("xc", [P, CW])
    gate_w = sb("gate_w", [P, 2, 2, P])
    rg = sb("rg", [P, CW])
    ig = sb("ig", [P, CW])
    th = sb("th", [P, CW])
    sq = sb("sq", [P, CW])
    t1 = sb("t1", [P, CW])
    rc = sb("rc", [P, CW])
    uu = sb("uu", [P, CW])
    aa = sb("aa", [P, CW])
    hs = sb("hs", [P, CW])
    gy = sb("gy", [P, T])
    lru_end = here[0]
    here[0] = under
    qT = sb("qT", [P, 2, T])
    kT = sb("kT", [P, 2, T])
    vT = sb("vT", [P, 2, T])
    kTok = sb("kTok", [P, 2, FT, P])
    vTok = sb("vTok", [P, 2, FT, P])
    cK = sb("cK", [P, 2, PAST // P, P])
    cV = sb("cV", [P, 2, PAST // P, P])
    kcT = sb("kcT", [P, PAST])
    assert lru_end <= here[0]
    sgP = sb("sgP", [P, 384])
    kpP = sb("kpP", [P, 384])
    rP = sb("rP", [P, 386])
    wP = sb("wP", [P, 384])
    pT = sb("pT", [P, 384])
    sgS = sb("sgS", [TS, PAST + TS])
    kpS = sb("kpS", [TS, PAST + TS])
    rS = sb("rS", [TS, PAST + TS + 1])
    wS = sb("wS", [TS, PAST + TS])
    pS = sb("pS", [P, 160])
    free_early = here[0]
    mixed = sb("mixed", [P, KT, T])
    ring = [sb(f"ring{s}", [P, KT, P]) for s in range(RING)]
    prow = sb("prow", [P, P])
    prow2 = sb("prow2", [NP2, P])
    negc = sb("negc", [P, KT])
    lz = sb("lz", [P, 5, KT])
    states = sb("states", [P, P])
    statesT = sb("statesT", [P, P])
    sg = sb("sg", [P, T])
    mx = sb("mx", [P, T])
    yT = sb("yT", [P, 2, T])
    end1 = here[0]

    here[0] = mark
    pieces = [sb(f"piece{s}", [P, 8 * 512]) for s in range(PIECES)]
    early = sum(1 for s in range(PIECES) if mark + (s + 1) * 8 * 512 * 4 <= free_early)
    hT = sb("hT", [P, KT, T])
    hg = sb("hg", [P, KT, CAP])
    act = sb("act", [P, FM, CAP])
    sig = sb("sig", [P, FM, CAP])
    og = sb("og", [CAP, D])
    G = sb("G", [P, FT, CAP])
    CG = sb("CG", [P, FT, EPG, CAP])
    GT = sb("GT", [CAP, T])
    cB = sb("cB", [P, EPG, CAP])
    wr = sb("wr", [P, KT, 20])
    br = sb("br", [P, 20])
    lg = sb("lg", [P, FT, 20])
    m1 = sb("m1", [P, FT, 1])
    r4 = sb("r4", [P, 12, FT, 4])
    pg = sb("pg", [P, FT, 1])
    r1 = sb("r1", [P, 6, FT, 1])
    psel = sb("psel", [P, FT, 4, 4])
    comb = sb("comb", [P, FT, NE])
    pos = sb("pos", [P, FT, NG])
    cnt = sb("cnt", [P, 4])
    cmax = sb("cmax", [P, 1])
    cnt_i = sb("cnt_i", [P, 1], I32)
    assert max(here[0], end1) <= nc.sbuf_usable_end, (here[0], end1, nc.sbuf_usable_end)
    router_w_free = T_PA

    xp = x_prompt.rearrange("a (f p) d -> p (a f) d", p=P)
    yp = y_prompt.rearrange("a (f p) d -> p (a f) d", p=P)
    w_in_v = w_in[0].rearrange("(k p) n -> p k n", p=P)
    w_pa_v = w_pa[0].rearrange("(k p) n -> p k n", p=P)
    w_pb_v = w_pb[0].rearrange("(k p) n -> p k n", p=P)
    w_o_v = w_o[0].rearrange("(k p) n -> p k n", p=P)
    wa_v = lru_wa[0].rearrange("n c d -> c n d")
    wx_v = lru_wx[0].rearrange("n c d -> c n d")
    ck_v = cache_k[0, 0].rearrange("(b p) h d -> p b h d", p=P)
    cv_v = cache_v[0, 0].rearrange("(b p) h d -> p b h d", p=P)
    pk_v = prompt_k[0, 0].rearrange("(f p) h d -> p f h d", p=P)
    pv_v = prompt_v[0, 0].rearrange("(f p) h d -> p f h d", p=P)
    up_v = expert_w_up[0].rearrange("e (k p) n -> p e k n", p=P)
    dn_v = expert_w_down[0].rearrange("e (k p) n -> p e k n", p=P)

    def chan(a):
        return a.rearrange("r (n p) -> (r n) p", p=P)

    with ExitStack() as ctx:
        def sem(name):
            return ctx.enter_context(nc.semaphore(name))

        bank = [ctx.enter_context(nc.psum_tensor(f"bank{i}", [P, 512], F32)) for i in range(8)]
        acc = bank[0:2]
        tr = bank[2:4]
        zP, zS, zN, ov = bank[4:8]
        gateA, gateX = bank[4:6]
        out4 = bank[0:4]
        gB, uB = bank[4:6]
        xb2 = bank[6:8]

        x_in, par_in, rw_in, gain_in = sem("x_in"), sem("par_in"), sem("rw_in"), sem("gain_in")
        ring_in = [sem(f"ring_in{s}") for s in range(RING)]
        piece_in = [sem(f"piece_in{s}") for s in range(PIECES)]
        gw_in = [sem(f"gw_in{s}") for s in range(2)]
        cache_in = [sem(f"cache_in{s}") for s in range(2)]
        kv_out = [sem(f"kv_out{s}") for s in range(2)]
        st_out, y_out = sem("st_out"), sem("y_out")
        consts, consts2 = sem("consts"), sem("consts2")
        act_s, dve_s = sem("act_s"), sem("dve_s")
        par_ps, par_ready, negc_ready = sem("par_ps"), sem("par_ready"), sem("negc_ready")
        ssq_ready, rms_ready, xn_ready = sem("ssq_ready"), sem("rms_ready"), sem("xn_ready")
        h_ps, h_ready = sem("h_ps"), sem("h_ready")
        tile_done = sem("tile_done")
        acc_used = [sem(f"acc_used{b}") for b in range(2)]
        xb_ready, conv_s, xc_ready = sem("xb_ready"), sem("conv_s"), sem("xc_ready")
        gates_ps, gates_s, th_ready = sem("gates_ps"), sem("gates_s"), sem("th_ready")
        gy_ready, lru_s, ob_ready = sem("gy_ready"), sem("lru_s"), sem("ob_ready")
        states_ps, states_ready = sem("states_ps"), sem("states_ready")
        sg_ready, mix_s, mix_ready = sem("sg_ready"), sem("mix_s"), sem("mix_ready")
        qkv_ready = sem("qkv_ready")
        kc_ps, kcT_ready = sem("kc_ps"), sem("kcT_ready")
        ktok_ps, kTok_ready = sem("ktok_ps"), sem("kTok_ready")
        vtok_ps, vTok_ready = sem("vtok_ps"), sem("vTok_ready")
        zP_ready, zS_ready = sem("zP_ready"), sem("zS_ready")
        sigP_ready, sigS_ready = sem("sigP_ready"), sem("sigS_ready")
        scan_s, wP_ready, wS_ready = sem("scan_s"), sem("wP_ready"), sem("wS_ready")
        pt_ps, pT_ready = sem("pt_ps"), sem("pT_ready")
        ps_ps, pS_ready = sem("ps_ps"), sem("pS_ready")
        ov_done, oa_ready = sem("ov_done"), sem("oa_ready")
        yT_ready, y_ps, x1_ready = sem("yT_ready"), sem("y_ps"), sem("x1_ready")
        hT_ps, hT_ready = sem("hT_ps"), sem("hT_ready")
        lg_ps, lg_ready, ge_ready, dd_ready, ed_ready = (sem("lg_ps"), sem("lg_ready"), sem("ge_ready"),
                                                         sem("dd_ready"), sem("ed_ready"))
        oh_ready, pos_ps, routed = sem("oh_ready"), sem("pos_ps"), sem("routed")
        G_s, G_ready = sem("G_s"), sem("G_ready")
        gt_ps, cb_ps, hg_ps, hg_ready = sem("gt_ps"), sem("cb_ps"), sem("hg_ps"), sem("hg_ready")
        GT_ready, cB_ready = sem("GT_ready"), sem("cB_ready")
        x_used = [sem(f"x_used{b}") for b in range(2)]
        silu_ready, act_s2, act_ready = sem("silu_ready"), sem("act_s2"), sem("act_ready")
        piece_done, og_ready = sem("piece_done"), sem("og_ready")
        sc_ps = sem("sc_ps")
        x1_final = sem("x1_final")
        yo_ready = sem("yo_ready")

        block = ctx.enter_context(nc.Block())

        @block.sync
        def _(sp):
            sp.dma_start(x1[:, 0:2, :], xp).then_inc(x_in, 16)
            sp.dma_start(x1[0:TS, 2, :], x_sample[0]).then_inc(x_in, 16)
            for dst, src in ((prow[C_CW:C_CB, :], chan(conv_w[0])), (prow[C_CB:C_BA, :], chan(conv_b)),
                             (prow[C_BA:C_BX, :], chan(lru_ba)), (prow[C_BX:C_N1, :], chan(lru_bx)),
                             (prow[C_N1:P, :], chan(norm1_g)),
                             (prow2[C_LAM:C_H0, :], chan(lru_lambda)),
                             (prow2[C_H0:C_SC, :], chan(state_lru[0])),
                             (prow2[C_SC:NP2, :], chan(state_conv[0, 0]))):
                sp.dma_start(dst, src).then_inc(par_in, 16)

            def load(tile, slot, src):
                need(sp, tile_done, tile - RING + 1)
                sp.dma_start(ring[slot][:, :, :], src).then_inc(ring_in[slot], 16)

            def lru_loads(i):
                for b in range(2):
                    n = 2 * i + b
                    tile = T_LRU + 2 * n
                    load(tile, 2 * b, w_in_v[:, :, ds(n * P + COL["xb"], P)])
                    load(tile + 1, 2 * b + 1, w_in_v[:, :, ds(n * P + COL["y"], P)])
                    need(sp, gates_ps, n - 1)
                    sp.dma_start(gate_w[:, b, 0, :], wa_v[:, ds(n, 1), :]).then_inc(gw_in[b], 16)
                    sp.dma_start(gate_w[:, b, 1, :], wx_v[:, ds(n, 1), :]).then_inc(gw_in[b], 16)

            peeled(sp, KT // 2, lru_loads)

            def gated_loads(base, gcol, w_v):
                def body(i):
                    for b in range(2):
                        m = 2 * i + b
                        sp.wait_ge(tile_done, base + 2 * m + 2 - RING)
                        sp.dma_start(ring[2 * b][:, :, :], w_in_v[:, :, ds(m * P + gcol, P)])\
                          .then_inc(ring_in[2 * b], 16)
                        sp.dma_start(ring[2 * b + 1][:, :, :], w_v[:, :, ds(m * P, P)])\
                          .then_inc(ring_in[2 * b + 1], 16)
                with sp.Fori(0, KT // 2) as i:
                    body(i)

            gated_loads(T_PB, COL["gb"], w_pb_v)

            def cache_load(head, b):
                need(sp, ov_done, head - 1)
                sp.dma_start(cK[:, b, :, :], ck_v[:, :, ds(head, 1), :]).then_inc(cache_in[b], 16)
                sp.dma_start(cV[:, b, :, :], cv_v[:, :, ds(head, 1), :]).then_inc(cache_in[b], 16)

            def att_loads(i):
                for j in range(4):
                    head = 4 * i + j
                    for c, name in enumerate("qkv"):
                        load(T_ATT + 3 * head + c, (3 * j + c) % RING,
                             w_in_v[:, :, ds(head * P + COL[name], P)])
                        if c == 0 and not (isinstance(head, int) and head == 0):
                            cache_load(head - 1, (j + 1) % 2)

            peeled(sp, H // 4, att_loads)
            cache_load(H - 1, 1)
            gated_loads(T_PA, COL["ga"], w_pa_v)

            with sp.Fori(0, KT // 4) as i:
                for j in range(4):
                    load(T_WO + 4 * i + j, j, w_o_v[:, :, ds((4 * i + j) * P, P)])

            def piece(e, s):
                if s < 4:
                    k0, c0 = 8 * (s % 2), 512 * (s // 2)
                    return (pieces[s][:, :].rearrange("p (a k n) -> p a k n", a=1, k=8),
                            up_v[:, ds(e, 1), k0:k0 + 8, c0:c0 + 512])
                return (pieces[s][:, :].rearrange("p (a k n) -> p a k n", a=1, k=2),
                        dn_v[:, ds(e, 1), 2 * (s - 4):2 * (s - 4) + 2, :])

            def load_piece(e, s):
                dst, src = piece(e, s)
                sp.dma_start(dst, src).then_inc(piece_in[s], 16)

            sp.wait_ge(tile_done, T_WO)
            for b in range(2):
                sp.wait_ge(kv_out[b], 64 * (H // 2))
            for s in range(early):
                load_piece(0, s)
            sp.wait_ge(x1_ready, KT)
            for dst, src in ((wr[:, :, 0:4], router_group_w[0].rearrange("(k p) g -> p k g", p=P)),
                             *((wr[:, :, 4 + 4 * g:8 + 4 * g],
                                router_sub_w[0, g].rearrange("(k p) e -> p k e", p=P)) for g in range(NG)),
                             (br[:, 0:4], router_group_b[0:1, :].partition_broadcast(P)),
                             (br[:, 4:20], router_sub_b.rearrange("a g e -> a (g e)").partition_broadcast(P))):
                sp.dma_start(dst, src).then_inc(rw_in, 16)
            for s in range(early, PIECES):
                load_piece(0, s)

            def expert_loads(e, done):
                for s in range(PIECES):
                    sp.wait_ge(piece_done, done + s + 1)
                    load_piece(e, s)

            with sp.Fori(1, NE) as e:
                expert_loads(e, PIECES * (e - 1))

            sp.wait_ge(xn_ready, 2 * FT)
            sp.dma_start(gain[:, :], final_norm_g.rearrange("(a n) -> a n", a=1).partition_broadcast(P))\
              .then_inc(gain_in, 16)

            sp.wait_ge(routed, 1)
            n = sp.value_load(cnt_i[0:1, 0:1], min_val=0, max_val=T)
            with sp.If(n > CAP):
                for c in range(1, CHUNKS):
                    with sp.Fori(0, NE) as e:
                        expert_loads(e, PIECES * (e + NE * c - 1))

            for f in range(FT):
                sp.wait_ge(yo_ready, f + 1)
                dst = yp[:, f, :] if f < 2 else y_sample[0]
                sp.dma_start(dst, xn[0:ROWS[f], f, :]).then_inc(y_out, 16)
            sp.wait_ge(y_out, 16 * FT)

        @block.gpsimd
        def _(pool):
            def const(ins):
                ins.then_inc(consts, 1)
            const(pool.memset(ident[:, :], 0.0))
            const(pool.memset(ident16[:, :], 0.0))
            const(pool.memset(ones[:, :], 1.0))
            const(pool.memset(before[:, :], 1.0))
            const(pool.memset(mask16[:, :], 0.0))
            const(pool.iota(slots_i[:, :], pattern=[[1, T]], base=0, channel_multiplier=0))
            for k in range(4):
                const(pool.memset(first4[:, k:k + 1], 4.0 - k))
            const(pool.memset(eps_t[:, :], EPS))
            const(pool.memset(xpad[:, 0:HIST], 0.0))
            const(pool.memset(rP[:, 128:129], 1.0))
            const(pool.memset(rP[:, 385:386], 1.0))
            const(pool.memset(rS[:, PAST + TS:PAST + TS + 1], 1.0))
            pool.wait_ge(consts, 15)
            for t in (ident, ident16):
                pool.affine_select(out=t[:, :], in_=t[:, :], compare_op=ALU.not_equal, fill=1.0, base=0,
                                   pattern=[[-1, P]], channel_multiplier=1).then_inc(consts2, 1)
            pool.affine_select(out=before[:, :], in_=before[:, :], compare_op=ALU.is_gt, fill=0.0, base=0,
                               pattern=[[1, P]], channel_multiplier=-1).then_inc(consts2, 1)
            pool.affine_select(out=mask16[:, :], in_=mask16[:, :], compare_op=ALU.is_gt, fill=NEG, base=0,
                               pattern=[[-1, P]], channel_multiplier=1).then_inc(consts2, 1)
            pool.tensor_copy(slots[:, :], slots_i[:, :]).then_inc(consts2, 1)

        @block.scalar
        def _(a):
            a.dma_start(gain[:, :], norm2_g[0:1, :].partition_broadcast(P)).then_inc(gain_in, 16)

            def square_sums(f):
                a.activation(xn[0:ROWS[f], f, :], x1[0:ROWS[f], f, :], ACT.Square,
                             accum_out=ssq[0:ROWS[f], f:f + 1]).then_inc(ssq_ready, 1)

            def roots(nth):
                a.wait_ge(ssq_ready, FT * nth)
                for f in range(FT):
                    a.activation(rms[0:ROWS[f], f:f + 1], ssq[0:ROWS[f], f:f + 1], ACT.Sqrt,
                                 bias=eps_t[0:ROWS[f], :], scale=1.0 / D).then_inc(rms_ready, 1)

            a.wait_ge(x_in, 32)
            a.wait_ge(consts, 15)
            for f in range(FT):
                square_sums(f)
            roots(1)
            own = Steps(a, act_s)
            a.wait_ge(par_ps, 1)
            own.step(a.activation(prm[:, :], tr[0][:, 0:P], ACT.Copy))
            a.activation(prm2[:, :], tr[1][:, 0:NP2], ACT.Copy).then_inc(par_ready, 1)
            own.settle()
            a.wait_ge(par_ready, 1)
            own.link(a.activation(lz[:, 0, :], prm2[:, C_LAM:C_LAM + KT], ACT.Abs))
            a.activation(lz[:, 1, :], lz[:, 0, :], ACT.Exp, scale=-1.0).then_inc(par_ready, 1)
            for k in range(KT):
                a.wait_ge(h_ps, k + 1)
                a.activation(h[:, k, :], bank[4 + k % 4][:, 0:T], ACT.Copy,
                             scale=prm[:, C_N1 + k:C_N1 + k + 1]).then_inc(h_ready, 1)
            a.wait_ge(negc_ready, 1)

            def lru(i):
                for b in range(2):
                    n = 2 * i + b
                    tile = T_LRU + 2 * n
                    a.wait_ge(tile_done, tile + 1)
                    need(a, xc_ready, n)
                    a.activation(xpad[:, HIST:HIST + TP], acc[0][:, 0:TP], ACT.Copy).then_inc(xb_ready, 1)
                    a.activation(xpad[:, XW - TS:XW], acc[0][:, TP:T], ACT.Copy).then_inc(xb_ready, 1)
                    a.wait_ge(xb_ready, 2 * n + 2)
                    a.sem_inc(acc_used[0], 1)
                    a.wait_ge(tile_done, tile + 2)
                    need(a, ob_ready, n)
                    a.activation(gy[:, :], acc[1][:, 0:T], ACT.Gelu_apprx_tanh).then_inc(gy_ready, 1)
                    a.wait_ge(gy_ready, n + 1)
                    a.sem_inc(acc_used[1], 1)
                    a.wait_ge(gates_ps, n + 1)
                    own = Steps(a, gates_s, 2 * n)
                    own.step(a.activation(rg[:, :], gateA[:, 0:CW], ACT.Sigmoid,
                                          bias=prm[:, ds(n + C_BA, 1)]))
                    own.step(a.activation(ig[:, :], gateX[:, 0:CW], ACT.Sigmoid,
                                          bias=prm[:, ds(n + C_BX, 1)]))
                    own.settle()
                    a.activation(th[:, :], rg[:, :], ACT.Tanh, scale=negc[:, ds(n, 1)]).then_inc(th_ready, 1)
                    a.wait_ge(th_ready, 2 * n + 1)
                    a.activation(sq[:, :], th[:, :], ACT.Sqrt).then_inc(th_ready, 1)

            peeled(a, KT // 2, lru)

            def gates(base, m0):
                def body(i):
                    for b in range(2):
                        m = 2 * i + b
                        a.wait_ge(tile_done, base + 2 * m + 1)
                        need(a, mix_ready, m + m0)
                        a.activation(sg[:, :], acc[0][:, 0:T], ACT.Sigmoid).then_inc(sg_ready, 1)
                        a.wait_ge(sg_ready, m + m0 + 1)
                        a.sem_inc(acc_used[0], 1)
                peeled(a, KT // 2, body)

            gates(T_PB, 0)
            a.wait_ge(states_ps, 1)
            a.activation(statesT[:, :], tr[0][:, 0:P], ACT.Copy).then_inc(states_ready, 1)
            a.wait_ge(states_ready, 1)
            for dst, lo, hi in ((prompt_conv[0, 0], 0, 48), (sample_conv[0, 0], 48, 96),
                                (prompt_lru[0], 96, 112), (sample_lru[0], 112, 128)):
                a.dma_start(chan(dst), statesT[lo:hi, :]).then_inc(st_out, 16)

            def take(head, j, c, dst):
                tile = T_ATT + 3 * head + c
                a.wait_ge(tile_done, tile + 1)
                a.activation(dst[:, j % 2, :], acc[(3 * j + c) % 2][:, 0:T], ACT.Copy).then_inc(qkv_ready, 1)
                a.wait_ge(qkv_ready, 3 * head + c + 1)
                a.sem_inc(acc_used[(3 * j + c) % 2], 1)

            def store(src, b, head, prompt, sample):
                a.dma_start(prompt[:, :, ds(head, 1), :], src[:, b, 0:2, :]).then_inc(kv_out[b], 16)
                a.dma_start(sample[0, 0, :, ds(head, 1), :], src[0:TS, b, 2, :]).then_inc(kv_out[b], 16)

            def att1(head, b, nth):
                need(a, kv_out[b], 64 * nth)
                a.wait_ge(ktok_ps, head + 1)
                a.activation(kTok[:, b, 0:2, :], tr[1][:, 0:256].rearrange("p (f d) -> p f d", f=2),
                             ACT.Copy).then_inc(kTok_ready, 1)
                a.activation(kTok[0:TS, b, 2, :], tr[1][0:TS, 256:384], ACT.Copy).then_inc(kTok_ready, 1)
                a.wait_ge(zP_ready, head + 1)
                need(a, wP_ready, head)
                a.activation(sgP[:, :], zP[:, 0:384], ACT.Sigmoid, scale=SCALE).then_inc(sigP_ready, 1)
                a.activation(kpP[:, :], zP[:, 0:384], ACT.Sigmoid, scale=-SCALE).then_inc(sigP_ready, 1)
                a.wait_ge(kTok_ready, 2 * head + 2)
                store(kTok, b, head, pk_v, sample_k)
                a.wait_ge(zS_ready, head + 1)
                need(a, wS_ready, head)
                for dst, s in ((sgS, SCALE), (kpS, -SCALE)):
                    a.activation(dst[:, 0:PAST], zS[0:TS, :], ACT.Sigmoid, scale=s).then_inc(sigS_ready, 1)
                    a.activation(dst[:, PAST:], zN[0:TS, 0:TS], ACT.Sigmoid, scale=s).then_inc(sigS_ready, 1)
                a.wait_ge(vtok_ps, head + 1)
                a.activation(vTok[:, b, 0:2, :], tr[0][:, 0:256].rearrange("p (f d) -> p f d", f=2),
                             ACT.Copy).then_inc(vTok_ready, 1)
                a.activation(vTok[0:TS, b, 2, :], tr[0][0:TS, 256:384], ACT.Copy).then_inc(vTok_ready, 1)
                a.wait_ge(vTok_ready, 2 * head + 2)
                store(vTok, b, head, pv_v, sample_v)

            def att2(head):
                a.wait_ge(pt_ps, head + 1)
                a.activation(pT[:, :], tr[1][:, 0:384], ACT.Copy).then_inc(pT_ready, 1)

            def att3(head):
                a.wait_ge(ov_done, head + 1)
                a.activation(o[:, ds(head, 1), :], ov[:, 0:T], ACT.Copy).then_inc(oa_ready, 1)

            def att(i):
                for j in range(4):
                    head = 4 * i + j
                    prev = not (isinstance(head, int) and head == 0)
                    b, nth = (j + 1) % 2, (2 * i + (j - 1) // 2)
                    take(head, j, 0, qT)
                    if prev:
                        att1(head - 1, b, nth)
                    take(head, j, 1, kT)
                    if prev:
                        att2(head - 1)
                    take(head, j, 2, vT)
                    if prev:
                        att3(head - 1)

            peeled(a, H // 4, att)
            att1(H - 1, 1, H // 2 - 1)
            att2(H - 1)
            att3(H - 1)
            gates(T_PA, KT)

            def wo(i):
                for j in range(4):
                    m = 4 * i + j
                    a.wait_ge(tile_done, T_WO + m + 1)
                    a.activation(yT[:, j % 2, :], acc[j % 2][:, 0:T], ACT.Copy).then_inc(yT_ready, 1)
                    a.wait_ge(yT_ready, m + 1)
                    a.sem_inc(acc_used[j % 2], 1)
            with a.Fori(0, KT // 4) as i:
                wo(i)

            a.wait_ge(x1_ready, KT)
            for f in range(FT):
                square_sums(f)
            roots(2)
            for k in range(KT):
                a.wait_ge(hT_ps, k + 1)
                a.activation(hT[:, k, :], bank[4 + k % 4][:, 0:T], ACT.Copy).then_inc(hT_ready, 1)

            a.wait_ge(lg_ready, 1)
            a.activation(r4[:, 1, :, :], r4[:, 0, :, :], ACT.Exp).then_inc(ge_ready, 1)
            a.wait_ge(dd_ready, 1)
            a.activation(r1[:, 1, :, :], r1[:, 0, :, :], ACT.Exp).then_inc(ed_ready, 1)

            def group(gp):
                a.wait_ge(gt_ps, gp + 1)
                a.activation(GT[:, :], xb2[0][0:CAP, 0:T], ACT.Copy).then_inc(GT_ready, 1)
                a.wait_ge(GT_ready, gp + 1)
                a.sem_inc(x_used[0], 1)
                for q in range(4):
                    a.wait_ge(hg_ps, 4 * gp + q + 1)
                    a.activation(hg[:, 4 * q:4 * q + 4, :],
                                 xb2[q % 2][:, 0:4 * CAP].rearrange("p (k c) -> p k c", k=4),
                                 ACT.Copy).then_inc(hg_ready, 1)
                    a.wait_ge(hg_ready, 4 * gp + q + 1)
                    a.sem_inc(x_used[q % 2], 1)
                for j in range(EPG):
                    a.wait_ge(piece_done, PIECES * (EPG * gp + j) + 4)
                    a.activation(sig[:, :, :], gB[:, 0:FM * CAP].rearrange("p (m c) -> p m c", m=FM),
                                 ACT.Silu).then_inc(silu_ready, 1)
                a.wait_ge(piece_done, PIECES * EPG * (gp + 1))
                for nb in range(2):
                    a.activation(og[:, nb * 512:(nb + 1) * 512], out4[nb][0:CAP, :], ACT.Copy)\
                     .then_inc(og_ready, 1)

            peeled(a, NG, group)
            a.wait_ge(routed, 1)
            n = a.value_load(cnt_i[0:1, 0:1], min_val=0, max_val=T)
            with a.If(n > CAP):
                with a.Fori(NG, NG * CHUNKS) as gp:
                    group(gp)

            a.wait_ge(x1_final, 1)
            for f in range(FT):
                square_sums(f)
            roots(3)
            a.wait_ge(st_out, 64)
            for b in range(2):
                a.wait_ge(kv_out[b], 64 * (H // 2))

        @block.tensor
        def _(pe):
            pe.wait_ge(consts2, 5)
            pe.wait_ge(par_in, 16 * 8)
            pe.transpose(tr[0][:, 0:P], prow[:, :], ident[:, :])
            pe.transpose(tr[1][:, 0:NP2], prow2[:, :], ident[0:NP2, 0:NP2]).then_inc(par_ps, 1)

            def turn(dst, src, f0=0):
                for f in range(FT):
                    ins = pe.transpose(dst[:, f * P:f * P + ROWS[f]], src(f), ident[0:ROWS[f], 0:ROWS[f]])
                return ins

            pe.wait_ge(xn_ready, FT)
            for k in range(KT):
                need(pe, h_ready, k - 3)
                turn(bank[4 + k % 4], lambda f: xn[0:ROWS[f], f, k * P:(k + 1) * P]).then_inc(h_ps, 1)
            pe.wait_ge(h_ready, KT)

            def tile_product(slot, fills, used, rhs):
                pe.wait_ge(ring_in[slot], 16 * fills)
                need(pe, acc_used[slot % 2], used)
                for k in range(KT):
                    ins = pe.matmul(acc[slot % 2][:, 0:T], ring[slot][:, k, :], rhs[:, k, :],
                                    start=(k == 0), stop=(k == KT - 1))
                ins.then_inc(tile_done, 1)

            def lru(i):
                for b in range(2):
                    n = 2 * i + b
                    for c in range(2):
                        tile_product(2 * b + c, T_LRU // 4 + i + 1, T_LRU // 2 + 2 * i + b, h)
                    pe.wait_ge(xc_ready, n + 1)
                    pe.wait_ge(gw_in[b], 32 * (i + 1))
                    need(pe, th_ready, 2 * n)
                    pe.matmul(gateA[:, 0:CW], gate_w[:, b, 0, :], xc[:, :], start=True, stop=True)
                    pe.matmul(gateX[:, 0:CW], gate_w[:, b, 1, :], xc[:, :], start=True, stop=True)\
                      .then_inc(gates_ps, 1)

            peeled(pe, KT // 2, lru)

            def gated(base, ready, count):
                def body(i):
                    for b in range(2):
                        tile_product(2 * b, base // 4 + i + 1, base // 2 + 2 * i + b, h)
                        pe.wait_ge(ready, count)
                        tile_product(2 * b + 1, base // 4 + i + 1, base // 2 + 2 * i + b, o)
                with pe.Fori(0, KT // 2) as i:
                    body(i)

            gated(T_PB, ob_ready, KT)
            pe.transpose(tr[0][:, 0:P], states[:, :], ident[:, :]).then_inc(states_ps, 1)
            pe.wait_ge(states_ready, 1)

            def att1(head, b, nth):
                pe.wait_ge(cache_in[b], 32 * (nth + 1))
                pe.wait_ge(qkv_ready, 3 * head + 3)
                need(pe, pS_ready, 2 * head)
                for kb in range(PAST // P):
                    ins = pe.transpose(tr[0][:, kb * P:(kb + 1) * P], cK[:, b, kb, :], ident[:, :])
                ins.then_inc(kc_ps, 1)
                need(pe, pT_ready, head)
                for f in range(FT):
                    ins = pe.transpose(tr[1][0:ROWS[f], f * P:(f + 1) * P],
                                       kT[:, b, f * P:f * P + ROWS[f]], ident[:, :])
                ins.then_inc(ktok_ps, 1)
                need(pe, sigP_ready, 2 * head)
                pe.matmul(zP[:, 0:128], qT[:, b, 0:128], kT[:, b, 0:128], start=True, stop=False,
                          skip_group_check=True)
                pe.matmul(zP[:, 0:128], ident16[:, :], mask16[:, :], start=False, stop=True,
                          skip_group_check=True)
                pe.matmul(zP[:, 128:384], qT[:, b, 128:256], kT[:, b, 0:256], start=True, stop=False,
                          skip_group_check=True)
                pe.matmul(zP[:, 256:384], ident16[:, :], mask16[:, :], start=False, stop=True,
                          skip_group_check=True).then_inc(zP_ready, 1)
                need(pe, sigS_ready, 4 * head)
                pe.matmul(zN[0:TS, 0:TS], qT[:, b, TP:T], kT[:, b, TP:T], start=True, stop=False,
                          skip_group_check=True)
                pe.matmul(zN[0:TS, 0:TS], ident16[:, 0:TS], mask16[:, 0:TS], start=False, stop=True,
                          skip_group_check=True)
                pe.wait_ge(kcT_ready, head + 1)
                pe.matmul(zS[0:TS, :], qT[:, b, TP:T], kcT[:, :], start=True, stop=True).then_inc(zS_ready, 1)
                for f in range(FT):
                    ins = pe.transpose(tr[0][0:ROWS[f], f * P:(f + 1) * P],
                                       vT[:, b, f * P:f * P + ROWS[f]], ident[:, :])
                ins.then_inc(vtok_ps, 1)

            def att2(head):
                pe.wait_ge(wP_ready, head + 1)
                pe.wait_ge(kTok_ready, 2 * head + 2)
                for c in range(3):
                    if c == 2:
                        pe.wait_ge(wS_ready, head + 1)
                        pe.wait_ge(vTok_ready, 2 * head + 2)
                    ins = pe.transpose(tr[1][:, c * P:(c + 1) * P], wP[:, c * P:(c + 1) * P], ident[:, :])
                ins.then_inc(pt_ps, 1)
                for kb in range(PAST // P):
                    pe.transpose(tr[0][:, kb * TS:(kb + 1) * TS], wS[:, kb * P:(kb + 1) * P],
                                 ident[0:TS, 0:TS])
                pe.transpose(tr[0][0:TS, 128:160], wS[:, PAST:PAST + TS], ident[0:TS, 0:TS])\
                  .then_inc(ps_ps, 1)

            def att3(head, b):
                pe.wait_ge(pT_ready, head + 1)
                pe.wait_ge(pS_ready, 2 * head + 2)
                need(pe, oa_ready, head)
                pe.matmul(ov[:, 0:256], vTok[:, b, 0, :], pT[:, 0:256], start=True, stop=False,
                          skip_group_check=True)
                pe.matmul(ov[:, 128:256], vTok[:, b, 1, :], pT[:, 256:384], start=False, stop=True,
                          skip_group_check=True)
                for kb in range(PAST // P):
                    pe.matmul(ov[:, TP:T], cV[:, b, kb, :], pS[:, kb * TS:(kb + 1) * TS],
                              start=(kb == 0), stop=False, skip_group_check=True)
                pe.matmul(ov[:, TP:T], vTok[0:TS, b, 2, :], pS[0:TS, 128:160], start=False, stop=True,
                          skip_group_check=True).then_inc(ov_done, 1)

            def att(i):
                for j in range(4):
                    head = 4 * i + j
                    prev = not (isinstance(head, int) and head == 0)
                    b, nth = (j + 1) % 2, (2 * i + (j - 1) // 2)
                    for c in range(3):
                        u = 3 * j + c
                        tile_product(u % RING, T_ATT // 4 + 3 * i + u // 4 + 1,
                                     T_ATT // 2 + 6 * i + u // 2, h)
                        if prev:
                            (lambda: att1(head - 1, b, nth), lambda: att2(head - 1),
                             lambda: att3(head - 1, b))[c]()

            peeled(pe, H // 4, att)
            att1(H - 1, 1, H // 2 - 1)
            att2(H - 1)
            att3(H - 1, 1)
            gated(T_PA, oa_ready, H)

            def y_turn(m, b):
                pe.wait_ge(yT_ready, m + 1)
                need(pe, x1_ready, m - 1)
                for f in range(FT):
                    ins = pe.transpose(tr[b][0:ROWS[f], f * P:(f + 1) * P],
                                       yT[:, b, f * P:f * P + ROWS[f]], ident[:, :])
                ins.then_inc(y_ps, 1)

            pe.wait_ge(mix_ready, 2 * KT)

            def wo(i):
                for j in range(4):
                    tile_product(j, T_WO // 4 + i + 1, T_WO // 2 + 2 * i + j // 2, mixed)
                    if not (isinstance(i, int) and i == 0 and j == 0):
                        y_turn(4 * i + j - 1, (j + 1) % 2)
            peeled(pe, KT // 4, wo)
            y_turn(KT - 1, 1)

            pe.wait_ge(xn_ready, 2 * FT)
            for k in range(KT):
                need(pe, hT_ready, k - 3)
                turn(bank[4 + k % 4], lambda f: xn[0:ROWS[f], f, k * P:(k + 1) * P]).then_inc(hT_ps, 1)
            pe.wait_ge(hT_ready, KT)
            pe.wait_ge(rw_in, 16 * 7)
            for f in range(FT):
                for k in range(KT):
                    ins = pe.matmul(bank[f][0:ROWS[f], 0:20], hT[:, k, f * P:f * P + ROWS[f]], wr[:, k, :],
                                    start=(k == 0), stop=(k == KT - 1))
            ins.then_inc(lg_ps, 1)
            pe.wait_ge(oh_ready, 1)
            oh = r4[:, 3, :, :]
            for f in range(FT):
                for e in range(f + 1):
                    lhs = before if e == f else ones
                    pe.matmul(bank[4 + f][0:ROWS[f], 0:NG], lhs[0:ROWS[e], 0:ROWS[f]], oh[0:ROWS[e], e, :],
                              start=(e == 0), stop=(e == f))
            for e in range(FT):
                ins = pe.matmul(bank[7][:, 0:NG], ones[0:ROWS[e], :], oh[0:ROWS[e], e, :],
                                start=(e == 0), stop=(e == FT - 1))
            ins.then_inc(pos_ps, 1)
            pe.wait_ge(routed, 1)

            def group(gp):
                pe.wait_ge(G_ready, gp + 1)
                need(pe, x_used[0], 9 * gp)
                for f in range(FT):
                    ins = pe.transpose(xb2[0][0:CAP, f * P:f * P + ROWS[f]], G[0:ROWS[f], f, :],
                                       ident[0:ROWS[f], 0:ROWS[f]])
                ins.then_inc(gt_ps, 1)
                need(pe, x_used[1], 9 * gp)
                for f in range(FT):
                    ins = pe.matmul(xb2[1][:, 0:EPG * CAP], ones[0:ROWS[f], :],
                                    CG[0:ROWS[f], f, :, :].rearrange("p e c -> p (e c)"),
                                    start=(f == 0), stop=(f == FT - 1))
                ins.then_inc(cb_ps, 1)
                for q in range(4):
                    pe.wait_ge(x_used[q % 2], 9 * gp + 1 + q // 2)
                    for kk in range(4):
                        k = 4 * q + kk
                        for f in range(FT):
                            ins = pe.matmul(xb2[q % 2][:, kk * CAP:(kk + 1) * CAP],
                                            xn[0:ROWS[f], f, k * P:(k + 1) * P], G[0:ROWS[f], f, :],
                                            start=(f == 0), stop=(f == FT - 1))
                    ins.then_inc(hg_ps, 1)
                for j in range(EPG):
                    ep = EPG * gp + j
                    need(pe, act_ready, ep)
                    for s in range(4):
                        pe.wait_ge(piece_in[s], 16 * (ep + 1))
                        w = pieces[s][:, :].rearrange("p (k n) -> p k n", k=8)
                        if j == 0 and s < 2:
                            pe.wait_ge(hg_ready, 4 * gp + 2 + 2 * s)
                        dst = gB if s < 2 else uB
                        for k in range(8):
                            for m in range(FM):
                                ins = pe.matmul(dst[:, m * CAP:(m + 1) * CAP], w[:, k, m * P:(m + 1) * P],
                                                hg[:, 8 * (s % 2) + k, :],
                                                start=(s % 2 == 0 and k == 0 and m == 0),
                                                stop=(s % 2 == 1 and k == 7), skip_group_check=True)
                        ins.then_inc(piece_done, 1)
                    pe.wait_ge(act_ready, ep + 1)
                    if j == 0:
                        need(pe, og_ready, 4 * gp)
                    for s in range(2):
                        pe.wait_ge(piece_in[4 + s], 16 * (ep + 1))
                        w = pieces[4 + s][:, :].rearrange("p (k n) -> p k n", k=2)
                        for kk in range(2):
                            m = 2 * s + kk
                            for nb in range(4):
                                ins = pe.matmul(out4[nb][0:CAP, :], act[:, m, :],
                                                w[:, kk, nb * 512:(nb + 1) * 512],
                                                start=(j == 0 and m == 0), stop=(j == EPG - 1 and m == FM - 1))
                        ins.then_inc(piece_done, 1)
                pe.wait_ge(og_ready, 4 * gp + 4)
                pe.wait_ge(GT_ready, gp + 1)
                for u in range(4 * FT):
                    f, nb = u // 4, u % 4
                    pe.wait_ge(x_used[u % 2], 9 * gp + 3 + u // 2)
                    pe.matmul(xb2[u % 2][0:ROWS[f], :], GT[:, f * P:f * P + ROWS[f]],
                              og[:, nb * 512:(nb + 1) * 512], start=True, stop=True).then_inc(sc_ps, 1)

            peeled(pe, NG, group)
            n = pe.value_load(cnt_i[0:1, 0:1], min_val=0, max_val=T)
            with pe.If(n > CAP):
                with pe.Fori(NG, NG * CHUNKS) as gp:
                    group(gp)

        @block.vector
        def _(v):
            own = Steps(v, dve_s)

            def norm(nth, dst_sem, row):
                v.wait_ge(rms_ready, FT * nth)
                for f in range(FT):
                    own.step(v.reciprocal(rstd[0:ROWS[f], f:f + 1], rms[0:ROWS[f], f:f + 1]))
                own.settle()
                for f in range(FT):
                    R = ROWS[f]
                    if row:
                        ins = v.scalar_tensor_tensor(xn[0:R, f, :], x1[0:R, f, :], rstd[0:R, f:f + 1],
                                                     gain[0:R, :], ALU.mult, ALU.mult)
                    else:
                        ins = v.tensor_scalar(xn[0:R, f, :], x1[0:R, f, :], rstd[0:R, f:f + 1], None, ALU.mult)
                    ins.then_inc(dst_sem, 1)

            norm(1, xn_ready, False)

            v.wait_ge(par_ready, 2)
            z, s, s2, p = (lz[:, 1, :], lz[:, 2, :], lz[:, 3, :], lz[:, 4, :])
            own.link(v.tensor_scalar(s, z, 2.0, None, ALU.add))
            own.link(v.reciprocal(s, s))
            own.link(v.tensor_tensor(s, s, z, ALU.mult))
            own.link(v.tensor_tensor(s2, s, s, ALU.mult))
            own.link(v.tensor_scalar(p, s2, 1.0 / 17.0, None, ALU.mult))
            for k in (15, 13, 11, 9, 7, 5, 3):
                own.link(v.scalar_tensor_tensor(p, p, 1.0 / k, s2, ALU.add, ALU.mult))
            own.link(v.scalar_tensor_tensor(p, p, 1.0, s, ALU.add, ALU.mult))
            own.link(v.tensor_scalar(s, prm2[:, C_LAM:C_LAM + KT], -1.0, 0.0, ALU.mult, ALU.max))
            own.link(v.tensor_scalar(p, p, 8.0, None, ALU.mult))
            v.scalar_tensor_tensor(negc[:, :], s, 4.0, p, ALU.mult, ALU.add).then_inc(negc_ready, 1)

            states3 = states[:, :].rearrange("p (k n) -> p k n", n=KT)
            hist3 = prm2[:, C_SC:C_SC + HIST * KT].rearrange("p (k n) -> p k n", n=KT)

            LRU_STEPS = 17

            def lru(i):
                for b in range(2):
                    n = 2 * i + b
                    st = Steps(v, lru_s, LRU_STEPS * n)
                    v.wait_ge(xb_ready, 2 * n + 2)
                    st.step(v.tensor_copy(xpad[:, HIST + TP:HIST + TP + HIST], hist3[:, :, ds(n, 1)]))
                    st.settle()
                    need(v, gates_ps, n)
                    st.link(v.tensor_scalar(xc[:, :], xpad[:, 0:CW], prm[:, ds(n + C_CW, 1)],
                                            prm[:, ds(n + C_CB, 1)], ALU.mult, ALU.add))
                    for tap in (1, 2):
                        st.link(v.scalar_tensor_tensor(xc[:, :], xpad[:, tap:tap + CW],
                                                       prm[:, ds(n + C_CW + tap * KT, 1)], xc[:, :],
                                                       ALU.mult, ALU.add))
                    st.step(v.tensor_copy(states3[:, 0:3, ds(n, 1)], xpad[:, TP:TP + HIST]))
                    st.step(v.tensor_copy(states3[:, 3:6, ds(n, 1)], xpad[:, XW - HIST:XW]))
                    st.settle()
                    v.scalar_tensor_tensor(xc[:, :], xpad[:, 3:3 + CW], prm[:, ds(n + C_CW + 3 * KT, 1)],
                                           xc[:, :], ALU.mult, ALU.add).then_inc(xc_ready, 1)
                    v.wait_ge(th_ready, 2 * n + 1)
                    v.wait_ge(xc_ready, n + 1)
                    st.link(v.tensor_scalar(t1[:, :], th[:, :], 1.0, None, ALU.add))
                    st.step(v.reciprocal(rc[:, :], t1[:, :]))
                    v.wait_ge(th_ready, 2 * n + 2)
                    st.link(v.tensor_tensor(uu[:, :], ig[:, :], xc[:, :], ALU.mult))
                    st.step(v.tensor_scalar(aa[:, :], rc[:, :], 2.0, -1.0, ALU.mult, ALU.add))
                    st.link(v.tensor_tensor(uu[:, :], uu[:, :], sq[:, :], ALU.mult))
                    st.link(v.scalar_tensor_tensor(uu[:, :], uu[:, :], 2.0, rc[:, :], ALU.mult, ALU.mult))
                    st.step(v.memset(aa[:, S0 - 1:S0], 0.0))
                    st.link(v.tensor_copy(uu[:, S0 - 1:S0], prm2[:, ds(n + C_H0, 1)]))
                    st.link(v.tensor_tensor_scan(hs[:, :], aa[:, :], uu[:, :], 0.0, ALU.mult, ALU.add))
                    st.step(v.tensor_copy(states3[:, 6:7, ds(n, 1)], hs[:, TP - 1:TP]))
                    st.step(v.tensor_copy(states3[:, 7:8, ds(n, 1)], hs[:, CW - 1:CW]))
                    v.wait_ge(gy_ready, n + 1)
                    v.tensor_tensor(o[:, ds(n, 1), 0:TP], gy[:, 0:TP], hs[:, 0:TP], ALU.mult)\
                     .then_inc(mix_s, 1)
                    v.tensor_tensor(o[:, ds(n, 1), TP:T], gy[:, TP:T], hs[:, S0:CW], ALU.mult)\
                     .then_inc(mix_s, 1)
                    st.settle()
                    v.wait_ge(mix_s, 2 * n + 2)
                    v.sem_inc(ob_ready, 1)
                    assert st.n == LRU_STEPS, st.n

            peeled(v, KT // 2, lru)

            def gated(base, m0, add):
                def body(i):
                    for b in range(2):
                        m = 2 * i + b
                        v.wait_ge(tile_done, base + 2 * m + 2)
                        v.wait_ge(sg_ready, m + m0 + 1)
                        if not add:
                            v.tensor_tensor(mixed[:, ds(m, 1), :], acc[1][:, 0:T], sg[:, :], ALU.mult)\
                             .then_inc(acc_used[1], 1)
                        else:
                            v.tensor_tensor(mx[:, :], acc[1][:, 0:T], sg[:, :], ALU.mult)\
                             .then_inc(acc_used[1], 1)
                        v.wait_ge(acc_used[1], base // 2 + m + 1)
                        if not add:
                            v.sem_inc(mix_ready, 1)
                        else:
                            v.tensor_tensor(mixed[:, ds(m, 1), :], mixed[:, ds(m, 1), :], mx[:, :], ALU.add)\
                             .then_inc(mix_ready, 1)
                with v.Fori(0, KT // 2) as i:
                    body(i)

            gated(T_PB, 0, False)

            def att1(head):
                v.wait_ge(kc_ps, head + 1)
                need(v, zS_ready, head)
                v.tensor_copy(kcT[:, :], tr[0][:, :]).then_inc(kcT_ready, 1)
                v.wait_ge(sigP_ready, 2 * head + 2)
                v.tensor_tensor_scan(rP[:, 0:128][:, ::-1], kpP[:, 0:128][:, ::-1], kpP[:, 0:128][:, ::-1],
                                     1.0, ALU.mult, ALU.bypass).then_inc(scan_s, 1)
                v.tensor_tensor_scan(rP[:, 129:385][:, ::-1], kpP[:, 128:384][:, ::-1],
                                     kpP[:, 128:384][:, ::-1], 1.0, ALU.mult, ALU.bypass).then_inc(scan_s, 1)
                v.wait_ge(scan_s, 3 * head + 2)
                need(v, pt_ps, head)
                v.tensor_tensor(wP[:, 0:128], sgP[:, 0:128], rP[:, 1:129], ALU.mult).then_inc(mix_s, 1)
                v.tensor_tensor(wP[:, 128:384], sgP[:, 128:384], rP[:, 130:386], ALU.mult).then_inc(mix_s, 1)
                v.wait_ge(mix_s, 2 * KT + 2 * head + 2)
                v.sem_inc(wP_ready, 1)
                v.wait_ge(sigS_ready, 4 * head + 4)
                n = PAST + TS
                v.tensor_tensor_scan(rS[:, 0:n][:, ::-1], kpS[:, :][:, ::-1], kpS[:, :][:, ::-1],
                                     1.0, ALU.mult, ALU.bypass).then_inc(scan_s, 1)
                v.wait_ge(scan_s, 3 * head + 3)
                need(v, ps_ps, head)
                v.tensor_tensor(wS[:, :], sgS[:, :], rS[:, 1:n + 1], ALU.mult).then_inc(wS_ready, 1)

            def att2(head):
                v.wait_ge(ps_ps, head + 1)
                need(v, ov_done, head)
                v.tensor_copy(pS[:, 0:128], tr[0][:, 0:128]).then_inc(pS_ready, 1)
                v.tensor_copy(pS[0:TS, 128:160], tr[0][0:TS, 128:160]).then_inc(pS_ready, 1)

            v.wait_ge(consts, 15)
            att1(0)
            att2(0)
            with v.Fori(1, H) as head:
                att1(head)
                att2(head)

            gated(T_PA, KT, True)

            def residual(i):
                for j in range(2):
                    m = 2 * i + j
                    v.wait_ge(y_ps, m + 1)
                    c = ds(m * P, P)
                    v.tensor_tensor(x1[:, 0:2, c], tr[j][:, 0:256].rearrange("p (f d) -> p f d", f=2),
                                    x1[:, 0:2, c], ALU.add).then_inc(mix_s, 1)
                    v.tensor_tensor(x1[0:TS, 2, c], tr[j][0:TS, 256:384], x1[0:TS, 2, c], ALU.add)\
                     .then_inc(mix_s, 1)
                    v.wait_ge(mix_s, 2 * KT + 2 * H + 2 * m + 2)
                    v.sem_inc(x1_ready, 1)
            with v.Fori(0, KT // 2) as i:
                residual(i)

            v.wait_ge(gain_in, 16)
            norm(2, xn_ready, True)

            for t, c in ((lg, 0.0), (pos, 0.0)):
                own.step(v.memset(t[:, :, :], c))
            own.settle()
            v.wait_ge(rw_in, 16 * 7)
            v.wait_ge(lg_ps, 1)
            for f in range(FT):
                own.step(v.tensor_tensor(lg[0:ROWS[f], f, :], bank[f][0:ROWS[f], 0:20], br[0:ROWS[f], :], ALU.add))
            own.settle()

            def bc(t, n=4):
                return t.to_broadcast([P, FT, n])

            f4 = first4[:, :].rearrange("p (a c) -> p a c", a=1).to_broadcast([P, FT, 4])

            def first_max(x, top, one, tmp):
                own.link(v.tensor_reduce(top, x, AX.X, ALU.max))
                own.link(v.tensor_tensor(tmp, x, bc(top), ALU.is_equal))
                own.link(v.tensor_tensor(tmp, tmp, f4, ALU.mult))
                own.link(v.tensor_reduce(r1[:, 5, :, :], tmp, AX.X, ALU.max))
                own.link(v.tensor_tensor(one, tmp, bc(r1[:, 5, :, :]), ALU.is_equal))

            oh = r4[:, 3, :, :]
            first_max(lg[:, :, 0:4], m1[:, :, :], oh, r4[:, 2, :, :])
            own.link(v.tensor_tensor(r4[:, 0, :, :], lg[:, :, 0:4], bc(m1[:, :, :]), ALU.subtract))
            v.sem_inc(lg_ready, 1)
            v.sem_inc(oh_ready, 1)
            own.link(v.tensor_tensor(psel[:, :, :, :], lg[:, :, 4:20].rearrange("p f (g e) -> p f g e", g=4),
                                     oh.rearrange("p f (g a) -> p f g a", a=1).to_broadcast([P, FT, 4, 4]),
                                     ALU.mult))
            sel, one1, one2, cut = r4[:, 4, :, :], r4[:, 5, :, :], r4[:, 6, :, :], r4[:, 7, :, :]
            own.link(v.tensor_reduce(sel, psel[:, :, :, :].rearrange("p f g e -> p f e g"), AX.X, ALU.add))
            first_max(sel, r1[:, 2, :, :], one1, r4[:, 2, :, :])
            own.link(v.scalar_tensor_tensor(cut, one1, NEG, sel, ALU.mult, ALU.add))
            first_max(cut, r1[:, 3, :, :], one2, r4[:, 2, :, :])
            own.link(v.tensor_tensor(r1[:, 0, :, :], r1[:, 3, :, :], r1[:, 2, :, :], ALU.subtract))
            v.sem_inc(dd_ready, 1)
            v.wait_ge(ge_ready, 1)
            own.link(v.tensor_reduce(pg[:, :, :], r4[:, 1, :, :], AX.X, ALU.add))
            own.link(v.reciprocal(pg[:, :, :], pg[:, :, :]))
            v.wait_ge(ed_ready, 1)
            own.link(v.tensor_scalar(r1[:, 2, :, :], r1[:, 1, :, :], 1.0, None, ALU.add))
            own.link(v.reciprocal(r1[:, 2, :, :], r1[:, 2, :, :]))
            own.link(v.tensor_tensor(r1[:, 2, :, :], r1[:, 2, :, :], pg[:, :, :], ALU.mult))
            own.link(v.tensor_tensor(r1[:, 3, :, :], r1[:, 2, :, :], r1[:, 1, :, :], ALU.mult))
            own.link(v.tensor_tensor(one1, one1, bc(r1[:, 2, :, :]), ALU.mult))
            own.link(v.tensor_tensor(one2, one2, bc(r1[:, 3, :, :]), ALU.mult))
            own.link(v.tensor_tensor(one1, one1, one2, ALU.add))
            own.link(v.tensor_tensor(comb[:, :, :].rearrange("p f (g e) -> p f g e", g=4),
                                     oh.rearrange("p f (g a) -> p f g a", a=1).to_broadcast([P, FT, 4, 4]),
                                     one1.rearrange("p f (a e) -> p f a e", a=1).to_broadcast([P, FT, 4, 4]),
                                     ALU.mult))
            v.wait_ge(pos_ps, 1)
            for f in range(FT):
                own.step(v.tensor_copy(pos[0:ROWS[f], f, :], bank[4 + f][0:ROWS[f], 0:NG]))
            own.link(v.tensor_scalar(r4[:, 8, :, :], oh, -1.0e6, 1.0e6, ALU.mult, ALU.add))
            own.link(v.tensor_tensor(pos[:, :, :], pos[:, :, :], r4[:, 8, :, :], ALU.add))
            own.link(v.tensor_reduce(cmax[:, :], bank[7][:, 0:NG], AX.X, ALU.max))
            v.tensor_copy(cnt_i[:, :], cmax[:, :]).then_inc(routed, 1)

            GS = 2 * FT

            def group(gp, g, c0):
                v.wait_ge(consts2, 5)
                need(v, hg_ps, 4 * gp)
                for f in range(FT):
                    v.tensor_scalar(G[:, f, :], slots[:, c0:c0 + CAP], pos[:, f, ds(g, 1)], None,
                                    ALU.is_equal).then_inc(G_s, 1)
                v.wait_ge(G_s, GS * gp + FT)
                for f in range(FT):
                    v.tensor_tensor(CG[:, f, :, :],
                                    G[:, f, :].rearrange("p (a c) -> p a c", a=1).to_broadcast([P, EPG, CAP]),
                                    comb[:, f, ds(4 * g, 4)].rearrange("p (e a) -> p e a", a=1)
                                    .to_broadcast([P, EPG, CAP]), ALU.mult).then_inc(G_s, 1)
                v.wait_ge(G_s, GS * gp + 2 * FT)
                v.sem_inc(G_ready, 1)
                v.wait_ge(cb_ps, gp + 1)
                v.tensor_copy(cB[:, :, :], xb2[1][:, 0:EPG * CAP].rearrange("p (e c) -> p e c", e=EPG))\
                 .then_inc(x_used[1], 1)
                v.wait_ge(x_used[1], 9 * gp + 1)
                for j in range(EPG):
                    ep = EPG * gp + j
                    v.wait_ge(silu_ready, ep + 1)
                    v.tensor_tensor(sig[:, :, :], sig[:, :, :],
                                    uB[:, 0:FM * CAP].rearrange("p (m c) -> p m c", m=FM), ALU.mult)\
                     .then_inc(act_s2, 1)
                    v.wait_ge(act_s2, ep + 1)
                    v.tensor_tensor(act[:, :, :], sig[:, :, :],
                                    cB[:, j, :].rearrange("p (a c) -> p a c", a=1).to_broadcast([P, FM, CAP]),
                                    ALU.mult).then_inc(act_ready, 1)
                v.wait_ge(piece_done, PIECES * EPG * (gp + 1))
                for nb in range(2, 4):
                    v.tensor_copy(og[:, nb * 512:(nb + 1) * 512], out4[nb][0:CAP, :]).then_inc(og_ready, 1)
                for u in range(4 * FT):
                    f, nb = u // 4, u % 4
                    c = slice(nb * 512, (nb + 1) * 512)
                    v.wait_ge(sc_ps, 4 * FT * gp + u + 1)
                    v.tensor_tensor(x1[0:ROWS[f], f, c], xb2[u % 2][0:ROWS[f], :], x1[0:ROWS[f], f, c], ALU.add)\
                     .then_inc(x_used[u % 2], 1)
                for b in range(2):
                    v.wait_ge(x_used[b], 9 * gp + 9)

            v.wait_ge(routed, 1)
            peeled(v, NG, lambda g: group(g, g, 0))
            n = v.value_load(cnt_i[0:1, 0:1], min_val=0, max_val=T)
            with v.If(n > CAP):
                for c in range(1, CHUNKS):
                    with v.Fori(0, NG) as g:
                        group(g + NG * c, g, c * CAP)
            v.memset(ssq[:, :], 0.0).then_inc(x1_final, 1)
            v.wait_ge(gain_in, 32)
            norm(3, yo_ready, True)


INS = ["x_prompt", "x_sample", "cache_k", "cache_v", "state_conv", "state_lru", "norm1_g", "w_in",
       "conv_w", "conv_b", "lru_wa", "lru_ba", "lru_wx", "lru_bx", "lru_lambda", "w_pa", "w_pb", "w_o",
       "norm2_g", "router_group_w", "router_group_b", "router_sub_w", "router_sub_b", "expert_w_up",
       "expert_w_down", "final_norm_g"]
OUTS = [(1, TP, D), (1, TS, D), (1, 1, TP, H, P), (1, 1, TP, H, P), (1, 1, HIST, D), (1, 1, D),
        (1, 1, TS, H, P), (1, 1, TS, H, P), (1, 1, HIST, D), (1, 1, D)]


def kernel(**inputs):
    import numpy as np
    import concourse.bacc as bacc
    from concourse.bass_utils import run_bass_kernel_spmd

    nc = bacc.Bacc("TRN2", target_bir_lowering=False, num_devices=1)
    arrays, args = {}, []
    for name in INS:
        a = np.ascontiguousarray(inputs[name])
        arrays[f"in_{name}"] = a
        args.append(nc.dram_tensor(f"in_{name}", a.shape, mybir.dt.from_np(a.dtype), kind="ExternalInput").ap())
    for i, shape in enumerate(OUTS):
        args.append(nc.dram_tensor(f"out_{i}", shape, F32, kind="ExternalOutput").ap())
    build(nc, *args)
    r = run_bass_kernel_spmd(nc, [arrays], core_ids=[0])
    return tuple(r.results[0][f"out_{i}"] for i in range(len(OUTS)))
```

```python
from contextlib import ExitStack

import concourse.bass as bass
from concourse import mybir

F32 = mybir.dt.float32
F32R = mybir.dt.float32r
BF16 = mybir.dt.bfloat16
I32 = mybir.dt.int32
ALU = mybir.AluOpType
ACT = mybir.ActivationFunctionType
AX = mybir.AxisListType

P = 128
D = 2048
KT = D // P
TP, TS = 256, 32
T = TP + TS
FT = 3
ROWS = [P, P, TS]
H = 16
PAST = 512
SCALE = float(P) ** -0.5
CONV = 4
HIST = CONV - 1
XW = HIST + TP + HIST + TS
CW = TP + HIST + TS
S0 = TP + HIST
NG, EPG, FF = 4, 4, 512
NE = NG * EPG
FM = FF // P
CAP = 96
CHUNKS = T // CAP
EPS = 1e-6
LRU_C = 8.0
NEG = -1.0e30
RING = 4
HALVES = 4
PIECES = 6

T_LRU = 0
T_PB = T_LRU + 2 * KT
T_ATT = T_PB + 2 * KT
T_PA = T_ATT + 3 * H
T_WO = T_PA + 2 * KT
T_END = T_WO + KT
COL = {"q": 0, "k": D, "v": 2 * D, "xb": 3 * D, "y": 4 * D, "ga": 5 * D, "gb": 6 * D}

C_CW, C_CB, C_BA, C_BX, C_N1 = 0, 64, 80, 96, 112
C_LAM, C_H0, C_SC = 0, 16, 32
NP2 = 80


def need(eng, sem, value):
    if isinstance(value, int) and value <= 0:
        return
    eng.wait_ge(sem, value)


class Steps:

    def __init__(self, eng, sem, base=0):
        self.eng, self.sem, self.base, self.n = eng, sem, base, 0

    def step(self, ins):
        self.n += 1
        ins.then_inc(self.sem, 1)

    def settle(self):
        self.eng.wait_ge(self.sem, self.base + self.n)

    def link(self, ins):
        self.step(ins)
        self.settle()


def peeled(eng, n, body):
    body(0)
    with eng.Fori(1, n) as i:
        body(i)


def build(nc, x_prompt, x_sample, cache_k, cache_v, state_conv, state_lru, norm1_g, w_in, conv_w,
          conv_b, lru_wa, lru_ba, lru_wx, lru_bx, lru_lambda, w_pa, w_pb, w_o, norm2_g,
          router_group_w, router_group_b, router_sub_w, router_sub_b, expert_w_up, expert_w_down,
          final_norm_g, y_prompt, y_sample, prompt_k, prompt_v, prompt_conv, prompt_lru,
          sample_k, sample_v, sample_conv, sample_lru):
    ds = bass.ds

    here = [nc.sbuf_base]

    def sb(name, shape, dt=F32):
        size = 2 if dt == BF16 else 4
        for s in shape[1:]:
            size *= s
        here[0] = (here[0] + 31) // 32 * 32
        t = nc.alloc_sbuf_tensor_at(name, shape, dt, offset=here[0])
        here[0] += size
        return t

    ident = sb("ident", [P, P])
    ones = sb("ones", [P, P])
    before = sb("before", [P, P])
    ident16 = sb("ident16", [P, P], BF16)
    mask16 = sb("mask16", [P, P], BF16)
    slots_i = sb("slots_i", [P, T], I32)
    slots = sb("slots", [P, T])
    first4 = sb("first4", [P, 4])
    eps_t = sb("eps_t", [P, 1])
    prm = sb("prm", [P, P])
    prm2 = sb("prm2", [P, NP2])
    ssq = sb("ssq", [P, FT])
    rms = sb("rms", [P, FT])
    rstd = sb("rstd", [P, FT])
    mark = here[0]

    hH = sb("hH", [P, KT, T], F32R)
    hL = sb("hL", [P, KT, T], F32R)
    at_o = here[0]
    oH = sb("oH", [P, KT, T], F32R)
    oL = sb("oL", [P, KT, T], F32R)
    under = here[0]
    xc = sb("xc", [P, CW])
    rg = sb("rg", [P, CW])
    ig = sb("ig", [P, CW])
    th = sb("th", [P, CW])
    sq = sb("sq", [P, CW])
    t1 = sb("t1", [P, CW])
    rc = sb("rc", [P, CW])
    uu = sb("uu", [P, CW])
    aa = sb("aa", [P, CW])
    hs = sb("hs", [P, CW])
    gy = sb("gy", [P, T])
    ob = sb("ob", [P, T])
    lru_end = here[0]
    here[0] = under
    qT = sb("qT", [P, 2, T])
    kT = sb("kT", [P, 2, T])
    vT = sb("vT", [P, 2, T])
    kTok = sb("kTok", [P, 2, FT, P])
    vTok = sb("vTok", [P, 2, FT, P])
    cK = sb("cK", [P, 2, PAST // P, P])
    cV = sb("cV", [P, 2, PAST // P, P])
    kcT = sb("kcT", [P, PAST])
    assert lru_end <= here[0]
    sgP = sb("sgP", [P, 384])
    kpP = sb("kpP", [P, 384])
    rP = sb("rP", [P, 386])
    wP = sb("wP", [P, 384])
    pT = sb("pT", [P, 384])
    sgS = sb("sgS", [TS, PAST + TS])
    kpS = sb("kpS", [TS, PAST + TS])
    rS = sb("rS", [TS, PAST + TS + 1])
    wS = sb("wS", [TS, PAST + TS])
    pS = sb("pS", [P, 160])
    at_mixed = here[0]
    mixed = sb("mixed", [P, KT, T])
    ring = [sb(f"ring{s}", [P, KT, P]) for s in range(RING)]
    wH = [sb(f"wH{s}", [P, KT // 2, P], F32R) for s in range(HALVES)]
    wL = [sb(f"wL{s}", [P, KT // 2, P], F32R) for s in range(HALVES)]
    at_prow = here[0]
    prow = sb("prow", [P, P])
    prow2 = sb("prow2", [NP2, P])
    xpad = sb("xpad", [P, XW])
    gate_w = sb("gate_w", [P, 2, 2, P])
    negh = sb("negh", [P, KT])
    hb = sb("hb", [P, 2 * KT])
    lz = sb("lz", [P, 5, KT])
    states = sb("states", [P, P])
    statesT = sb("statesT", [P, P])
    sg = sb("sg", [P, T])
    mx = sb("mx", [P, T])
    end1 = here[0]
    here[0] = at_prow
    yT = sb("yT", [P, 2, T])

    here[0] = at_o
    x0 = sb("x0", [P, FT, D])
    xn0 = sb("xn0", [P, FT, D])
    assert here[0] <= at_mixed

    here[0] = mark
    xn = sb("xn", [P, FT, D])
    hg = sb("hg", [P, KT, CAP])
    act = sb("act", [P, FM, CAP])
    sig = sb("sig", [P, FM, CAP])
    assert here[0] <= at_o
    here[0] = at_o
    early = 2
    pieces = [sb(f"piece{s}", [P, 8 * 512]) for s in range(early)]
    x1 = sb("x1", [P, FT, D])
    gain = sb("gain", [P, D])
    assert here[0] <= at_mixed
    wr = sb("wr", [P, KT, 20])
    br = sb("br", [P, 20])
    lg = sb("lg", [P, FT, 20])
    m1 = sb("m1", [P, FT, 1])
    r4 = sb("r4", [P, 12, FT, 4])
    pg = sb("pg", [P, FT, 1])
    r1 = sb("r1", [P, 6, FT, 1])
    psel = sb("psel", [P, FT, 4, 4])
    comb = sb("comb", [P, FT, NE])
    pos = sb("pos", [P, FT, NG])
    cmax = sb("cmax", [P, 1])
    cnt_i = sb("cnt_i", [P, 1], I32)
    pieces += [sb(f"piece{s}", [P, 8 * 512]) for s in range(early, PIECES)]
    at_hT = here[0]
    hT = sb("hT", [P, KT, T])
    end2 = here[0]
    here[0] = at_hT
    og = sb("og", [CAP, D])
    G = sb("G", [P, FT, CAP])
    CG = sb("CG", [P, FT, EPG, CAP])
    GT = sb("GT", [CAP, T])
    cB = sb("cB", [P, EPG, CAP])
    assert max(here[0], end1, end2) <= nc.sbuf_usable_end, (here[0], end1, end2, nc.sbuf_usable_end)

    xp = x_prompt.rearrange("a (f p) d -> p (a f) d", p=P)
    yp = y_prompt.rearrange("a (f p) d -> p (a f) d", p=P)
    w_in_v = w_in[0].rearrange("(k p) n -> p k n", p=P)
    w_pa_v = w_pa[0].rearrange("(k p) n -> p k n", p=P)
    w_pb_v = w_pb[0].rearrange("(k p) n -> p k n", p=P)
    w_o_v = w_o[0].rearrange("(k p) n -> p k n", p=P)
    wa_v = lru_wa[0].rearrange("n c d -> c n d")
    wx_v = lru_wx[0].rearrange("n c d -> c n d")
    ck_v = cache_k[0, 0].rearrange("(b p) h d -> p b h d", p=P)
    cv_v = cache_v[0, 0].rearrange("(b p) h d -> p b h d", p=P)
    pk_v = prompt_k[0, 0].rearrange("(f p) h d -> p f h d", p=P)
    pv_v = prompt_v[0, 0].rearrange("(f p) h d -> p f h d", p=P)
    up_v = expert_w_up[0].rearrange("e (k p) n -> p e k n", p=P)
    dn_v = expert_w_down[0].rearrange("e (k p) n -> p e k n", p=P)

    def chan(a):
        return a.rearrange("r (n p) -> (r n) p", p=P)

    with ExitStack() as ctx:
        def sem(name):
            return ctx.enter_context(nc.semaphore(name))

        bank = [ctx.enter_context(nc.psum_tensor(f"bank{i}", [P, 512], F32)) for i in range(8)]
        acc = bank[0:2]
        tr = bank[2:4]
        zP, zS, zN, ov = bank[4:8]
        gateA, gateX = bank[4:6]
        out4 = bank[0:4]
        gB, uB = bank[4:6]
        xb2 = bank[6:8]

        x_in, par_in, rw_in, gain_in = sem("x_in"), sem("par_in"), sem("rw_in"), sem("gain_in")
        ring_in = [sem(f"ring_in{s}") for s in range(RING)]
        piece_in = [sem(f"piece_in{s}") for s in range(PIECES)]
        gw_in = [sem(f"gw_in{s}") for s in range(2)]
        cache_in = [sem(f"cache_in{s}") for s in range(2)]
        kv_out = [sem(f"kv_out{s}") for s in range(2)]
        st_out, y_out = sem("st_out"), sem("y_out")
        consts, consts2 = sem("consts"), sem("consts2")
        act_s, dve_s = sem("act_s"), sem("dve_s")
        par_ps, par_ready, negh_ready = sem("par_ps"), sem("par_ready"), sem("negh_ready")
        ssq_ready, rms_ready, xn_ready = sem("ssq_ready"), sem("rms_ready"), sem("xn_ready")
        h_ps, hH_ready, h_ready = sem("h_ps"), sem("hH_ready"), sem("h_ready")
        hi_ready, lo_ready = sem("hi_ready"), sem("lo_ready")
        half_done = sem("half_done")
        mixsplit_s, mixsplit_ready = sem("mixsplit_s"), sem("mixsplit_ready")
        xr_in, gain2_in = sem("xr_in"), sem("gain2_in")
        oaH_ready, oH_s = sem("oaH_ready"), sem("oH_s")
        acc_used = [sem(f"acc_used{b}") for b in range(2)]
        xb_ready, conv_s, xc_ready = sem("xb_ready"), sem("conv_s"), sem("xc_ready")
        gates_ps, gates_s, th_ready = sem("gates_ps"), sem("gates_s"), sem("th_ready")
        gy_ready, lru_s, ob_ready = sem("gy_ready"), sem("lru_s"), sem("ob_ready")
        states_ps, states_ready = sem("states_ps"), sem("states_ready")
        sg_ready, mix_s, mix_ready = sem("sg_ready"), sem("mix_s"), sem("mix_ready")
        qkv_ready = sem("qkv_ready")
        kc_ps, kcT_ready = sem("kc_ps"), sem("kcT_ready")
        ktok_ps, kTok_ready = sem("ktok_ps"), sem("kTok_ready")
        vtok_ps, vTok_ready = sem("vtok_ps"), sem("vTok_ready")
        zP_ready, zS_ready = sem("zP_ready"), sem("zS_ready")
        sigP_ready, sigS_ready = sem("sigP_ready"), sem("sigS_ready")
        scan_s, wP_ready, wS_ready = sem("scan_s"), sem("wP_ready"), sem("wS_ready")
        pt_ps, pT_ready = sem("pt_ps"), sem("pT_ready")
        ps_ps, pS_ready = sem("ps_ps"), sem("pS_ready")
        ov_done, oa_ready = sem("ov_done"), sem("oa_ready")
        yT_ready, y_ps, x1_ready = sem("yT_ready"), sem("y_ps"), sem("x1_ready")
        hT_ps, hT_ready = sem("hT_ps"), sem("hT_ready")
        lg_ps, lg_ready, ge_ready, dd_ready, ed_ready = (sem("lg_ps"), sem("lg_ready"), sem("ge_ready"),
                                                         sem("dd_ready"), sem("ed_ready"))
        oh_ready, pos_ps, routed = sem("oh_ready"), sem("pos_ps"), sem("routed")
        G_s, G_ready = sem("G_s"), sem("G_ready")
        gt_ps, cb_ps, hg_ps, hg_ready = sem("gt_ps"), sem("cb_ps"), sem("hg_ps"), sem("hg_ready")
        GT_ready, cB_ready = sem("GT_ready"), sem("cB_ready")
        x_used = [sem(f"x_used{b}") for b in range(2)]
        silu_ready, act_s2, act_ready = sem("silu_ready"), sem("act_s2"), sem("act_ready")
        piece_done, og_ready = sem("piece_done"), sem("og_ready")
        sc_ps = sem("sc_ps")
        x1_final = sem("x1_final")
        yo_ready = sem("yo_ready")

        block = ctx.enter_context(nc.Block())

        @block.sync
        def _(sp):
            sp.dma_start(x0[:, 0:2, :], xp).then_inc(x_in, 16)
            sp.dma_start(x0[0:TS, 2, :], x_sample[0]).then_inc(x_in, 16)
            for dst, src in ((prow[C_CW:C_CB, :], chan(conv_w[0])), (prow[C_CB:C_BA, :], chan(conv_b)),
                             (prow[C_BA:C_BX, :], chan(lru_ba)), (prow[C_BX:C_N1, :], chan(lru_bx)),
                             (prow[C_N1:P, :], chan(norm1_g)),
                             (prow2[C_LAM:C_H0, :], chan(lru_lambda)),
                             (prow2[C_H0:C_SC, :], chan(state_lru[0])),
                             (prow2[C_SC:NP2, :], chan(state_conv[0, 0]))):
                sp.dma_start(dst, src).then_inc(par_in, 16)

            def load(tile, slot, src):
                need(sp, lo_ready, 2 * (tile - RING + 1))
                sp.dma_start(ring[slot][:, :, :], src).then_inc(ring_in[slot], 16)

            def lru_loads(i):
                for b in range(2):
                    n = 2 * i + b
                    tile = T_LRU + 2 * n
                    load(tile, 2 * b, w_in_v[:, :, ds(n * P + COL["xb"], P)])
                    load(tile + 1, 2 * b + 1, w_in_v[:, :, ds(n * P + COL["y"], P)])
                    need(sp, gates_ps, n - 1)
                    sp.dma_start(gate_w[:, b, 0, :], wa_v[:, ds(n, 1), :]).then_inc(gw_in[b], 16)
                    sp.dma_start(gate_w[:, b, 1, :], wx_v[:, ds(n, 1), :]).then_inc(gw_in[b], 16)

            peeled(sp, KT // 2, lru_loads)

            def gated_loads(base, gcol, w_v):
                def body(i):
                    for b in range(2):
                        m = 2 * i + b
                        sp.wait_ge(lo_ready, 2 * (base + 2 * m + 2 - RING))
                        sp.dma_start(ring[2 * b][:, :, :], w_in_v[:, :, ds(m * P + gcol, P)])\
                          .then_inc(ring_in[2 * b], 16)
                        sp.dma_start(ring[2 * b + 1][:, :, :], w_v[:, :, ds(m * P, P)])\
                          .then_inc(ring_in[2 * b + 1], 16)
                with sp.Fori(0, KT // 2) as i:
                    body(i)

            gated_loads(T_PB, COL["gb"], w_pb_v)

            def cache_load(head, b):
                need(sp, ov_done, head - 1)
                sp.dma_start(cK[:, b, :, :], ck_v[:, :, ds(head, 1), :]).then_inc(cache_in[b], 16)
                sp.dma_start(cV[:, b, :, :], cv_v[:, :, ds(head, 1), :]).then_inc(cache_in[b], 16)

            def att_loads(i):
                for j in range(4):
                    head = 4 * i + j
                    for c, name in enumerate("qkv"):
                        load(T_ATT + 3 * head + c, (3 * j + c) % RING,
                             w_in_v[:, :, ds(head * P + COL[name], P)])
                        if c == 0 and not (isinstance(head, int) and head == 0):
                            cache_load(head - 1, (j + 1) % 2)

            peeled(sp, H // 4, att_loads)
            cache_load(H - 1, 1)
            gated_loads(T_PA, COL["ga"], w_pa_v)

            with sp.Fori(0, KT // 4) as i:
                for j in range(4):
                    load(T_WO + 4 * i + j, j, w_o_v[:, :, ds((4 * i + j) * P, P)])

            def piece(e, s):
                if s < 4:
                    k0, c0 = 8 * (s % 2), 512 * (s // 2)
                    return (pieces[s][:, :].rearrange("p (a k n) -> p a k n", a=1, k=8),
                            up_v[:, ds(e, 1), k0:k0 + 8, c0:c0 + 512])
                return (pieces[s][:, :].rearrange("p (a k n) -> p a k n", a=1, k=2),
                        dn_v[:, ds(e, 1), 2 * (s - 4):2 * (s - 4) + 2, :])

            def load_piece(e, s):
                dst, src = piece(e, s)
                sp.dma_start(dst, src).then_inc(piece_in[s], 16)

            sp.wait_ge(half_done, 2 * T_WO)
            for b in range(2):
                sp.wait_ge(kv_out[b], 64 * (H // 2))
            for s in range(early):
                load_piece(0, s)
            sp.wait_ge(x1_ready, KT)
            for dst, src in ((wr[:, :, 0:4], router_group_w[0].rearrange("(k p) g -> p k g", p=P)),
                             *((wr[:, :, 4 + 4 * g:8 + 4 * g],
                                router_sub_w[0, g].rearrange("(k p) e -> p k e", p=P)) for g in range(NG)),
                             (br[:, 0:4], router_group_b[0:1, :].partition_broadcast(P)),
                             (br[:, 4:20], router_sub_b.rearrange("a g e -> a (g e)").partition_broadcast(P))):
                sp.dma_start(dst, src).then_inc(rw_in, 16)
            for s in range(early, PIECES):
                load_piece(0, s)

            def expert_loads(e, done):
                for s in range(PIECES):
                    sp.wait_ge(piece_done, done + s + 1)
                    load_piece(e, s)

            with sp.Fori(1, NE) as e:
                expert_loads(e, PIECES * (e - 1))

            sp.wait_ge(xn_ready, 2 * FT)
            sp.dma_start(gain[:, :], final_norm_g.rearrange("(a n) -> a n", a=1).partition_broadcast(P))\
              .then_inc(gain_in, 16)

            sp.wait_ge(routed, 1)
            n = sp.value_load(cnt_i[0:1, 0:1], min_val=0, max_val=T)
            with sp.If(n > CAP):
                for c in range(1, CHUNKS):
                    with sp.Fori(0, NE) as e:
                        expert_loads(e, PIECES * (e + NE * c - 1))

            for f in range(FT):
                sp.wait_ge(yo_ready, f + 1)
                dst = yp[:, f, :] if f < 2 else y_sample[0]
                sp.dma_start(dst, xn[0:ROWS[f], f, :]).then_inc(y_out, 16)
            sp.wait_ge(y_out, 16 * FT)

        @block.gpsimd
        def _(pool):
            def const(ins):
                ins.then_inc(consts, 1)
            const(pool.memset(ident[:, :], 0.0))
            const(pool.memset(ident16[:, :], 0.0))
            const(pool.memset(ones[:, :], 1.0))
            const(pool.memset(before[:, :], 1.0))
            const(pool.memset(mask16[:, :], 0.0))
            const(pool.iota(slots_i[:, :], pattern=[[1, T]], base=0, channel_multiplier=0))
            for k in range(4):
                const(pool.memset(first4[:, k:k + 1], 4.0 - k))
            const(pool.memset(eps_t[:, :], EPS))
            const(pool.memset(xpad[:, 0:HIST], 0.0))
            const(pool.memset(rP[:, 128:129], 1.0))
            const(pool.memset(rP[:, 385:386], 1.0))
            const(pool.memset(rS[:, PAST + TS:PAST + TS + 1], 1.0))
            pool.wait_ge(consts, 15)
            for t in (ident, ident16):
                pool.affine_select(out=t[:, :], in_=t[:, :], compare_op=ALU.not_equal, fill=1.0, base=0,
                                   pattern=[[-1, P]], channel_multiplier=1).then_inc(consts2, 1)
            pool.affine_select(out=before[:, :], in_=before[:, :], compare_op=ALU.is_gt, fill=0.0, base=0,
                               pattern=[[1, P]], channel_multiplier=-1).then_inc(consts2, 1)
            pool.affine_select(out=mask16[:, :], in_=mask16[:, :], compare_op=ALU.is_gt, fill=NEG, base=0,
                               pattern=[[-1, P]], channel_multiplier=1).then_inc(consts2, 1)
            pool.tensor_copy(slots[:, :], slots_i[:, :]).then_inc(consts2, 1)
            pool.wait_ge(half_done, 2 * T_WO)
            for b in range(2):
                pool.wait_ge(kv_out[b], 64 * (H // 2))
            pool.dma_start(x1[:, 0:2, :], xp).then_inc(xr_in, 16)
            pool.dma_start(x1[0:TS, 2, :], x_sample[0]).then_inc(xr_in, 16)
            pool.dma_start(gain[:, :], norm2_g[0:1, :].partition_broadcast(P)).then_inc(gain2_in, 16)

        @block.scalar
        def _(a):
            def split(tile, slot, fill):
                for half in range(2):
                    if half == 0:
                        a.wait_ge(ring_in[slot], 16 * fill)
                    need(a, half_done, 2 * tile + half + 1 - HALVES)
                    a.activation(wH[2 * (slot % 2) + half][:, :, :], ring[slot][:, 8 * half:8 * half + 8, :],
                                 ACT.Copy).then_inc(hi_ready, 1)

            def ahead(base, size, i, u):
                split(base + size * i + u + 2, (u + 2) % RING, base // RING + size // RING * i + (u + 2) // RING + 1)

            def square_sums(f, dst, src):
                a.activation(dst[0:ROWS[f], f, :], src[0:ROWS[f], f, :], ACT.Square,
                             accum_out=ssq[0:ROWS[f], f:f + 1]).then_inc(ssq_ready, 1)

            def roots(nth):
                a.wait_ge(ssq_ready, FT * nth)
                for f in range(FT):
                    a.activation(rms[0:ROWS[f], f:f + 1], ssq[0:ROWS[f], f:f + 1], ACT.Sqrt,
                                 bias=eps_t[0:ROWS[f], :], scale=1.0 / D).then_inc(rms_ready, 1)

            a.wait_ge(x_in, 32)
            a.wait_ge(consts, 15)
            for f in range(FT):
                square_sums(f, xn0, x0)
            roots(1)
            split(0, 0, 1)
            split(1, 1, 1)
            own = Steps(a, act_s)
            a.wait_ge(par_ps, 1)
            own.step(a.activation(prm[:, :], tr[0][:, 0:P], ACT.Copy))
            a.activation(prm2[:, :], tr[1][:, 0:NP2], ACT.Copy).then_inc(par_ready, 1)
            own.settle()
            a.wait_ge(par_ready, 1)
            own.link(a.activation(lz[:, 0, :], prm2[:, C_LAM:C_LAM + KT], ACT.Abs))
            a.activation(lz[:, 1, :], lz[:, 0, :], ACT.Exp, scale=-1.0).then_inc(par_ready, 1)
            for k in range(KT):
                a.wait_ge(h_ps, k + 1)
                a.activation(hH[:, k, :], bank[4 + k % 4][:, 0:T], ACT.Copy,
                             scale=prm[:, C_N1 + k:C_N1 + k + 1]).then_inc(hH_ready, 1)
            a.wait_ge(negh_ready, 1)

            def lru(i):
                for b in range(2):
                    n = 2 * i + b
                    tile = T_LRU + 2 * n
                    ahead(T_LRU, 4, i, 2 * b)
                    a.wait_ge(half_done, 2 * (tile + 1))
                    need(a, xc_ready, n)
                    a.activation(xpad[:, HIST:HIST + TP], acc[0][:, 0:TP], ACT.Copy).then_inc(xb_ready, 1)
                    a.activation(xpad[:, XW - TS:XW], acc[0][:, TP:T], ACT.Copy).then_inc(xb_ready, 1)
                    a.wait_ge(xb_ready, 2 * n + 2)
                    a.sem_inc(acc_used[0], 1)
                    ahead(T_LRU, 4, i, 2 * b + 1)
                    a.wait_ge(half_done, 2 * (tile + 2))
                    need(a, ob_ready, n)
                    a.activation(gy[:, :], acc[1][:, 0:T], ACT.Gelu_apprx_tanh).then_inc(gy_ready, 1)
                    a.wait_ge(gy_ready, n + 1)
                    a.sem_inc(acc_used[1], 1)
                    a.wait_ge(gates_ps, n + 1)
                    own = Steps(a, gates_s, 2 * n)
                    own.step(a.activation(rg[:, :], gateA[:, 0:CW], ACT.Tanh,
                                          bias=hb[:, ds(n, 1)], scale=0.5))
                    own.step(a.activation(ig[:, :], gateX[:, 0:CW], ACT.Tanh,
                                          bias=hb[:, ds(n + KT, 1)], scale=0.5))
                    own.settle()
                    a.activation(th[:, :], rg[:, :], ACT.Tanh, bias=negh[:, ds(n, 1)],
                                 scale=negh[:, ds(n, 1)]).then_inc(th_ready, 1)
                    a.wait_ge(th_ready, 2 * n + 1)
                    a.activation(sq[:, :], th[:, :], ACT.Sqrt).then_inc(th_ready, 1)

            peeled(a, KT // 2, lru)

            def gates(base, m0):
                def body(i):
                    for b in range(2):
                        m = 2 * i + b
                        ahead(base, 4, i, 2 * b)
                        a.wait_ge(half_done, 2 * (base + 2 * m + 1))
                        need(a, mix_ready, m + m0)
                        a.activation(sg[:, :], acc[0][:, 0:T], ACT.Sigmoid).then_inc(sg_ready, 1)
                        a.wait_ge(sg_ready, m + m0 + 1)
                        a.sem_inc(acc_used[0], 1)
                        ahead(base, 4, i, 2 * b + 1)
                peeled(a, KT // 2, body)

            gates(T_PB, 0)
            a.wait_ge(states_ps, 1)
            a.activation(statesT[:, :], tr[0][:, 0:P], ACT.Copy).then_inc(states_ready, 1)
            a.wait_ge(states_ready, 1)
            for dst, lo, hi in ((prompt_conv[0, 0], 0, 48), (sample_conv[0, 0], 48, 96),
                                (prompt_lru[0], 96, 112), (sample_lru[0], 112, 128)):
                a.dma_start(chan(dst), statesT[lo:hi, :]).then_inc(st_out, 16)

            def take(head, i, j, c, dst):
                tile = T_ATT + 3 * head + c
                ahead(T_ATT, 12, i, 3 * j + c)
                a.wait_ge(half_done, 2 * (tile + 1))
                a.activation(dst[:, j % 2, :], acc[(3 * j + c) % 2][:, 0:T], ACT.Copy).then_inc(qkv_ready, 1)
                a.wait_ge(qkv_ready, 3 * head + c + 1)
                a.sem_inc(acc_used[(3 * j + c) % 2], 1)

            def store(src, b, head, prompt, sample):
                a.dma_start(prompt[:, :, ds(head, 1), :], src[:, b, 0:2, :]).then_inc(kv_out[b], 16)
                a.dma_start(sample[0, 0, :, ds(head, 1), :], src[0:TS, b, 2, :]).then_inc(kv_out[b], 16)

            def att1(head, b, nth):
                need(a, kv_out[b], 64 * nth)
                a.wait_ge(ktok_ps, head + 1)
                a.activation(kTok[:, b, 0:2, :], tr[1][:, 0:256].rearrange("p (f d) -> p f d", f=2),
                             ACT.Copy).then_inc(kTok_ready, 1)
                a.activation(kTok[0:TS, b, 2, :], tr[1][0:TS, 256:384], ACT.Copy).then_inc(kTok_ready, 1)
                a.wait_ge(zP_ready, head + 1)
                need(a, wP_ready, head)
                a.activation(sgP[:, :], zP[:, 0:384], ACT.Sigmoid, scale=SCALE).then_inc(sigP_ready, 1)
                a.activation(kpP[:, :], zP[:, 0:384], ACT.Sigmoid, scale=-SCALE).then_inc(sigP_ready, 1)
                a.wait_ge(kTok_ready, 2 * head + 2)
                store(kTok, b, head, pk_v, sample_k)
                a.wait_ge(zS_ready, head + 1)
                need(a, wS_ready, head)
                for dst, s in ((sgS, SCALE), (kpS, -SCALE)):
                    a.activation(dst[:, 0:PAST], zS[0:TS, :], ACT.Sigmoid, scale=s).then_inc(sigS_ready, 1)
                    a.activation(dst[:, PAST:], zN[0:TS, 0:TS], ACT.Sigmoid, scale=s).then_inc(sigS_ready, 1)
                a.wait_ge(vtok_ps, head + 1)
                a.activation(vTok[:, b, 0:2, :], tr[0][:, 0:256].rearrange("p (f d) -> p f d", f=2),
                             ACT.Copy).then_inc(vTok_ready, 1)
                a.activation(vTok[0:TS, b, 2, :], tr[0][0:TS, 256:384], ACT.Copy).then_inc(vTok_ready, 1)
                a.wait_ge(vTok_ready, 2 * head + 2)
                store(vTok, b, head, pv_v, sample_v)

            def att2(head):
                a.wait_ge(pt_ps, head + 1)
                a.activation(pT[:, :], tr[1][:, 0:384], ACT.Copy).then_inc(pT_ready, 1)

            def att3(head):
                a.wait_ge(ov_done, head + 1)
                a.activation(oH[:, ds(head, 1), :], ov[:, 0:T], ACT.Copy).then_inc(oaH_ready, 1)

            def att(i):
                for j in range(4):
                    head = 4 * i + j
                    prev = not (isinstance(head, int) and head == 0)
                    b, nth = (j + 1) % 2, (2 * i + (j - 1) // 2)
                    take(head, i, j, 0, qT)
                    if prev:
                        att1(head - 1, b, nth)
                    take(head, i, j, 1, kT)
                    if prev:
                        att2(head - 1)
                    take(head, i, j, 2, vT)
                    if prev:
                        att3(head - 1)

            peeled(a, H // 4, att)
            att1(H - 1, 1, H // 2 - 1)
            att2(H - 1)
            att3(H - 1)
            gates(T_PA, KT)

            for q in range(4):
                a.wait_ge(mix_ready, KT + 4 * (q + 1))
                a.activation(hH[:, 4 * q:4 * q + 4, :], mixed[:, 4 * q:4 * q + 4, :], ACT.Copy)\
                 .then_inc(mixsplit_s, 1)

            def wo(i, last=False):
                for j in range(4):
                    m = 4 * i + j
                    if not (last and j >= 2):
                        ahead(T_WO, 4, i, j)
                    a.wait_ge(half_done, 2 * (T_WO + m + 1))
                    a.activation(yT[:, j % 2, :], acc[j % 2][:, 0:T], ACT.Copy).then_inc(yT_ready, 1)
                    a.wait_ge(yT_ready, m + 1)
                    a.sem_inc(acc_used[j % 2], 1)
            with a.Fori(0, KT // 4 - 1) as i:
                wo(i)
            wo(KT // 4 - 1, last=True)

            a.wait_ge(x1_ready, KT)
            for f in range(FT):
                square_sums(f, xn, x1)
            roots(2)
            for k in range(KT):
                a.wait_ge(hT_ps, k + 1)
                a.activation(hT[:, k, :], bank[4 + k % 4][:, 0:T], ACT.Copy).then_inc(hT_ready, 1)

            a.wait_ge(lg_ready, 1)
            a.activation(r4[:, 1, :, :], r4[:, 0, :, :], ACT.Exp).then_inc(ge_ready, 1)
            a.wait_ge(dd_ready, 1)
            a.activation(r1[:, 1, :, :], r1[:, 0, :, :], ACT.Exp).then_inc(ed_ready, 1)

            def group(gp):
                a.wait_ge(gt_ps, gp + 1)
                a.activation(GT[:, :], xb2[0][0:CAP, 0:T], ACT.Copy).then_inc(GT_ready, 1)
                a.wait_ge(GT_ready, gp + 1)
                a.sem_inc(x_used[0], 1)
                for q in range(4):
                    a.wait_ge(hg_ps, 4 * gp + q + 1)
                    a.activation(hg[:, 4 * q:4 * q + 4, :],
                                 xb2[q % 2][:, 0:4 * CAP].rearrange("p (k c) -> p k c", k=4),
                                 ACT.Copy).then_inc(hg_ready, 1)
                    a.wait_ge(hg_ready, 4 * gp + q + 1)
                    a.sem_inc(x_used[q % 2], 1)
                for j in range(EPG):
                    a.wait_ge(piece_done, PIECES * (EPG * gp + j) + 4)
                    a.activation(sig[:, :, :], gB[:, 0:FM * CAP].rearrange("p (m c) -> p m c", m=FM),
                                 ACT.Silu).then_inc(silu_ready, 1)
                a.wait_ge(piece_done, PIECES * EPG * (gp + 1))
                for nb in range(2):
                    a.activation(og[:, nb * 512:(nb + 1) * 512], out4[nb][0:CAP, :], ACT.Copy)\
                     .then_inc(og_ready, 1)

            peeled(a, NG, group)
            a.wait_ge(routed, 1)
            n = a.value_load(cnt_i[0:1, 0:1], min_val=0, max_val=T)
            with a.If(n > CAP):
                with a.Fori(NG, NG * CHUNKS) as gp:
                    group(gp)

            a.wait_ge(x1_final, 1)
            for f in range(FT):
                square_sums(f, xn, x1)
            roots(3)
            a.wait_ge(st_out, 64)
            for b in range(2):
                a.wait_ge(kv_out[b], 64 * (H // 2))

        @block.tensor
        def _(pe):
            pe.wait_ge(consts2, 5)
            pe.wait_ge(par_in, 16 * 8)
            pe.transpose(tr[0][:, 0:P], prow[:, :], ident[:, :])
            pe.transpose(tr[1][:, 0:NP2], prow2[:, :], ident[0:NP2, 0:NP2]).then_inc(par_ps, 1)

            def turn(dst, src, f0=0):
                for f in range(FT):
                    ins = pe.transpose(dst[:, f * P:f * P + ROWS[f]], src(f), ident[0:ROWS[f], 0:ROWS[f]])
                return ins

            pe.wait_ge(xn_ready, FT)
            for k in range(KT):
                need(pe, h_ready, k - 3)
                turn(bank[4 + k % 4], lambda f: xn0[0:ROWS[f], f, k * P:(k + 1) * P]).then_inc(h_ps, 1)
            pe.wait_ge(h_ready, KT)

            def tile_product(tile, u, used, rH, rL, parts=False):
                need(pe, acc_used[u % 2], used)
                dst = acc[u % 2][:, 0:T]
                for k in range(KT):
                    half, kk = k // 8, k % 8
                    if kk == 0:
                        pe.wait_ge(lo_ready, 2 * tile + half + 1)
                    if parts and k % 4 == 0:
                        pe.wait_ge(mixsplit_ready, k // 4 + 1)
                    hi, lo = wH[2 * (u % 2) + half][:, kk, :], wL[2 * (u % 2) + half][:, kk, :]
                    pe.matmul(dst, hi, rH[:, k, :], start=(k == 0), stop=False)
                    pe.matmul(dst, hi, rL[:, k, :], start=False, stop=False)
                    ins = pe.matmul(dst, lo, rH[:, k, :], start=False, stop=(k == KT - 1))
                    if kk == 7:
                        ins.then_inc(half_done, 1)

            def lru(i):
                for b in range(2):
                    n = 2 * i + b
                    for c in range(2):
                        tile_product(T_LRU + 4 * i + 2 * b + c, 2 * b + c, T_LRU // 2 + 2 * i + b, hH, hL)
                    pe.wait_ge(xc_ready, n + 1)
                    pe.wait_ge(gw_in[b], 32 * (i + 1))
                    need(pe, th_ready, 2 * n)
                    pe.matmul(gateA[:, 0:CW], gate_w[:, b, 0, :], xc[:, :], start=True, stop=True)
                    pe.matmul(gateX[:, 0:CW], gate_w[:, b, 1, :], xc[:, :], start=True, stop=True)\
                      .then_inc(gates_ps, 1)

            peeled(pe, KT // 2, lru)

            def gated(base, ready, count):
                def body(i):
                    for b in range(2):
                        tile_product(base + 4 * i + 2 * b, 2 * b, base // 2 + 2 * i + b, hH, hL)
                        pe.wait_ge(ready, count)
                        tile_product(base + 4 * i + 2 * b + 1, 2 * b + 1, base // 2 + 2 * i + b, oH, oL)
                with pe.Fori(0, KT // 2) as i:
                    body(i)

            gated(T_PB, ob_ready, KT)
            pe.transpose(tr[0][:, 0:P], states[:, :], ident[:, :]).then_inc(states_ps, 1)
            pe.wait_ge(states_ready, 1)

            def att1(head, b, nth):
                pe.wait_ge(cache_in[b], 32 * (nth + 1))
                pe.wait_ge(qkv_ready, 3 * head + 3)
                need(pe, pS_ready, 2 * head)
                for kb in range(PAST // P):
                    ins = pe.transpose(tr[0][:, kb * P:(kb + 1) * P], cK[:, b, kb, :], ident[:, :])
                ins.then_inc(kc_ps, 1)
                need(pe, pT_ready, head)
                for f in range(FT):
                    ins = pe.transpose(tr[1][0:ROWS[f], f * P:(f + 1) * P],
                                       kT[:, b, f * P:f * P + ROWS[f]], ident[:, :])
                ins.then_inc(ktok_ps, 1)
                need(pe, sigP_ready, 2 * head)
                pe.matmul(zP[:, 0:128], qT[:, b, 0:128], kT[:, b, 0:128], start=True, stop=False,
                          skip_group_check=True)
                pe.matmul(zP[:, 0:128], ident16[:, :], mask16[:, :], start=False, stop=True,
                          skip_group_check=True)
                pe.matmul(zP[:, 128:384], qT[:, b, 128:256], kT[:, b, 0:256], start=True, stop=False,
                          skip_group_check=True)
                pe.matmul(zP[:, 256:384], ident16[:, :], mask16[:, :], start=False, stop=True,
                          skip_group_check=True).then_inc(zP_ready, 1)
                need(pe, sigS_ready, 4 * head)
                pe.matmul(zN[0:TS, 0:TS], qT[:, b, TP:T], kT[:, b, TP:T], start=True, stop=False,
                          skip_group_check=True)
                pe.matmul(zN[0:TS, 0:TS], ident16[:, 0:TS], mask16[:, 0:TS], start=False, stop=True,
                          skip_group_check=True)
                pe.wait_ge(kcT_ready, head + 1)
                pe.matmul(zS[0:TS, :], qT[:, b, TP:T], kcT[:, :], start=True, stop=True).then_inc(zS_ready, 1)
                for f in range(FT):
                    ins = pe.transpose(tr[0][0:ROWS[f], f * P:(f + 1) * P],
                                       vT[:, b, f * P:f * P + ROWS[f]], ident[:, :])
                ins.then_inc(vtok_ps, 1)

            def att2(head):
                pe.wait_ge(wP_ready, head + 1)
                pe.wait_ge(kTok_ready, 2 * head + 2)
                for c in range(3):
                    if c == 2:
                        pe.wait_ge(wS_ready, head + 1)
                        pe.wait_ge(vTok_ready, 2 * head + 2)
                    ins = pe.transpose(tr[1][:, c * P:(c + 1) * P], wP[:, c * P:(c + 1) * P], ident[:, :])
                ins.then_inc(pt_ps, 1)
                for kb in range(PAST // P):
                    pe.transpose(tr[0][:, kb * TS:(kb + 1) * TS], wS[:, kb * P:(kb + 1) * P],
                                 ident[0:TS, 0:TS])
                pe.transpose(tr[0][0:TS, 128:160], wS[:, PAST:PAST + TS], ident[0:TS, 0:TS])\
                  .then_inc(ps_ps, 1)

            def att3(head, b):
                pe.wait_ge(pT_ready, head + 1)
                pe.wait_ge(pS_ready, 2 * head + 2)
                need(pe, oa_ready, head)
                pe.matmul(ov[:, 0:256], vTok[:, b, 0, :], pT[:, 0:256], start=True, stop=False,
                          skip_group_check=True)
                pe.matmul(ov[:, 128:256], vTok[:, b, 1, :], pT[:, 256:384], start=False, stop=True,
                          skip_group_check=True)
                for kb in range(PAST // P):
                    pe.matmul(ov[:, TP:T], cV[:, b, kb, :], pS[:, kb * TS:(kb + 1) * TS],
                              start=(kb == 0), stop=False, skip_group_check=True)
                pe.matmul(ov[:, TP:T], vTok[0:TS, b, 2, :], pS[0:TS, 128:160], start=False, stop=True,
                          skip_group_check=True).then_inc(ov_done, 1)

            def att(i):
                for j in range(4):
                    head = 4 * i + j
                    prev = not (isinstance(head, int) and head == 0)
                    b, nth = (j + 1) % 2, (2 * i + (j - 1) // 2)
                    for c in range(3):
                        u = 3 * j + c
                        tile_product(T_ATT + 12 * i + u, u, T_ATT // 2 + 6 * i + u // 2, hH, hL)
                        if prev:
                            (lambda: att1(head - 1, b, nth), lambda: att2(head - 1),
                             lambda: att3(head - 1, b))[c]()

            peeled(pe, H // 4, att)
            att1(H - 1, 1, H // 2 - 1)
            att2(H - 1)
            att3(H - 1, 1)
            gated(T_PA, oa_ready, H)

            def y_turn(m, b):
                pe.wait_ge(yT_ready, m + 1)
                need(pe, x1_ready, m - 1)
                for f in range(FT):
                    ins = pe.transpose(tr[b][0:ROWS[f], f * P:(f + 1) * P],
                                       yT[:, b, f * P:f * P + ROWS[f]], ident[:, :])
                ins.then_inc(y_ps, 1)

            def wo(i):
                for j in range(4):
                    first = isinstance(i, int) and i == 0 and j == 0
                    tile_product(T_WO + 4 * i + j, j, T_WO // 2 + 2 * i + j // 2, hH, hL, parts=first)
                    if not first:
                        y_turn(4 * i + j - 1, (j + 1) % 2)
            peeled(pe, KT // 4, wo)
            y_turn(KT - 1, 1)

            pe.wait_ge(xn_ready, 2 * FT)
            for k in range(KT):
                need(pe, hT_ready, k - 3)
                turn(bank[4 + k % 4], lambda f: xn[0:ROWS[f], f, k * P:(k + 1) * P]).then_inc(hT_ps, 1)
            pe.wait_ge(hT_ready, KT)
            pe.wait_ge(rw_in, 16 * 7)
            for f in range(FT):
                for k in range(KT):
                    ins = pe.matmul(bank[f][0:ROWS[f], 0:20], hT[:, k, f * P:f * P + ROWS[f]], wr[:, k, :],
                                    start=(k == 0), stop=(k == KT - 1))
            ins.then_inc(lg_ps, 1)
            pe.wait_ge(oh_ready, 1)
            oh = r4[:, 3, :, :]
            for f in range(FT):
                for e in range(f + 1):
                    lhs = before if e == f else ones
                    pe.matmul(bank[4 + f][0:ROWS[f], 0:NG], lhs[0:ROWS[e], 0:ROWS[f]], oh[0:ROWS[e], e, :],
                              start=(e == 0), stop=(e == f))
            for e in range(FT):
                ins = pe.matmul(bank[7][:, 0:NG], ones[0:ROWS[e], :], oh[0:ROWS[e], e, :],
                                start=(e == 0), stop=(e == FT - 1))
            ins.then_inc(pos_ps, 1)
            pe.wait_ge(routed, 1)

            def group(gp):
                pe.wait_ge(G_ready, gp + 1)
                need(pe, x_used[0], 9 * gp)
                for f in range(FT):
                    ins = pe.transpose(xb2[0][0:CAP, f * P:f * P + ROWS[f]], G[0:ROWS[f], f, :],
                                       ident[0:ROWS[f], 0:ROWS[f]])
                ins.then_inc(gt_ps, 1)
                need(pe, x_used[1], 9 * gp)
                for f in range(FT):
                    ins = pe.matmul(xb2[1][:, 0:EPG * CAP], ones[0:ROWS[f], :],
                                    CG[0:ROWS[f], f, :, :].rearrange("p e c -> p (e c)"),
                                    start=(f == 0), stop=(f == FT - 1))
                ins.then_inc(cb_ps, 1)
                for q in range(4):
                    pe.wait_ge(x_used[q % 2], 9 * gp + 1 + q // 2)
                    for kk in range(4):
                        k = 4 * q + kk
                        for f in range(FT):
                            ins = pe.matmul(xb2[q % 2][:, kk * CAP:(kk + 1) * CAP],
                                            xn[0:ROWS[f], f, k * P:(k + 1) * P], G[0:ROWS[f], f, :],
                                            start=(f == 0), stop=(f == FT - 1))
                    ins.then_inc(hg_ps, 1)
                for j in range(EPG):
                    ep = EPG * gp + j
                    need(pe, act_ready, ep)
                    for s in range(4):
                        pe.wait_ge(piece_in[s], 16 * (ep + 1))
                        w = pieces[s][:, :].rearrange("p (k n) -> p k n", k=8)
                        if j == 0 and s < 2:
                            pe.wait_ge(hg_ready, 4 * gp + 2 + 2 * s)
                        dst = gB if s < 2 else uB
                        for k in range(8):
                            for m in range(FM):
                                ins = pe.matmul(dst[:, m * CAP:(m + 1) * CAP], w[:, k, m * P:(m + 1) * P],
                                                hg[:, 8 * (s % 2) + k, :],
                                                start=(s % 2 == 0 and k == 0 and m == 0),
                                                stop=(s % 2 == 1 and k == 7), skip_group_check=True)
                        ins.then_inc(piece_done, 1)
                    pe.wait_ge(act_ready, ep + 1)
                    if j == 0:
                        need(pe, og_ready, 4 * gp)
                    for s in range(2):
                        pe.wait_ge(piece_in[4 + s], 16 * (ep + 1))
                        w = pieces[4 + s][:, :].rearrange("p (k n) -> p k n", k=2)
                        for kk in range(2):
                            m = 2 * s + kk
                            for nb in range(4):
                                ins = pe.matmul(out4[nb][0:CAP, :], act[:, m, :],
                                                w[:, kk, nb * 512:(nb + 1) * 512],
                                                start=(j == 0 and m == 0), stop=(j == EPG - 1 and m == FM - 1))
                        ins.then_inc(piece_done, 1)
                pe.wait_ge(og_ready, 4 * gp + 4)
                pe.wait_ge(GT_ready, gp + 1)
                for u in range(4 * FT):
                    f, nb = u // 4, u % 4
                    pe.wait_ge(x_used[u % 2], 9 * gp + 3 + u // 2)
                    pe.matmul(xb2[u % 2][0:ROWS[f], :], GT[:, f * P:f * P + ROWS[f]],
                              og[:, nb * 512:(nb + 1) * 512], start=True, stop=True).then_inc(sc_ps, 1)

            peeled(pe, NG, group)
            n = pe.value_load(cnt_i[0:1, 0:1], min_val=0, max_val=T)
            with pe.If(n > CAP):
                with pe.Fori(NG, NG * CHUNKS) as gp:
                    group(gp)

        @block.vector
        def _(v):
            own = Steps(v, dve_s)

            def split(tile, slot):
                for half in range(2):
                    hi, lo = wH[2 * (slot % 2) + half], wL[2 * (slot % 2) + half]
                    v.wait_ge(hi_ready, 2 * tile + half + 1)
                    v.tensor_tensor(lo[:, :, :], ring[slot][:, 8 * half:8 * half + 8, :],
                                    hi[:, :, :].bitcast(F32), ALU.subtract).then_inc(lo_ready, 1)

            def ahead(base, size, i, u):
                split(base + size * i + u + 2, (u + 2) % RING)

            def norm(nth, dst_sem, row, xn, x1):
                v.wait_ge(rms_ready, FT * nth)
                for f in range(FT):
                    own.step(v.reciprocal(rstd[0:ROWS[f], f:f + 1], rms[0:ROWS[f], f:f + 1]))
                own.settle()
                for f in range(FT):
                    R = ROWS[f]
                    if row:
                        ins = v.scalar_tensor_tensor(xn[0:R, f, :], x1[0:R, f, :], rstd[0:R, f:f + 1],
                                                     gain[0:R, :], ALU.mult, ALU.mult)
                    else:
                        ins = v.tensor_scalar(xn[0:R, f, :], x1[0:R, f, :], rstd[0:R, f:f + 1], None, ALU.mult)
                    ins.then_inc(dst_sem, 1)

            norm(1, xn_ready, False, xn0, x0)

            split(0, 0)
            split(1, 1)
            v.wait_ge(par_ready, 2)
            own.step(v.tensor_scalar(hb[:, :], prm[:, C_BA:C_N1], 0.5, None, ALU.mult))
            z, s, s2, p = (lz[:, 1, :], lz[:, 2, :], lz[:, 3, :], lz[:, 4, :])
            own.link(v.tensor_scalar(s, z, 2.0, None, ALU.add))
            own.link(v.reciprocal(s, s))
            own.link(v.tensor_tensor(s, s, z, ALU.mult))
            own.link(v.tensor_tensor(s2, s, s, ALU.mult))
            own.link(v.tensor_scalar(p, s2, 1.0 / 17.0, None, ALU.mult))
            for k in (15, 13, 11, 9, 7, 5, 3):
                own.link(v.scalar_tensor_tensor(p, p, 1.0 / k, s2, ALU.add, ALU.mult))
            own.link(v.scalar_tensor_tensor(p, p, 1.0, s, ALU.add, ALU.mult))
            own.link(v.tensor_scalar(s, prm2[:, C_LAM:C_LAM + KT], -1.0, 0.0, ALU.mult, ALU.max))
            own.link(v.tensor_scalar(p, p, 4.0, None, ALU.mult))
            v.scalar_tensor_tensor(negh[:, :], s, 2.0, p, ALU.mult, ALU.add).then_inc(negh_ready, 1)
            for k in range(KT):
                v.wait_ge(hH_ready, k + 1)
                v.scalar_tensor_tensor(hL[:, k, :], bank[4 + k % 4][:, 0:T], prm[:, C_N1 + k:C_N1 + k + 1],
                                       hH[:, k, :].bitcast(F32), ALU.mult, ALU.subtract).then_inc(h_ready, 1)

            states3 = states[:, :].rearrange("p (k n) -> p k n", n=KT)
            hist3 = prm2[:, C_SC:C_SC + HIST * KT].rearrange("p (k n) -> p k n", n=KT)

            LRU_STEPS = 19

            def lru(i):
                for b in range(2):
                    n = 2 * i + b
                    st = Steps(v, lru_s, LRU_STEPS * n)
                    ahead(T_LRU, 4, i, 2 * b)
                    v.wait_ge(xb_ready, 2 * n + 2)
                    st.step(v.tensor_copy(xpad[:, HIST + TP:HIST + TP + HIST], hist3[:, :, ds(n, 1)]))
                    st.settle()
                    need(v, gates_ps, n)
                    st.link(v.tensor_scalar(xc[:, :], xpad[:, 0:CW], prm[:, ds(n + C_CW, 1)],
                                            prm[:, ds(n + C_CB, 1)], ALU.mult, ALU.add))
                    for tap in (1, 2):
                        st.link(v.scalar_tensor_tensor(xc[:, :], xpad[:, tap:tap + CW],
                                                       prm[:, ds(n + C_CW + tap * KT, 1)], xc[:, :],
                                                       ALU.mult, ALU.add))
                    st.step(v.tensor_copy(states3[:, 0:3, ds(n, 1)], xpad[:, TP:TP + HIST]))
                    st.step(v.tensor_copy(states3[:, 3:6, ds(n, 1)], xpad[:, XW - HIST:XW]))
                    st.settle()
                    v.scalar_tensor_tensor(xc[:, :], xpad[:, 3:3 + CW], prm[:, ds(n + C_CW + 3 * KT, 1)],
                                           xc[:, :], ALU.mult, ALU.add).then_inc(xc_ready, 1)
                    ahead(T_LRU, 4, i, 2 * b + 1)
                    v.wait_ge(th_ready, 2 * n + 1)
                    v.wait_ge(xc_ready, n + 1)
                    st.link(v.tensor_scalar(t1[:, :], th[:, :], 1.0, None, ALU.add))
                    st.step(v.reciprocal(rc[:, :], t1[:, :]))
                    v.wait_ge(th_ready, 2 * n + 2)
                    st.link(v.scalar_tensor_tensor(uu[:, :], ig[:, :], 1.0, xc[:, :], ALU.add, ALU.mult))
                    st.step(v.tensor_scalar(aa[:, :], rc[:, :], 2.0, -1.0, ALU.mult, ALU.add))
                    st.link(v.tensor_tensor(uu[:, :], uu[:, :], sq[:, :], ALU.mult))
                    st.link(v.tensor_tensor(uu[:, :], uu[:, :], rc[:, :], ALU.mult))
                    st.step(v.memset(aa[:, S0 - 1:S0], 0.0))
                    st.link(v.tensor_copy(uu[:, S0 - 1:S0], prm2[:, ds(n + C_H0, 1)]))
                    st.link(v.tensor_tensor_scan(hs[:, :], aa[:, :], uu[:, :], 0.0, ALU.mult, ALU.add))
                    st.step(v.tensor_copy(states3[:, 6:7, ds(n, 1)], hs[:, TP - 1:TP]))
                    st.step(v.tensor_copy(states3[:, 7:8, ds(n, 1)], hs[:, CW - 1:CW]))
                    v.wait_ge(gy_ready, n + 1)
                    st.step(v.tensor_tensor(ob[:, 0:TP], gy[:, 0:TP], hs[:, 0:TP], ALU.mult))
                    st.link(v.tensor_tensor(ob[:, TP:T], gy[:, TP:T], hs[:, S0:CW], ALU.mult))
                    v.tensor_copy(oH[:, ds(n, 1), :], ob[:, :]).then_inc(oH_s, 1)
                    v.wait_ge(oH_s, n + 1)
                    v.tensor_tensor(oL[:, ds(n, 1), :], ob[:, :], oH[:, ds(n, 1), :].bitcast(F32), ALU.subtract)\
                     .then_inc(ob_ready, 1)
                    assert st.n == LRU_STEPS, st.n

            peeled(v, KT // 2, lru)

            def gated(base, m0, add):
                def body(i):
                    for b in range(2):
                        m = 2 * i + b
                        ahead(base, 4, i, 2 * b)
                        v.wait_ge(half_done, 2 * (base + 2 * m + 2))
                        v.wait_ge(sg_ready, m + m0 + 1)
                        if not add:
                            v.tensor_tensor(mixed[:, ds(m, 1), :], acc[1][:, 0:T], sg[:, :], ALU.mult)\
                             .then_inc(acc_used[1], 1)
                        else:
                            v.tensor_tensor(mx[:, :], acc[1][:, 0:T], sg[:, :], ALU.mult)\
                             .then_inc(acc_used[1], 1)
                        v.wait_ge(acc_used[1], base // 2 + m + 1)
                        if not add:
                            v.sem_inc(mix_ready, 1)
                        else:
                            v.tensor_tensor(mixed[:, ds(m, 1), :], mixed[:, ds(m, 1), :], mx[:, :], ALU.add)\
                             .then_inc(mix_ready, 1)
                        ahead(base, 4, i, 2 * b + 1)
                with v.Fori(0, KT // 2) as i:
                    body(i)

            gated(T_PB, 0, False)

            def att1(head):
                v.wait_ge(kc_ps, head + 1)
                need(v, zS_ready, head)
                v.tensor_copy(kcT[:, :], tr[0][:, :]).then_inc(kcT_ready, 1)
                v.wait_ge(sigP_ready, 2 * head + 2)
                v.tensor_tensor_scan(rP[:, 0:128][:, ::-1], kpP[:, 0:128][:, ::-1], kpP[:, 0:128][:, ::-1],
                                     1.0, ALU.mult, ALU.bypass).then_inc(scan_s, 1)
                v.tensor_tensor_scan(rP[:, 129:385][:, ::-1], kpP[:, 128:384][:, ::-1],
                                     kpP[:, 128:384][:, ::-1], 1.0, ALU.mult, ALU.bypass).then_inc(scan_s, 1)
                v.wait_ge(scan_s, 3 * head + 2)
                need(v, pt_ps, head)
                v.tensor_tensor(wP[:, 0:128], sgP[:, 0:128], rP[:, 1:129], ALU.mult).then_inc(mix_s, 1)
                v.tensor_tensor(wP[:, 128:384], sgP[:, 128:384], rP[:, 130:386], ALU.mult).then_inc(mix_s, 1)
                v.wait_ge(mix_s, 2 * head + 2)
                v.sem_inc(wP_ready, 1)
                v.wait_ge(sigS_ready, 4 * head + 4)
                n = PAST + TS
                v.tensor_tensor_scan(rS[:, 0:n][:, ::-1], kpS[:, :][:, ::-1], kpS[:, :][:, ::-1],
                                     1.0, ALU.mult, ALU.bypass).then_inc(scan_s, 1)
                v.wait_ge(scan_s, 3 * head + 3)
                need(v, ps_ps, head)
                v.tensor_tensor(wS[:, :], sgS[:, :], rS[:, 1:n + 1], ALU.mult).then_inc(wS_ready, 1)

            def att2(head):
                v.wait_ge(ps_ps, head + 1)
                need(v, ov_done, head)
                v.tensor_copy(pS[:, 0:128], tr[0][:, 0:128]).then_inc(pS_ready, 1)
                v.tensor_copy(pS[0:TS, 128:160], tr[0][0:TS, 128:160]).then_inc(pS_ready, 1)

            def att3(head):
                v.wait_ge(oaH_ready, head + 1)
                v.tensor_tensor(oL[:, ds(head, 1), :], ov[:, 0:T], oH[:, ds(head, 1), :].bitcast(F32),
                                ALU.subtract).then_inc(oa_ready, 1)

            def att(i):
                for j in range(4):
                    head = 4 * i + j
                    for c, step in enumerate((att1, att2, att3)):
                        ahead(T_ATT, 12, i, 3 * j + c)
                        if not (isinstance(head, int) and head == 0):
                            step(head - 1)

            v.wait_ge(consts, 15)
            peeled(v, H // 4, att)
            att1(H - 1)
            att2(H - 1)
            att3(H - 1)

            gated(T_PA, KT, True)

            for q in range(4):
                v.wait_ge(mixsplit_s, q + 1)
                c = slice(4 * q, 4 * q + 4)
                v.tensor_tensor(hL[:, c, :], mixed[:, c, :], hH[:, c, :].bitcast(F32), ALU.subtract)\
                 .then_inc(mixsplit_ready, 1)

            v.wait_ge(xr_in, 32)

            def residual(i, last=False):
                for j in range(4):
                    m = 4 * i + j - 1
                    if not (last and j >= 2):
                        ahead(T_WO, 4, i, j)
                    if not (isinstance(m, int) and m < 0):
                        add_tile(m, (j + 1) % 2)

            def add_tile(m, j):
                if True:
                    v.wait_ge(y_ps, m + 1)
                    c = ds(m * P, P)
                    v.tensor_tensor(x1[:, 0:2, c], tr[j][:, 0:256].rearrange("p (f d) -> p f d", f=2),
                                    x1[:, 0:2, c], ALU.add).then_inc(mix_s, 1)
                    v.tensor_tensor(x1[0:TS, 2, c], tr[j][0:TS, 256:384], x1[0:TS, 2, c], ALU.add)\
                     .then_inc(mix_s, 1)
                    v.wait_ge(mix_s, 2 * H + 2 * m + 2)
                    v.sem_inc(x1_ready, 1)
            residual(0)
            with v.Fori(1, KT // 4 - 1) as i:
                residual(i)
            residual(KT // 4 - 1, last=True)
            add_tile(KT - 1, 1)

            v.wait_ge(gain2_in, 16)
            norm(2, xn_ready, True, xn, x1)

            for t, c in ((lg, 0.0), (pos, 0.0)):
                own.step(v.memset(t[:, :, :], c))
            own.settle()
            v.wait_ge(rw_in, 16 * 7)
            v.wait_ge(lg_ps, 1)
            for f in range(FT):
                own.step(v.tensor_tensor(lg[0:ROWS[f], f, :], bank[f][0:ROWS[f], 0:20], br[0:ROWS[f], :], ALU.add))
            own.settle()

            def bc(t, n=4):
                return t.to_broadcast([P, FT, n])

            f4 = first4[:, :].rearrange("p (a c) -> p a c", a=1).to_broadcast([P, FT, 4])

            def first_max(x, top, one, tmp):
                own.link(v.tensor_reduce(top, x, AX.X, ALU.max))
                own.link(v.tensor_tensor(tmp, x, bc(top), ALU.is_equal))
                own.link(v.tensor_tensor(tmp, tmp, f4, ALU.mult))
                own.link(v.tensor_reduce(r1[:, 5, :, :], tmp, AX.X, ALU.max))
                own.link(v.tensor_tensor(one, tmp, bc(r1[:, 5, :, :]), ALU.is_equal))

            oh = r4[:, 3, :, :]
            first_max(lg[:, :, 0:4], m1[:, :, :], oh, r4[:, 2, :, :])
            own.link(v.tensor_tensor(r4[:, 0, :, :], lg[:, :, 0:4], bc(m1[:, :, :]), ALU.subtract))
            v.sem_inc(lg_ready, 1)
            v.sem_inc(oh_ready, 1)
            own.link(v.tensor_tensor(psel[:, :, :, :], lg[:, :, 4:20].rearrange("p f (g e) -> p f g e", g=4),
                                     oh.rearrange("p f (g a) -> p f g a", a=1).to_broadcast([P, FT, 4, 4]),
                                     ALU.mult))
            sel, one1, one2, cut = r4[:, 4, :, :], r4[:, 5, :, :], r4[:, 6, :, :], r4[:, 7, :, :]
            own.link(v.tensor_reduce(sel, psel[:, :, :, :].rearrange("p f g e -> p f e g"), AX.X, ALU.add))
            first_max(sel, r1[:, 2, :, :], one1, r4[:, 2, :, :])
            own.link(v.scalar_tensor_tensor(cut, one1, NEG, sel, ALU.mult, ALU.add))
            first_max(cut, r1[:, 3, :, :], one2, r4[:, 2, :, :])
            own.link(v.tensor_tensor(r1[:, 0, :, :], r1[:, 3, :, :], r1[:, 2, :, :], ALU.subtract))
            v.sem_inc(dd_ready, 1)
            v.wait_ge(ge_ready, 1)
            own.link(v.tensor_reduce(pg[:, :, :], r4[:, 1, :, :], AX.X, ALU.add))
            own.link(v.reciprocal(pg[:, :, :], pg[:, :, :]))
            v.wait_ge(ed_ready, 1)
            own.link(v.tensor_scalar(r1[:, 2, :, :], r1[:, 1, :, :], 1.0, None, ALU.add))
            own.link(v.reciprocal(r1[:, 2, :, :], r1[:, 2, :, :]))
            own.link(v.tensor_tensor(r1[:, 2, :, :], r1[:, 2, :, :], pg[:, :, :], ALU.mult))
            own.link(v.tensor_tensor(r1[:, 3, :, :], r1[:, 2, :, :], r1[:, 1, :, :], ALU.mult))
            own.link(v.tensor_tensor(one1, one1, bc(r1[:, 2, :, :]), ALU.mult))
            own.link(v.tensor_tensor(one2, one2, bc(r1[:, 3, :, :]), ALU.mult))
            own.link(v.tensor_tensor(one1, one1, one2, ALU.add))
            own.link(v.tensor_tensor(comb[:, :, :].rearrange("p f (g e) -> p f g e", g=4),
                                     oh.rearrange("p f (g a) -> p f g a", a=1).to_broadcast([P, FT, 4, 4]),
                                     one1.rearrange("p f (a e) -> p f a e", a=1).to_broadcast([P, FT, 4, 4]),
                                     ALU.mult))
            v.wait_ge(pos_ps, 1)
            for f in range(FT):
                own.step(v.tensor_copy(pos[0:ROWS[f], f, :], bank[4 + f][0:ROWS[f], 0:NG]))
            own.link(v.tensor_scalar(r4[:, 8, :, :], oh, -1.0e6, 1.0e6, ALU.mult, ALU.add))
            own.link(v.tensor_tensor(pos[:, :, :], pos[:, :, :], r4[:, 8, :, :], ALU.add))
            own.link(v.tensor_reduce(cmax[:, :], bank[7][:, 0:NG], AX.X, ALU.max))
            v.tensor_copy(cnt_i[:, :], cmax[:, :]).then_inc(routed, 1)

            GS = 2 * FT

            def group(gp, g, c0):
                v.wait_ge(consts2, 5)
                need(v, hg_ps, 4 * gp)
                for f in range(FT):
                    v.tensor_scalar(G[:, f, :], slots[:, c0:c0 + CAP], pos[:, f, ds(g, 1)], None,
                                    ALU.is_equal).then_inc(G_s, 1)
                v.wait_ge(G_s, GS * gp + FT)
                for f in range(FT):
                    v.tensor_tensor(CG[:, f, :, :],
                                    G[:, f, :].rearrange("p (a c) -> p a c", a=1).to_broadcast([P, EPG, CAP]),
                                    comb[:, f, ds(4 * g, 4)].rearrange("p (e a) -> p e a", a=1)
                                    .to_broadcast([P, EPG, CAP]), ALU.mult).then_inc(G_s, 1)
                v.wait_ge(G_s, GS * gp + 2 * FT)
                v.sem_inc(G_ready, 1)
                v.wait_ge(cb_ps, gp + 1)
                v.tensor_copy(cB[:, :, :], xb2[1][:, 0:EPG * CAP].rearrange("p (e c) -> p e c", e=EPG))\
                 .then_inc(x_used[1], 1)
                v.wait_ge(x_used[1], 9 * gp + 1)
                for j in range(EPG):
                    ep = EPG * gp + j
                    v.wait_ge(silu_ready, ep + 1)
                    v.tensor_tensor(sig[:, :, :], sig[:, :, :],
                                    uB[:, 0:FM * CAP].rearrange("p (m c) -> p m c", m=FM), ALU.mult)\
                     .then_inc(act_s2, 1)
                    v.wait_ge(act_s2, ep + 1)
                    v.tensor_tensor(act[:, :, :], sig[:, :, :],
                                    cB[:, j, :].rearrange("p (a c) -> p a c", a=1).to_broadcast([P, FM, CAP]),
                                    ALU.mult).then_inc(act_ready, 1)
                v.wait_ge(piece_done, PIECES * EPG * (gp + 1))
                for nb in range(2, 4):
                    v.tensor_copy(og[:, nb * 512:(nb + 1) * 512], out4[nb][0:CAP, :]).then_inc(og_ready, 1)
                for u in range(4 * FT):
                    f, nb = u // 4, u % 4
                    c = slice(nb * 512, (nb + 1) * 512)
                    v.wait_ge(sc_ps, 4 * FT * gp + u + 1)
                    v.tensor_tensor(x1[0:ROWS[f], f, c], xb2[u % 2][0:ROWS[f], :], x1[0:ROWS[f], f, c], ALU.add)\
                     .then_inc(x_used[u % 2], 1)
                for b in range(2):
                    v.wait_ge(x_used[b], 9 * gp + 9)

            v.wait_ge(routed, 1)
            peeled(v, NG, lambda g: group(g, g, 0))
            n = v.value_load(cnt_i[0:1, 0:1], min_val=0, max_val=T)
            with v.If(n > CAP):
                for c in range(1, CHUNKS):
                    with v.Fori(0, NG) as g:
                        group(g + NG * c, g, c * CAP)
            v.memset(ssq[:, :], 0.0).then_inc(x1_final, 1)
            v.wait_ge(gain_in, 16)
            norm(3, yo_ready, True, xn, x1)


INS = ["x_prompt", "x_sample", "cache_k", "cache_v", "state_conv", "state_lru", "norm1_g", "w_in",
       "conv_w", "conv_b", "lru_wa", "lru_ba", "lru_wx", "lru_bx", "lru_lambda", "w_pa", "w_pb", "w_o",
       "norm2_g", "router_group_w", "router_group_b", "router_sub_w", "router_sub_b", "expert_w_up",
       "expert_w_down", "final_norm_g"]
OUTS = [(1, TP, D), (1, TS, D), (1, 1, TP, H, P), (1, 1, TP, H, P), (1, 1, HIST, D), (1, 1, D),
        (1, 1, TS, H, P), (1, 1, TS, H, P), (1, 1, HIST, D), (1, 1, D)]


def kernel(**inputs):
    import numpy as np
    import concourse.bacc as bacc
    from concourse.bass_utils import run_bass_kernel_spmd

    nc = bacc.Bacc("TRN2", target_bir_lowering=False, num_devices=1)
    arrays, args = {}, []
    for name in INS:
        a = np.ascontiguousarray(inputs[name])
        arrays[f"in_{name}"] = a
        args.append(nc.dram_tensor(f"in_{name}", a.shape, mybir.dt.from_np(a.dtype), kind="ExternalInput").ap())
    for i, shape in enumerate(OUTS):
        args.append(nc.dram_tensor(f"out_{i}", shape, F32, kind="ExternalOutput").ap())
    build(nc, *args)
    r = run_bass_kernel_spmd(nc, [arrays], core_ids=[0])
    return tuple(r.results[0][f"out_{i}"] for i in range(len(OUTS)))
```

```python
from contextlib import ExitStack

import concourse.bass as bass
from concourse import mybir

F32 = mybir.dt.float32
F32R = mybir.dt.float32r
BF16 = mybir.dt.bfloat16
I32 = mybir.dt.int32
ALU = mybir.AluOpType
ACT = mybir.ActivationFunctionType
AX = mybir.AxisListType

P = 128
D = 2048
KT = D // P
TP, TS = 256, 32
T = TP + TS
FT = 3
ROWS = [P, P, TS]
H = 16
PAST = 512
SCALE = float(P) ** -0.5
CONV = 4
HIST = CONV - 1
XW = HIST + TP + HIST + TS
CW = TP + HIST + TS
S0 = TP + HIST
NG, EPG, FF = 4, 4, 512
NE = NG * EPG
FM = FF // P
CAP = 96
CHUNKS = T // CAP
EPS = 1e-6
LRU_C = 8.0
NEG = -1.0e30
RING = 4
HALVES = 4
RAW = 6
PU, PD = KT // 2, FM
PIECES = PU + PD
GP = EPG * PIECES
GH = 2 * GP
AHEAD = 2

ORDER = [(0, s) for s in range(PU)]
for _j in range(EPG):
    _up = [(_j + 1, s) for s in range(PU)] if _j + 1 < EPG else []
    ORDER += _up[:AHEAD] + [(_j, PU + s) for s in range(PD)] + _up[AHEAD:]
GATED = [2 * (ORDER.index((j, PU - 1)) + 1) for j in range(EPG)]
TURNED = [h + (2 if j + 1 < EPG else 0) for j, h in enumerate(GATED)]

T_LRU = 0
T_PB = T_LRU + 2 * KT
T_ATT = T_PB + 2 * KT
T_PA = T_ATT + 3 * H
T_WO = T_PA + 2 * KT
T_END = T_WO + KT
COL = {"q": 0, "k": D, "v": 2 * D, "xb": 3 * D, "y": 4 * D, "ga": 5 * D, "gb": 6 * D}

C_CW, C_CB, C_BA, C_BX, C_N1 = 0, 64, 80, 96, 112
C_LAM, C_H0, C_SC = 0, 16, 32
NP2 = 80
HG_BANK = (6, 7, 4, 5)


def need(eng, sem, value):
    if isinstance(value, int) and value <= 0:
        return
    eng.wait_ge(sem, value)


class Steps:

    def __init__(self, eng, sem, base=0):
        self.eng, self.sem, self.base, self.n = eng, sem, base, 0

    def step(self, ins):
        self.n += 1
        ins.then_inc(self.sem, 1)

    def settle(self):
        self.eng.wait_ge(self.sem, self.base + self.n)

    def link(self, ins):
        self.step(ins)
        self.settle()


def peeled(eng, n, body):
    body(0)
    with eng.Fori(1, n) as i:
        body(i)


def build(nc, x_prompt, x_sample, cache_k, cache_v, state_conv, state_lru, norm1_g, w_in, conv_w,
          conv_b, lru_wa, lru_ba, lru_wx, lru_bx, lru_lambda, w_pa, w_pb, w_o, norm2_g,
          router_group_w, router_group_b, router_sub_w, router_sub_b, expert_w_up, expert_w_down,
          final_norm_g, y_prompt, y_sample, prompt_k, prompt_v, prompt_conv, prompt_lru,
          sample_k, sample_v, sample_conv, sample_lru):
    ds = bass.ds

    here = [nc.sbuf_base]

    def sb(name, shape, dt=F32):
        size = 2 if dt == BF16 else 4
        for s in shape[1:]:
            size *= s
        here[0] = (here[0] + 31) // 32 * 32
        t = nc.alloc_sbuf_tensor_at(name, shape, dt, offset=here[0])
        here[0] += size
        return t

    ident = sb("ident", [P, P])
    ones = sb("ones", [P, P])
    before = sb("before", [P, P])
    ident16 = sb("ident16", [P, P], BF16)
    mask16 = sb("mask16", [P, P], BF16)
    slots_i = sb("slots_i", [P, T], I32)
    slots = sb("slots", [P, T])
    first4 = sb("first4", [P, 4])
    eps_t = sb("eps_t", [P, 1])
    prm = sb("prm", [P, P])
    prm2 = sb("prm2", [P, NP2])
    ssq = sb("ssq", [P, FT])
    rms = sb("rms", [P, FT])
    rstd = sb("rstd", [P, FT])
    mark = here[0]

    hH = sb("hH", [P, KT, T], F32R)
    hL = sb("hL", [P, KT, T], F32R)
    at_o = here[0]
    oH = sb("oH", [P, KT, T], F32R)
    oL = sb("oL", [P, KT, T], F32R)
    under = here[0]
    xc = sb("xc", [P, 2, CW])
    ct = sb("ct", [P, CW])
    cw = sb("cw", [P, 2, 5])
    rg = sb("rg", [P, CW])
    ig = sb("ig", [P, CW])
    th = sb("th", [P, CW])
    sq = sb("sq", [P, CW])
    t1 = sb("t1", [P, CW])
    rc = sb("rc", [P, CW])
    uu = sb("uu", [P, CW])
    aa = sb("aa", [P, CW])
    hs = sb("hs", [P, CW])
    gy = sb("gy", [P, T])
    ob = sb("ob", [P, T])
    lru_end = here[0]
    here[0] = under
    qT = sb("qT", [P, 2, T])
    kT = sb("kT", [P, 2, T])
    vT = sb("vT", [P, 2, T])
    kTok = sb("kTok", [P, 2, FT, P])
    vTok = sb("vTok", [P, 2, FT, P])
    cK = sb("cK", [P, 2, PAST // P, P])
    cV = sb("cV", [P, 2, PAST // P, P])
    kcT = sb("kcT", [P, PAST])
    assert lru_end <= here[0]
    sgP = sb("sgP", [P, 384])
    kpP = sb("kpP", [P, 384])
    rP = sb("rP", [P, 386])
    wP = sb("wP", [P, 384])
    pT = sb("pT", [P, 384])
    sgS = sb("sgS", [TS, PAST + TS])
    kpS = sb("kpS", [TS, PAST + TS])
    rS = sb("rS", [TS, PAST + TS + 1])
    wS = sb("wS", [TS, PAST + TS])
    pS = sb("pS", [P, 160])
    at_mixed = here[0]
    mixed = sb("mixed", [P, KT, T])
    at_ring = here[0]
    ring = [sb(f"ring{s}", [P, KT, P]) for s in range(RING)]
    wH = [sb(f"wH{s}", [P, KT // 2, P], F32R) for s in range(HALVES)]
    wL = [sb(f"wL{s}", [P, KT // 2, P], F32R) for s in range(HALVES)]
    at_prow = here[0]
    prow = sb("prow", [P, P])
    prow2 = sb("prow2", [NP2, P])
    xpad = sb("xpad", [P, XW])
    gate_w = sb("gate_w", [P, 2, 2, P])
    negh = sb("negh", [P, KT])
    hb = sb("hb", [P, 2 * KT])
    lz = sb("lz", [P, 5, KT])
    states = sb("states", [P, P])
    statesT = sb("statesT", [P, P])
    sg = sb("sg", [P, T])
    mx = sb("mx", [P, T])
    end1 = here[0]
    here[0] = at_prow
    yT = sb("yT", [P, 2, T])

    here[0] = at_o
    x0 = sb("x0", [P, FT, D])
    xn0 = sb("xn0", [P, FT, D])
    assert here[0] <= at_mixed

    here[0] = mark
    at_xn = here[0]
    xn = sb("xn", [P, FT, D])
    here[0] = at_xn
    xnL = sb("xnL", [P, FT, D], F32R)
    hgH = sb("hgH", [P, KT, CAP], F32R)
    hgL = sb("hgL", [P, KT, CAP], F32R)
    assert here[0] <= at_o
    here[0] = at_o
    raw = [sb(f"raw{s}", [P, 2048]) for s in range(RAW)]
    x1 = sb("x1", [P, FT, D])
    assert here[0] <= at_mixed
    at_split = here[0] = at_mixed
    sH = [sb(f"sH{s}", [P, 1024], F32R) for s in range(HALVES)]
    after_sH = here[0]
    here[0] = at_split
    gain = sb("gain", [P, D])
    wr = sb("wr", [P, KT, 20])
    br = sb("br", [P, 20])
    assert here[0] <= min(after_sH, at_ring)
    here[0] = after_sH
    sL = [sb(f"sL{s}", [P, 1024], F32R) for s in range(HALVES)]
    xnH = sb("xnH", [P, FT, D], F32R)
    lg = sb("lg", [P, FT, 20])
    m1 = sb("m1", [P, FT, 1])
    r4 = sb("r4", [P, 9, FT, 4])
    pg = sb("pg", [P, FT, 1])
    r1 = sb("r1", [P, 6, FT, 1])
    psel = sb("psel", [P, FT, 4, 4])
    comb = sb("comb", [P, FT, NE])
    pos = sb("pos", [P, FT, NG + 1])
    cmax = sb("cmax", [P, 1])
    cnt_i = sb("cnt_i", [P, 1], I32)
    cs = sb("cs", [CAP, EPG])
    silu = sb("silu", [CAP, FF])
    act = sb("act", [CAP, FF])
    atH = sb("atH", [P, FM, CAP], F32R)
    atL = sb("atL", [P, FM, CAP], F32R)
    at_hT = here[0]
    hT = sb("hT", [P, KT, T])
    lgT = sb("lgT", [20, T])
    end2 = here[0]
    here[0] = at_hT
    ogH = sb("ogH", [CAP, D], F32R)
    ogL = sb("ogL", [CAP, D], F32R)
    tok = sb("tok", [CAP, D])
    G = sb("G", [P, FT, CAP], F32R)
    GT = sb("GT", [CAP, T], F32R)
    assert max(here[0], end1, end2) <= nc.sbuf_usable_end, (here[0], end1, end2, nc.sbuf_usable_end)

    xp = x_prompt.rearrange("a (f p) d -> p (a f) d", p=P)
    yp = y_prompt.rearrange("a (f p) d -> p (a f) d", p=P)
    w_in_v = w_in[0].rearrange("(k p) n -> p k n", p=P)
    w_pa_v = w_pa[0].rearrange("(k p) n -> p k n", p=P)
    w_pb_v = w_pb[0].rearrange("(k p) n -> p k n", p=P)
    w_o_v = w_o[0].rearrange("(k p) n -> p k n", p=P)
    wa_v = lru_wa[0].rearrange("n c d -> c n d")
    wx_v = lru_wx[0].rearrange("n c d -> c n d")
    ck_v = cache_k[0, 0].rearrange("(b p) h d -> p b h d", p=P)
    cv_v = cache_v[0, 0].rearrange("(b p) h d -> p b h d", p=P)
    pk_v = prompt_k[0, 0].rearrange("(f p) h d -> p f h d", p=P)
    pv_v = prompt_v[0, 0].rearrange("(f p) h d -> p f h d", p=P)
    up_v = expert_w_up[0].rearrange("e (k p) n -> p e k n", p=P)
    dn_v = expert_w_down[0].rearrange("e (k p) n -> p e k n", p=P)

    def chan(a):
        return a.rearrange("r (n p) -> (r n) p", p=P)

    with ExitStack() as ctx:
        def sem(name):
            return ctx.enter_context(nc.semaphore(name))

        bank = [ctx.enter_context(nc.psum_tensor(f"bank{i}", [P, 512], F32)) for i in range(8)]
        acc = bank[0:2]
        tr = bank[2:4]
        zP, zS, zN, ov = bank[4:8]
        gateA, gateX = bank[4:6]
        out4 = bank[0:4]
        pair = [bank[6:8], bank[4:6]]

        x_in = [sem(f"x_in{f}") for f in range(FT)]
        par_in, rw_in, gain_in = sem("par_in"), sem("rw_in"), sem("gain_in")
        ring_in = [sem(f"ring_in{s}") for s in range(RING)]
        raw_in = [sem(f"raw_in{s}") for s in range(RAW)]
        gw_in = [sem(f"gw_in{s}") for s in range(2)]
        cache_in = [sem(f"cache_in{s}") for s in range(2)]
        kv_out = [sem(f"kv_out{s}") for s in range(2)]
        st_out, y_out = sem("st_out"), sem("y_out")
        consts, consts2 = sem("consts"), sem("consts2")
        act_s, dve_s = sem("act_s"), sem("dve_s")
        par_ps, par_ready, negh_ready = sem("par_ps"), sem("par_ready"), sem("negh_ready")
        ssq_ready, rms_ready, xn_ready = sem("ssq_ready"), sem("rms_ready"), sem("xn_ready")
        h_ps, hH_ready, h_ready = sem("h_ps"), sem("hH_ready"), sem("h_ready")
        hi_ready, lo_ready = sem("hi_ready"), sem("lo_ready")
        half_done = sem("half_done")
        mixsplit_s, mixsplit_ready = sem("mixsplit_s"), sem("mixsplit_ready")
        xr_in, gain2_in = sem("xr_in"), sem("gain2_in")
        go_ready = sem("go_ready")
        oaH_ready, oH_s = sem("oaH_ready"), sem("oH_s")
        acc_used = [sem(f"acc_used{b}") for b in range(2)]
        uu_ready, cw_ready, tails_ready = sem("uu_ready"), sem("cw_ready"), sem("tails_ready")
        xb_ready, conv_s, xc_ready = sem("xb_ready"), sem("conv_s"), sem("xc_ready")
        gates_ps, gates_s, th_ready = sem("gates_ps"), sem("gates_s"), sem("th_ready")
        gy_ready, lru_s, ob_ready = sem("gy_ready"), sem("lru_s"), sem("ob_ready")
        states_ps, states_ready = sem("states_ps"), sem("states_ready")
        sg_ready, mix_s, mix_ready = sem("sg_ready"), sem("mix_s"), sem("mix_ready")
        qkv_ready = sem("qkv_ready")
        kc_ps, kcT_ready = sem("kc_ps"), sem("kcT_ready")
        ktok_ps, kTok_ready = sem("ktok_ps"), sem("kTok_ready")
        vtok_ps, vTok_ready = sem("vtok_ps"), sem("vTok_ready")
        zP_ready, zS_ready = sem("zP_ready"), sem("zS_ready")
        sigP_ready, sigS_ready = sem("sigP_ready"), sem("sigS_ready")
        scan_s, wP_ready, wS_ready = sem("scan_s"), sem("wP_ready"), sem("wS_ready")
        pt_ps, pT_ready = sem("pt_ps"), sem("pT_ready")
        ps_ps, pS_ready = sem("ps_ps"), sem("pS_ready")
        ov_done, oa_ready = sem("ov_done"), sem("oa_ready")
        yT_ready, y_ps, x1_ready = sem("yT_ready"), sem("y_ps"), sem("x1_ready")
        hT_ps, hT_ready = sem("hT_ps"), sem("hT_ready")
        lgT_ps, lgT_ready = sem("lgT_ps"), sem("lgT_ready")
        lg_ps, lg_ready, ge_ready, dd_ready, ed_ready = (sem("lg_ps"), sem("lg_ready"), sem("ge_ready"),
                                                         sem("dd_ready"), sem("ed_ready"))
        oh_ready, pos_ps, routed = sem("oh_ready"), sem("pos_ps"), sem("routed")
        G_ready, gt_ps, cs_ps, hg_ps = sem("G_ready"), sem("gt_ps"), sem("cs_ps"), sem("hg_ps")
        GT_ready, cs_ready = sem("GT_ready"), sem("cs_ready")
        tok_ps, tok_ready = sem("tok_ps"), sem("tok_ready")
        hgH_ready, hgL_ready = sem("hgH_ready"), sem("hgL_ready")
        sH_ready, sL_ready, eh_done = sem("sH_ready"), sem("sL_ready"), sem("eh_done")
        silu_ready, act_ready, at_ps = sem("silu_ready"), sem("act_ready"), sem("at_ps")
        atH_ready, atL_ready = sem("atH_ready"), sem("atL_ready")
        ogH_ready, ogL_ready = sem("ogH_ready"), sem("ogL_ready")
        xnH_ready, xnL_ready = sem("xnH_ready"), sem("xnL_ready")
        added = sem("added")
        last_ps, last_added = sem("last_ps"), sem("last_added")
        sc_ps = sem("sc_ps")
        x1_final = sem("x1_final")
        yo_ready = sem("yo_ready")

        states3 = states[:, :].rearrange("p (k n) -> p k n", n=KT)
        taps3 = prm[:, C_CW:C_BA].rearrange("p (k n) -> p k n", n=KT)
        hist3 = prm2[:, C_SC:C_SC + HIST * KT].rearrange("p (k n) -> p k n", n=KT)

        block = ctx.enter_context(nc.Block())

        @block.sync
        def _(sp):
            for f in range(2):
                sp.dma_start(x0[:, f, :], xp[:, f, :]).then_inc(x_in[f], 16)
            sp.dma_start(x0[0:TS, 2, :], x_sample[0]).then_inc(x_in[2], 16)
            for dst, src in ((prow[C_CW:C_CB, :], chan(conv_w[0])), (prow[C_CB:C_BA, :], chan(conv_b)),
                             (prow[C_BA:C_BX, :], chan(lru_ba)), (prow[C_BX:C_N1, :], chan(lru_bx)),
                             (prow[C_N1:P, :], chan(norm1_g)),
                             (prow2[C_LAM:C_H0, :], chan(lru_lambda)),
                             (prow2[C_H0:C_SC, :], chan(state_lru[0])),
                             (prow2[C_SC:NP2, :], chan(state_conv[0, 0]))):
                sp.dma_start(dst, src).then_inc(par_in, 16)

            def load(tile, slot, src):
                need(sp, lo_ready, 2 * (tile - RING + 1))
                sp.dma_start(ring[slot][:, :, :], src).then_inc(ring_in[slot], 16)

            def lru_loads(i):
                for b in range(2):
                    n = 2 * i + b
                    tile = T_LRU + 2 * n
                    load(tile, 2 * b, w_in_v[:, :, ds(n * P + COL["xb"], P)])
                    load(tile + 1, 2 * b + 1, w_in_v[:, :, ds(n * P + COL["y"], P)])
                    need(sp, gates_ps, n - 1)
                    sp.dma_start(gate_w[:, b, 0, :], wa_v[:, ds(n, 1), :]).then_inc(gw_in[b], 16)
                    sp.dma_start(gate_w[:, b, 1, :], wx_v[:, ds(n, 1), :]).then_inc(gw_in[b], 16)

            peeled(sp, KT // 2, lru_loads)

            def gated_loads(base, gcol, w_v):
                def body(i):
                    for b in range(2):
                        m = 2 * i + b
                        sp.wait_ge(lo_ready, 2 * (base + 2 * m + 2 - RING))
                        sp.dma_start(ring[2 * b][:, :, :], w_in_v[:, :, ds(m * P + gcol, P)])\
                          .then_inc(ring_in[2 * b], 16)
                        sp.dma_start(ring[2 * b + 1][:, :, :], w_v[:, :, ds(m * P, P)])\
                          .then_inc(ring_in[2 * b + 1], 16)
                with sp.Fori(0, KT // 2) as i:
                    body(i)

            gated_loads(T_PB, COL["gb"], w_pb_v)

            def cache_load(head, b):
                need(sp, ov_done, head - 1)
                sp.dma_start(cK[:, b, :, :], ck_v[:, :, ds(head, 1), :]).then_inc(cache_in[b], 16)
                sp.dma_start(cV[:, b, :, :], cv_v[:, :, ds(head, 1), :]).then_inc(cache_in[b], 16)

            def att_loads(i):
                for j in range(4):
                    head = 4 * i + j
                    for c, name in enumerate("qkv"):
                        load(T_ATT + 3 * head + c, (3 * j + c) % RING,
                             w_in_v[:, :, ds(head * P + COL[name], P)])
                        if c == 0 and not (isinstance(head, int) and head == 0):
                            cache_load(head - 1, (j + 1) % 2)

            peeled(sp, H // 4, att_loads)
            cache_load(H - 1, 1)
            gated_loads(T_PA, COL["ga"], w_pa_v)

            with sp.Fori(0, KT // 4) as i:
                for j in range(4):
                    load(T_WO + 4 * i + j, j, w_o_v[:, :, ds((4 * i + j) * P, P)])

            sp.wait_ge(mixsplit_ready, 4)
            for dst, src in ((wr[:, :, 0:4], router_group_w[0].rearrange("(k p) g -> p k g", p=P)),
                             *((wr[:, :, 4 + 4 * g:8 + 4 * g],
                                router_sub_w[0, g].rearrange("(k p) e -> p k e", p=P)) for g in range(NG)),
                             (br[:, 0:4], router_group_b[0:1, :].partition_broadcast(P)),
                             (br[:, 4:20], router_sub_b.rearrange("a g e -> a (g e)").partition_broadcast(P))):
                sp.dma_start(dst, src).then_inc(rw_in, 16)

            def load_piece(g, n):
                j, s = ORDER[n]
                dst, e = raw[n % RAW][:, :], ds(EPG * g + j, 1)
                if s < PU:
                    src = up_v[:, e, 2 * s:2 * s + 2, :]
                    dst = dst.rearrange("p (a k n) -> p a k n", a=1, k=2)
                else:
                    src = dn_v[:, e, s - PU:s - PU + 1, :]
                    dst = dst.rearrange("p (a k n) -> p a k n", a=1, k=1)
                sp.dma_start(dst, src).then_inc(raw_in[n % RAW], 16)

            sp.wait_ge(half_done, 2 * T_WO)
            for b in range(2):
                sp.wait_ge(kv_out[b], 64 * (H // 2))
            for n in range(RAW):
                load_piece(0, n)

            def group_loads(g, c, n0=0):
                for n in range(n0, GP):
                    sp.wait_ge(sL_ready, GH * (g + NG * c) + 2 * (n + 1 - RAW))
                    load_piece(g, n)

            group_loads(0, 0, RAW)
            with sp.Fori(1, NG) as g:
                group_loads(g, 0)

            sp.wait_ge(routed, 1)
            n = sp.value_load(cnt_i[0:1, 0:1], min_val=0, max_val=T)
            with sp.If(n > CAP):
                for c in range(1, CHUNKS):
                    with sp.Fori(0, NG) as g:
                        group_loads(g, c)
                sp.wait_ge(eh_done, CHUNKS * NG * GH)

            sp.wait_ge(eh_done, NG * GH)
            sp.dma_start(gain[:, :], final_norm_g.rearrange("(a n) -> a n", a=1).partition_broadcast(P))\
              .then_inc(gain_in, 16)

            for f in range(FT):
                sp.wait_ge(yo_ready, f + 1)
                dst = yp[:, f, :] if f < 2 else y_sample[0]
                sp.dma_start(dst, xn[0:ROWS[f], f, :]).then_inc(y_out, 16)
            sp.wait_ge(y_out, 16 * FT)

        @block.gpsimd
        def _(pool):
            def const(ins):
                ins.then_inc(consts, 1)
            const(pool.memset(ident[:, :], 0.0))
            const(pool.memset(ident16[:, :], 0.0))
            const(pool.memset(ones[:, :], 1.0))
            const(pool.memset(before[:, :], 1.0))
            const(pool.memset(mask16[:, :], 0.0))
            const(pool.iota(slots_i[:, :], pattern=[[1, T]], base=0, channel_multiplier=0))
            for k in range(4):
                const(pool.memset(first4[:, k:k + 1], 4.0 - k))
            const(pool.memset(eps_t[:, :], EPS))
            const(pool.memset(xpad[:, 0:HIST], 0.0))
            const(pool.memset(rP[:, 128:129], 1.0))
            const(pool.memset(rP[:, 385:386], 1.0))
            const(pool.memset(rS[:, PAST + TS:PAST + TS + 1], 1.0))
            pool.wait_ge(consts, 15)
            for t in (ident, ident16):
                pool.affine_select(out=t[:, :], in_=t[:, :], compare_op=ALU.not_equal, fill=1.0, base=0,
                                   pattern=[[-1, P]], channel_multiplier=1).then_inc(consts2, 1)
            pool.affine_select(out=before[:, :], in_=before[:, :], compare_op=ALU.is_gt, fill=0.0, base=0,
                               pattern=[[1, P]], channel_multiplier=-1).then_inc(consts2, 1)
            pool.affine_select(out=mask16[:, :], in_=mask16[:, :], compare_op=ALU.is_gt, fill=NEG, base=0,
                               pattern=[[-1, P]], channel_multiplier=1).then_inc(consts2, 1)
            pool.tensor_copy(slots[:, :], slots_i[:, :]).then_inc(consts2, 1)

            CONV_STEPS = 7

            def conv(i):
                for b in range(2):
                    n = 2 * i + b
                    st = Steps(pool, conv_s, CONV_STEPS * n)
                    pool.wait_ge(xb_ready, 2 * n + 2)
                    pool.wait_ge(cw_ready, 2 * n + 2)
                    need(pool, uu_ready, n - 1)
                    def col(tap):
                        return cw[:, b, tap:tap + 1].to_broadcast([P, CW])
                    st.link(pool.tensor_tensor(xc[:, b, :], xpad[:, 0:CW], col(0), ALU.mult))
                    st.step(pool.tensor_tensor(ct[:, :], xpad[:, 1:1 + CW], col(1), ALU.mult))
                    st.link(pool.tensor_tensor(xc[:, b, :], xc[:, b, :], col(4), ALU.add))
                    for tap in (2, 3):
                        st.link(pool.tensor_tensor(xc[:, b, :], xc[:, b, :], ct[:, :], ALU.add))
                        st.link(pool.tensor_tensor(ct[:, :], xpad[:, tap:tap + CW], col(tap), ALU.mult))
                    pool.tensor_tensor(xc[:, b, :], xc[:, b, :], ct[:, :], ALU.add).then_inc(xc_ready, 1)
                    assert st.n == CONV_STEPS, st.n

            peeled(pool, KT // 2, conv)

            pool.wait_ge(half_done, 2 * T_WO)
            for b in range(2):
                pool.wait_ge(kv_out[b], 64 * (H // 2))
            pool.dma_start(x1[:, 0:2, :], xp).then_inc(xr_in, 16)
            pool.dma_start(x1[0:TS, 2, :], x_sample[0]).then_inc(xr_in, 16)
            pool.wait_ge(mixsplit_ready, 4)
            pool.dma_start(gain[:, :], norm2_g[0:1, :].partition_broadcast(P)).then_inc(gain2_in, 16)

        @block.scalar
        def _(a):
            def split(tile, slot, fill):
                for half in range(2):
                    if half == 0:
                        a.wait_ge(ring_in[slot], 16 * fill)
                    need(a, half_done, 2 * tile + half + 1 - HALVES)
                    a.activation(wH[2 * (slot % 2) + half][:, :, :], ring[slot][:, 8 * half:8 * half + 8, :],
                                 ACT.Copy).then_inc(hi_ready, 1)

            def ahead(base, size, i, u):
                split(base + size * i + u + 2, (u + 2) % RING, base // RING + size // RING * i + (u + 2) // RING + 1)

            def square_sums(f, dst, src):
                a.activation(dst[0:ROWS[f], f, :], src[0:ROWS[f], f, :], ACT.Square,
                             accum_out=ssq[0:ROWS[f], f:f + 1]).then_inc(ssq_ready, 1)

            def roots(nth, fs=range(FT)):
                for f in fs:
                    a.wait_ge(ssq_ready, FT * (nth - 1) + f + 1)
                    a.activation(rms[0:ROWS[f], f:f + 1], ssq[0:ROWS[f], f:f + 1], ACT.Sqrt,
                                 bias=eps_t[0:ROWS[f], :], scale=1.0 / D).then_inc(rms_ready, 1)

            a.wait_ge(consts, 15)
            for f in range(FT):
                a.wait_ge(x_in[f], 16)
                square_sums(f, xn0, x0)
                roots(1, (f,))
            own = Steps(a, act_s)
            a.wait_ge(par_ps, 1)
            own.step(a.activation(prm[:, :], tr[0][:, 0:P], ACT.Copy))
            a.activation(prm2[:, :], tr[1][:, 0:NP2], ACT.Copy).then_inc(par_ready, 1)
            own.settle()
            a.wait_ge(par_ready, 1)
            own.link(a.activation(lz[:, 0, :], prm2[:, C_LAM:C_LAM + KT], ACT.Abs))
            a.activation(lz[:, 1, :], lz[:, 0, :], ACT.Exp, scale=-1.0).then_inc(par_ready, 1)
            for k in range(KT):
                a.wait_ge(h_ps, k + 1)
                a.activation(hH[:, k, :], bank[4 + k % 4][:, 0:T], ACT.Copy,
                             scale=prm[:, C_N1 + k:C_N1 + k + 1]).then_inc(hH_ready, 1)
                if k == 3:
                    split(0, 0, 1)
                if k == 11:
                    split(1, 1, 1)
            a.wait_ge(negh_ready, 1)

            def lru(i):
                for b in range(2):
                    n = 2 * i + b
                    tile = T_LRU + 2 * n
                    ahead(T_LRU, 4, i, 2 * b)
                    a.wait_ge(half_done, 2 * (tile + 1))
                    need(a, xc_ready, n)
                    need(a, tails_ready, 2 * n)
                    a.activation(xpad[:, HIST:HIST + TP], acc[0][:, 0:TP], ACT.Copy).then_inc(xb_ready, 1)
                    a.activation(xpad[:, XW - TS:XW], acc[0][:, TP:T], ACT.Copy).then_inc(xb_ready, 1)
                    a.wait_ge(xb_ready, 2 * n + 2)
                    a.sem_inc(acc_used[0], 1)
                    prev = not (isinstance(n, int) and n == 0)
                    if prev:
                        gate_values(n - 1)
                    ahead(T_LRU, 4, i, 2 * b + 1)
                    if prev:
                        upper(n - 1)
                    a.wait_ge(half_done, 2 * (tile + 2))
                    a.activation(gy[:, :], acc[1][:, 0:T], ACT.Gelu_apprx_tanh).then_inc(gy_ready, 1)
                    a.wait_ge(gy_ready, n + 1)
                    a.sem_inc(acc_used[1], 1)

            def gate_values(n):
                a.wait_ge(gates_ps, n + 1)
                own = Steps(a, gates_s, 2 * n)
                own.step(a.activation(rg[:, :], gateA[:, 0:CW], ACT.Tanh, bias=hb[:, ds(n, 1)], scale=0.5))
                own.step(a.activation(ig[:, :], gateX[:, 0:CW], ACT.Tanh, bias=hb[:, ds(n + KT, 1)], scale=0.5))
                own.settle()
                a.activation(th[:, :], rg[:, :], ACT.Tanh, bias=negh[:, ds(n, 1)],
                             scale=negh[:, ds(n, 1)]).then_inc(th_ready, 1)
                a.wait_ge(th_ready, 2 * n + 1)
                a.activation(sq[:, :], th[:, :], ACT.Sqrt).then_inc(th_ready, 1)

            def upper(n):
                a.wait_ge(go_ready, n + 1)
                a.activation(oH[:, ds(n, 1), :], ob[:, :], ACT.Copy).then_inc(oH_s, 1)

            peeled(a, KT // 2, lru)
            gate_values(KT - 1)
            upper(KT - 1)

            def gates(base, m0):
                def body(i):
                    for b in range(2):
                        m = 2 * i + b
                        ahead(base, 4, i, 2 * b)
                        a.wait_ge(half_done, 2 * (base + 2 * m + 1))
                        need(a, mix_ready, m + m0)
                        a.activation(sg[:, :], acc[0][:, 0:T], ACT.Sigmoid).then_inc(sg_ready, 1)
                        a.wait_ge(sg_ready, m + m0 + 1)
                        a.sem_inc(acc_used[0], 1)
                        ahead(base, 4, i, 2 * b + 1)
                peeled(a, KT // 2, body)

            gates(T_PB, 0)
            a.wait_ge(states_ps, 1)
            a.activation(statesT[:, :], tr[0][:, 0:P], ACT.Copy).then_inc(states_ready, 1)
            a.wait_ge(states_ready, 1)
            for dst, lo, hi in ((prompt_conv[0, 0], 0, 48), (sample_conv[0, 0], 48, 96),
                                (prompt_lru[0], 96, 112), (sample_lru[0], 112, 128)):
                a.dma_start(chan(dst), statesT[lo:hi, :]).then_inc(st_out, 16)

            def take(head, i, j, c, dst):
                tile = T_ATT + 3 * head + c
                ahead(T_ATT, 12, i, 3 * j + c)
                a.wait_ge(half_done, 2 * (tile + 1))
                a.activation(dst[:, j % 2, :], acc[(3 * j + c) % 2][:, 0:T], ACT.Copy).then_inc(qkv_ready, 1)
                a.wait_ge(qkv_ready, 3 * head + c + 1)
                a.sem_inc(acc_used[(3 * j + c) % 2], 1)

            def store(src, b, head, prompt, sample):
                a.dma_start(prompt[:, :, ds(head, 1), :], src[:, b, 0:2, :]).then_inc(kv_out[b], 16)
                a.dma_start(sample[0, 0, :, ds(head, 1), :], src[0:TS, b, 2, :]).then_inc(kv_out[b], 16)

            def att1(head, b, nth):
                need(a, kv_out[b], 64 * nth)
                a.wait_ge(ktok_ps, head + 1)
                a.activation(kTok[:, b, 0:2, :], tr[1][:, 0:256].rearrange("p (f d) -> p f d", f=2),
                             ACT.Copy).then_inc(kTok_ready, 1)
                a.activation(kTok[0:TS, b, 2, :], tr[1][0:TS, 256:384], ACT.Copy).then_inc(kTok_ready, 1)
                a.wait_ge(zP_ready, head + 1)
                need(a, wP_ready, head)
                a.activation(sgP[:, :], zP[:, 0:384], ACT.Sigmoid, scale=SCALE).then_inc(sigP_ready, 1)
                a.activation(kpP[:, :], zP[:, 0:384], ACT.Sigmoid, scale=-SCALE).then_inc(sigP_ready, 1)
                a.wait_ge(kTok_ready, 2 * head + 2)
                store(kTok, b, head, pk_v, sample_k)
                a.wait_ge(zS_ready, head + 1)
                need(a, wS_ready, head)
                for dst, s in ((sgS, SCALE), (kpS, -SCALE)):
                    a.activation(dst[:, 0:PAST], zS[0:TS, :], ACT.Sigmoid, scale=s).then_inc(sigS_ready, 1)
                    a.activation(dst[:, PAST:], zN[0:TS, 0:TS], ACT.Sigmoid, scale=s).then_inc(sigS_ready, 1)
                a.wait_ge(vtok_ps, head + 1)
                a.activation(vTok[:, b, 0:2, :], tr[0][:, 0:256].rearrange("p (f d) -> p f d", f=2),
                             ACT.Copy).then_inc(vTok_ready, 1)
                a.activation(vTok[0:TS, b, 2, :], tr[0][0:TS, 256:384], ACT.Copy).then_inc(vTok_ready, 1)
                a.wait_ge(vTok_ready, 2 * head + 2)
                store(vTok, b, head, pv_v, sample_v)

            def att2(head):
                a.wait_ge(pt_ps, head + 1)
                a.activation(pT[:, :], tr[1][:, 0:384], ACT.Copy).then_inc(pT_ready, 1)

            def att3(head):
                a.wait_ge(ov_done, head + 1)
                a.activation(oH[:, ds(head, 1), :], ov[:, 0:T], ACT.Copy).then_inc(oaH_ready, 1)

            def att(i):
                for j in range(4):
                    head = 4 * i + j
                    prev = not (isinstance(head, int) and head == 0)
                    b, nth = (j + 1) % 2, (2 * i + (j - 1) // 2)
                    take(head, i, j, 0, qT)
                    if prev:
                        att1(head - 1, b, nth)
                    take(head, i, j, 1, kT)
                    if prev:
                        att2(head - 1)
                    take(head, i, j, 2, vT)
                    if prev:
                        att3(head - 1)

            peeled(a, H // 4, att)
            att1(H - 1, 1, H // 2 - 1)
            att2(H - 1)
            att3(H - 1)
            gates(T_PA, KT)

            for q in range(4):
                a.wait_ge(mix_ready, KT + 4 * (q + 1))
                a.activation(hH[:, 4 * q:4 * q + 4, :], mixed[:, 4 * q:4 * q + 4, :], ACT.Copy)\
                 .then_inc(mixsplit_s, 1)

            def wo(i, last=False):
                for j in range(4):
                    m = 4 * i + j
                    if not (last and j >= 2):
                        ahead(T_WO, 4, i, j)
                    a.wait_ge(half_done, 2 * (T_WO + m + 1))
                    a.activation(yT[:, j % 2, :], acc[j % 2][:, 0:T], ACT.Copy).then_inc(yT_ready, 1)
                    a.wait_ge(yT_ready, m + 1)
                    a.sem_inc(acc_used[j % 2], 1)
            with a.Fori(0, KT // 4 - 1) as i:
                wo(i)
            wo(KT // 4 - 1, last=True)

            a.wait_ge(x1_ready, KT)
            for f in range(FT):
                square_sums(f, xn, x1)
                roots(2, (f,))
            for k in range(KT):
                if k % 4 == 0 and k // 4 < FT:
                    f = k // 4
                    a.wait_ge(xn_ready, FT + f + 1)
                    a.activation(xnH[0:ROWS[f], f, :], xn[0:ROWS[f], f, :], ACT.Copy).then_inc(xnH_ready, 1)
                a.wait_ge(hT_ps, k + 1)
                a.activation(hT[:, k, :], bank[4 + k % 4][:, 0:T], ACT.Copy).then_inc(hT_ready, 1)

            a.wait_ge(lgT_ps, 1)
            a.activation(lgT[:, :], bank[3][0:20, 0:T], ACT.Copy).then_inc(lgT_ready, 1)
            a.wait_ge(lg_ready, 1)
            a.activation(r4[:, 1, :, :], r4[:, 0, :, :], ACT.Exp).then_inc(ge_ready, 1)
            a.wait_ge(dd_ready, 1)
            a.activation(r1[:, 1, :, :], r1[:, 0, :, :], ACT.Exp).then_inc(ed_ready, 1)

            def split(gp, t):
                if t % 2 == 0:
                    a.wait_ge(raw_in[t // 2 % RAW], 16 * (GH // 2 // RAW * gp + t // 2 // RAW + 1))
                if t >= HALVES:
                    a.wait_ge(eh_done, GH * gp + t + 1 - HALVES)
                a.activation(sH[t % HALVES][:, :], raw[t // 2 % RAW][:, 1024 * (t % 2):1024 * (t % 2 + 1)],
                             ACT.Copy).then_inc(sH_ready, 1)

            def group(gp):
                for nb in range(4):
                    a.wait_ge(tok_ps, 4 * gp + nb + 1)
                    a.activation(tok[:, nb * 512:(nb + 1) * 512], bank[4 + nb][0:CAP, :], ACT.Copy)\
                     .then_inc(tok_ready, 1)
                for t in range(HALVES):
                    split(gp, t)
                a.wait_ge(gt_ps, gp + 1)
                a.activation(GT[:, :], bank[4][0:CAP, 0:T], ACT.Copy).then_inc(GT_ready, 1)
                for q in range(4):
                    a.wait_ge(hg_ps, 4 * gp + q + 1)
                    a.activation(hgH[:, 4 * q:4 * q + 4, :],
                                 bank[HG_BANK[q]][:, 0:4 * CAP].rearrange("p (k c) -> p k c", k=4),
                                 ACT.Copy).then_inc(hgH_ready, 1)
                for t in range(HALVES, GH):
                    for j in range(EPG):
                        if t == TURNED[j] + HALVES - 1 + (j == EPG - 1):
                            a.wait_ge(at_ps, EPG * gp + j + 1)
                            a.activation(atH[:, :, :],
                                         pair[j % 2][0][:, 0:FM * CAP].rearrange("p (m c) -> p m c", m=FM),
                                         ACT.Copy).then_inc(atH_ready, 1)
                        if t == GATED[j] + HALVES - 1:
                            a.wait_ge(eh_done, GH * gp + GATED[j])
                            a.activation(silu[:, :], pair[j % 2][0][0:CAP, :], ACT.Silu).then_inc(silu_ready, 1)
                    split(gp, t)
                a.wait_ge(eh_done, GH * (gp + 1))
                for nb in range(4):
                    a.activation(ogH[:, nb * 512:(nb + 1) * 512], out4[nb][0:CAP, :], ACT.Copy)\
                     .then_inc(ogH_ready, 1)

            a.wait_ge(xn_ready, 2 * FT)
            a.wait_ge(lg_ps, 1)
            a.wait_ge(routed, 1)
            peeled(a, NG, group)
            n = a.value_load(cnt_i[0:1, 0:1], min_val=0, max_val=T)
            with a.If(n > CAP):
                with a.Fori(NG, NG * CHUNKS) as gp:
                    group(gp)

            for f in range(FT):
                a.wait_ge(x1_final, f + 1)
                square_sums(f, xn, x1)
                roots(3, (f,))
            a.wait_ge(st_out, 64)
            for b in range(2):
                a.wait_ge(kv_out[b], 64 * (H // 2))

        @block.tensor
        def _(pe):
            pe.wait_ge(consts2, 5)
            pe.wait_ge(par_in, 16 * 8)
            pe.transpose(tr[0][:, 0:P], prow[:, :], ident[:, :])
            pe.transpose(tr[1][:, 0:NP2], prow2[:, :], ident[0:NP2, 0:NP2]).then_inc(par_ps, 1)

            def turn(dst, src, f0=0):
                for f in range(FT):
                    ins = pe.transpose(dst[:, f * P:f * P + ROWS[f]], src(f), ident[0:ROWS[f], 0:ROWS[f]])
                return ins

            pe.wait_ge(xn_ready, FT)
            for k in range(KT):
                need(pe, h_ready, k - 3)
                turn(bank[4 + k % 4], lambda f: xn0[0:ROWS[f], f, k * P:(k + 1) * P]).then_inc(h_ps, 1)

            def tile_product(tile, u, used, rH, rL, parts=False, first=False):
                need(pe, acc_used[u % 2], used)
                dst = acc[u % 2][:, 0:T]
                for k in range(KT):
                    half, kk = k // 8, k % 8
                    if kk == 0:
                        pe.wait_ge(lo_ready, 2 * tile + half + 1)
                    if first:
                        pe.wait_ge(h_ready, k + 1)
                    if parts and k % 4 == 0:
                        pe.wait_ge(mixsplit_ready, k // 4 + 1)
                    hi, lo = wH[2 * (u % 2) + half][:, kk, :], wL[2 * (u % 2) + half][:, kk, :]
                    pe.matmul(dst, hi, rH[:, k, :], start=(k == 0), stop=False)
                    pe.matmul(dst, hi, rL[:, k, :], start=False, stop=False)
                    ins = pe.matmul(dst, lo, rH[:, k, :], start=False, stop=(k == KT - 1))
                    if kk == 7:
                        ins.then_inc(half_done, 1)

            def lru(i):
                for b in range(2):
                    n = 2 * i + b
                    for c in range(2):
                        tile_product(T_LRU + 4 * i + 2 * b + c, 2 * b + c, T_LRU // 2 + 2 * i + b, hH, hL,
                                     first=isinstance(n, int) and n == 0 and c == 0)
                        if c == 0 and not (isinstance(n, int) and n == 0):
                            gate_products(n - 1, 1 - b, i + b)

            def gate_products(n, b, fills):
                pe.wait_ge(xc_ready, n + 1)
                pe.wait_ge(gw_in[b], 32 * fills)
                need(pe, th_ready, 2 * n)
                pe.matmul(gateA[:, 0:CW], gate_w[:, b, 0, :], xc[:, b, :], start=True, stop=True)
                pe.matmul(gateX[:, 0:CW], gate_w[:, b, 1, :], xc[:, b, :], start=True, stop=True)\
                  .then_inc(gates_ps, 1)

            peeled(pe, KT // 2, lru)
            gate_products(KT - 1, 1, KT // 2)

            def gated(base, ready, count):
                def body(i):
                    for b in range(2):
                        tile_product(base + 4 * i + 2 * b, 2 * b, base // 2 + 2 * i + b, hH, hL)
                        pe.wait_ge(ready, count)
                        tile_product(base + 4 * i + 2 * b + 1, 2 * b + 1, base // 2 + 2 * i + b, oH, oL)
                with pe.Fori(0, KT // 2) as i:
                    body(i)

            gated(T_PB, ob_ready, KT)
            pe.transpose(tr[0][:, 0:P], states[:, :], ident[:, :]).then_inc(states_ps, 1)
            pe.wait_ge(states_ready, 1)

            def att1(head, b, nth):
                pe.wait_ge(cache_in[b], 32 * (nth + 1))
                pe.wait_ge(qkv_ready, 3 * head + 3)
                need(pe, pS_ready, 2 * head)
                for kb in range(PAST // P):
                    ins = pe.transpose(tr[0][:, kb * P:(kb + 1) * P], cK[:, b, kb, :], ident[:, :])
                ins.then_inc(kc_ps, 1)
                need(pe, pT_ready, head)
                for f in range(FT):
                    ins = pe.transpose(tr[1][0:ROWS[f], f * P:(f + 1) * P],
                                       kT[:, b, f * P:f * P + ROWS[f]], ident[:, :])
                ins.then_inc(ktok_ps, 1)
                need(pe, sigP_ready, 2 * head)
                pe.matmul(zP[:, 0:128], qT[:, b, 0:128], kT[:, b, 0:128], start=True, stop=False,
                          skip_group_check=True)
                pe.matmul(zP[:, 0:128], ident16[:, :], mask16[:, :], start=False, stop=True,
                          skip_group_check=True)
                pe.matmul(zP[:, 128:384], qT[:, b, 128:256], kT[:, b, 0:256], start=True, stop=False,
                          skip_group_check=True)
                pe.matmul(zP[:, 256:384], ident16[:, :], mask16[:, :], start=False, stop=True,
                          skip_group_check=True).then_inc(zP_ready, 1)
                need(pe, sigS_ready, 4 * head)
                pe.matmul(zN[0:TS, 0:TS], qT[:, b, TP:T], kT[:, b, TP:T], start=True, stop=False,
                          skip_group_check=True)
                pe.matmul(zN[0:TS, 0:TS], ident16[:, 0:TS], mask16[:, 0:TS], start=False, stop=True,
                          skip_group_check=True)
                pe.wait_ge(kcT_ready, head + 1)
                pe.matmul(zS[0:TS, :], qT[:, b, TP:T], kcT[:, :], start=True, stop=True).then_inc(zS_ready, 1)
                for f in range(FT):
                    ins = pe.transpose(tr[0][0:ROWS[f], f * P:(f + 1) * P],
                                       vT[:, b, f * P:f * P + ROWS[f]], ident[:, :])
                ins.then_inc(vtok_ps, 1)

            def att2(head):
                pe.wait_ge(wP_ready, head + 1)
                pe.wait_ge(kTok_ready, 2 * head + 2)
                for c in range(3):
                    if c == 2:
                        pe.wait_ge(wS_ready, head + 1)
                        pe.wait_ge(vTok_ready, 2 * head + 2)
                    ins = pe.transpose(tr[1][:, c * P:(c + 1) * P], wP[:, c * P:(c + 1) * P], ident[:, :])
                ins.then_inc(pt_ps, 1)
                for kb in range(PAST // P):
                    pe.transpose(tr[0][:, kb * TS:(kb + 1) * TS], wS[:, kb * P:(kb + 1) * P],
                                 ident[0:TS, 0:TS])
                pe.transpose(tr[0][0:TS, 128:160], wS[:, PAST:PAST + TS], ident[0:TS, 0:TS])\
                  .then_inc(ps_ps, 1)

            def att3(head, b):
                pe.wait_ge(pT_ready, head + 1)
                pe.wait_ge(pS_ready, 2 * head + 2)
                need(pe, oa_ready, head)
                pe.matmul(ov[:, 0:256], vTok[:, b, 0, :], pT[:, 0:256], start=True, stop=False,
                          skip_group_check=True)
                pe.matmul(ov[:, 128:256], vTok[:, b, 1, :], pT[:, 256:384], start=False, stop=True,
                          skip_group_check=True)
                for kb in range(PAST // P):
                    pe.matmul(ov[:, TP:T], cV[:, b, kb, :], pS[:, kb * TS:(kb + 1) * TS],
                              start=(kb == 0), stop=False, skip_group_check=True)
                pe.matmul(ov[:, TP:T], vTok[0:TS, b, 2, :], pS[0:TS, 128:160], start=False, stop=True,
                          skip_group_check=True).then_inc(ov_done, 1)

            def att(i):
                for j in range(4):
                    head = 4 * i + j
                    prev = not (isinstance(head, int) and head == 0)
                    b, nth = (j + 1) % 2, (2 * i + (j - 1) // 2)
                    for c in range(3):
                        u = 3 * j + c
                        tile_product(T_ATT + 12 * i + u, u, T_ATT // 2 + 6 * i + u // 2, hH, hL)
                        if prev:
                            (lambda: att1(head - 1, b, nth), lambda: att2(head - 1),
                             lambda: att3(head - 1, b))[c]()

            peeled(pe, H // 4, att)
            att1(H - 1, 1, H // 2 - 1)
            att2(H - 1)
            att3(H - 1, 1)
            gated(T_PA, oa_ready, H)

            def y_turn(m, b):
                pe.wait_ge(yT_ready, m + 1)
                need(pe, x1_ready, m - 1)
                for f in range(FT):
                    ins = pe.transpose(tr[b][0:ROWS[f], f * P:(f + 1) * P],
                                       yT[:, b, f * P:f * P + ROWS[f]], ident[:, :])
                ins.then_inc(y_ps, 1)

            def wo(i):
                for j in range(4):
                    first = isinstance(i, int) and i == 0 and j == 0
                    tile_product(T_WO + 4 * i + j, j, T_WO // 2 + 2 * i + j // 2, hH, hL, parts=first)
                    if not first:
                        y_turn(4 * i + j - 1, (j + 1) % 2)
            peeled(pe, KT // 4, wo)
            y_turn(KT - 1, 1)

            pe.wait_ge(xn_ready, 2 * FT)
            for k in range(KT):
                need(pe, hT_ready, k - 3)
                turn(bank[4 + k % 4], lambda f: xn[0:ROWS[f], f, k * P:(k + 1) * P]).then_inc(hT_ps, 1)
            pe.wait_ge(rw_in, 16 * 7)
            for k in range(KT):
                pe.wait_ge(hT_ready, k + 1)
                ins = pe.matmul(bank[3][0:20, 0:T], wr[:, k, :], hT[:, k, :], start=(k == 0), stop=(k == KT - 1))
            ins.then_inc(lgT_ps, 1)
            pe.wait_ge(lgT_ready, 1)
            for f in range(FT):
                ins = pe.transpose(bank[f][0:ROWS[f], 0:20], lgT[:, f * P:f * P + ROWS[f]], ident[0:20, 0:20])
            ins.then_inc(lg_ps, 1)
            pe.wait_ge(oh_ready, 1)
            oh = r4[:, 3, :, :]
            for f in range(FT):
                for e in range(f + 1):
                    lhs = before if e == f else ones
                    pe.matmul(bank[4 + f][0:ROWS[f], 0:NG], lhs[0:ROWS[e], 0:ROWS[f]], oh[0:ROWS[e], e, :],
                              start=(e == 0), stop=(e == f))
            for e in range(FT):
                ins = pe.matmul(bank[7][:, 0:NG], ones[0:ROWS[e], :], oh[0:ROWS[e], e, :],
                                start=(e == 0), stop=(e == FT - 1))
            ins.then_inc(pos_ps, 1)
            pe.wait_ge(routed, 1)
            pe.wait_ge(xnL_ready, FT)

            def three(dsts, wtH, wtL, hi, lo, start, stop):
                for c in range(2):
                    pe.matmul(dsts[c][0:CAP, :], wtH, hi[:, c * 512:(c + 1) * 512], start=start, stop=False)
                for c in range(2):
                    pe.matmul(dsts[c][0:CAP, :], wtH, lo[:, c * 512:(c + 1) * 512], start=False, stop=False)
                for c in range(2):
                    ins = pe.matmul(dsts[c][0:CAP, :], wtL, hi[:, c * 512:(c + 1) * 512], start=False, stop=stop)
                ins.then_inc(eh_done, 1)

            def scatter(gp, done=sc_ps, out=added, before=0):
                for u in range(4 * FT):
                    f, nb = u // 4, u % 4
                    if f == 0:
                        pe.wait_ge(ogL_ready, 4 * gp + nb + 1)
                    else:
                        pe.wait_ge(out, before + u - 3)
                    for og in (ogH, ogL):
                        ins = pe.matmul(out4[nb][0:ROWS[f], :], GT[:, f * P:f * P + ROWS[f]],
                                        og[:, nb * 512:(nb + 1) * 512], start=(og is ogH), stop=(og is ogL))
                    ins.then_inc(done, 1)

            def group(g, c, first=False):
                gp = g + NG * c
                pe.wait_ge(G_ready, FT * (g + (NG + 1) * c + 1))
                for nb in range(4):
                    for f in range(FT):
                        for x in (xnH, xnL):
                            ins = pe.matmul(bank[4 + nb][0:CAP, :], G[0:ROWS[f], f, :],
                                            x[0:ROWS[f], f, nb * 512:(nb + 1) * 512],
                                            start=(f == 0 and x is xnH), stop=(f == FT - 1 and x is xnL))
                    ins.then_inc(tok_ps, 1)
                if not first:
                    scatter(gp - 1, before=4 * FT * (gp - 1))
                pe.wait_ge(tok_ready, 4 * gp + 4)
                for f in range(FT):
                    ins = pe.transpose(bank[4][0:CAP, f * P:f * P + ROWS[f]], G[0:ROWS[f], f, :].bitcast(F32),
                                       ident[0:ROWS[f], 0:ROWS[f]])
                ins.then_inc(gt_ps, 1)
                for f in range(FT):
                    ins = pe.matmul(bank[5][0:CAP, 0:EPG], G[0:ROWS[f], f, :].bitcast(F32),
                                    comb[0:ROWS[f], f, ds(4 * g, 4)], start=(f == 0), stop=(f == FT - 1))
                ins.then_inc(cs_ps, 1)
                for q in range(4):
                    if q == 2:
                        pe.wait_ge(GT_ready, gp + 1)
                    if q == 3:
                        pe.wait_ge(cs_ready, gp + 1)
                    for kk in range(4):
                        k = 4 * q + kk
                        ins = pe.transpose(bank[HG_BANK[q]][:, kk * CAP:(kk + 1) * CAP],
                                           tok[:, k * P:(k + 1) * P], ident[0:CAP, 0:CAP])
                    ins.then_inc(hg_ps, 1)
                for t in range(GH):
                    (j, s), half = ORDER[t // 2], t % 2
                    if t in TURNED:
                        i = TURNED.index(t)
                        pe.wait_ge(act_ready, EPG * gp + i + 1)
                        for m in range(FM):
                            ins = pe.transpose(pair[i % 2][0][:, m * CAP:(m + 1) * CAP],
                                               act[:, m * P:(m + 1) * P], ident[0:CAP, 0:CAP])
                        ins.then_inc(at_ps, 1)
                    if j == 0 and s in (0, 4, 6) and half == 0:
                        pe.wait_ge(hgL_ready, 4 * gp + {0: 2, 4: 3, 6: 4}[s])
                    if s == PU and half == 0:
                        pe.wait_ge(atL_ready, EPG * gp + j + 1)
                        if j == 0 and not first:
                            pe.wait_ge(added, 4 * FT * gp)
                    pe.wait_ge(sL_ready, GH * gp + t + 1)
                    if s < PU:
                        k = 2 * s + half
                        three(pair[j % 2], hgH[:, k, :], hgL[:, k, :], sH[t % HALVES], sL[t % HALVES],
                              k == 0, k == KT - 1)
                    else:
                        m = s - PU
                        three(out4[2 * half:2 * half + 2], atH[:, m, :], atL[:, m, :], sH[t % HALVES],
                              sL[t % HALVES], j == 0 and m == 0, j == EPG - 1 and m == FM - 1)

            n = pe.value_load(cnt_i[0:1, 0:1], min_val=0, max_val=T)
            def groups(c):
                group(0, c, first=(c == 0))
                with pe.Fori(1, NG) as g:
                    group(g, c)

            groups(0)
            with pe.If(n > CAP):
                for c in range(1, CHUNKS):
                    groups(c)
                pe.wait_ge(ogL_ready, 4 * NG * CHUNKS)
            scatter(NG - 1, last_ps, last_added)

        @block.vector
        def _(v):
            own = Steps(v, dve_s)

            def split(tile, slot):
                for half in range(2):
                    hi, lo = wH[2 * (slot % 2) + half], wL[2 * (slot % 2) + half]
                    v.wait_ge(hi_ready, 2 * tile + half + 1)
                    v.tensor_tensor(lo[:, :, :], ring[slot][:, 8 * half:8 * half + 8, :],
                                    hi[:, :, :].bitcast(F32), ALU.subtract).then_inc(lo_ready, 1)

            def ahead(base, size, i, u):
                split(base + size * i + u + 2, (u + 2) % RING)

            def norm(nth, dst_sem, row, xn, x1, fs=range(FT)):
                for f in fs:
                    v.wait_ge(rms_ready, FT * (nth - 1) + f + 1)
                    own.link(v.reciprocal(rstd[0:ROWS[f], f:f + 1], rms[0:ROWS[f], f:f + 1]))
                    R = ROWS[f]
                    if row:
                        ins = v.scalar_tensor_tensor(xn[0:R, f, :], x1[0:R, f, :], rstd[0:R, f:f + 1],
                                                     gain[0:R, :], ALU.mult, ALU.mult)
                    else:
                        ins = v.tensor_scalar(xn[0:R, f, :], x1[0:R, f, :], rstd[0:R, f:f + 1], None, ALU.mult)
                    ins.then_inc(dst_sem, 1)

            norm(1, xn_ready, False, xn0, x0)

            v.wait_ge(par_ready, 2)
            own.step(v.tensor_scalar(hb[:, :], prm[:, C_BA:C_N1], 0.5, None, ALU.mult))
            z, s, s2, p = (lz[:, 1, :], lz[:, 2, :], lz[:, 3, :], lz[:, 4, :])
            own.link(v.tensor_scalar(s, z, 2.0, None, ALU.add))
            own.link(v.reciprocal(s, s))
            own.link(v.tensor_tensor(s, s, z, ALU.mult))
            own.link(v.tensor_tensor(s2, s, s, ALU.mult))
            own.link(v.tensor_scalar(p, s2, 1.0 / 17.0, None, ALU.mult))
            for k in (15, 13, 11, 9, 7, 5, 3):
                own.link(v.scalar_tensor_tensor(p, p, 1.0 / k, s2, ALU.add, ALU.mult))
            own.link(v.scalar_tensor_tensor(p, p, 1.0, s, ALU.add, ALU.mult))
            own.link(v.tensor_scalar(s, prm2[:, C_LAM:C_LAM + KT], -1.0, 0.0, ALU.mult, ALU.max))
            own.link(v.tensor_scalar(p, p, 4.0, None, ALU.mult))
            v.scalar_tensor_tensor(negh[:, :], s, 2.0, p, ALU.mult, ALU.add).then_inc(negh_ready, 1)
            for k in range(KT):
                v.wait_ge(hH_ready, k + 1)
                v.scalar_tensor_tensor(hL[:, k, :], bank[4 + k % 4][:, 0:T], prm[:, C_N1 + k:C_N1 + k + 1],
                                       hH[:, k, :].bitcast(F32), ALU.mult, ALU.subtract).then_inc(h_ready, 1)
                if k == 3:
                    split(0, 0)
                if k == 11:
                    split(1, 1)

            LRU_STEPS = 12

            def lru(i):
                for b in range(2):
                    n = 2 * i + b
                    need(v, xc_ready, n)
                    v.tensor_copy(cw[:, b, :], taps3[:, :, ds(n, 1)]).then_inc(cw_ready, 1)
                    v.tensor_copy(xpad[:, HIST + TP:HIST + TP + HIST], hist3[:, :, ds(n, 1)]).then_inc(cw_ready, 1)
                    ahead(T_LRU, 4, i, 2 * b)
                    v.wait_ge(xb_ready, 2 * n + 2)
                    v.tensor_copy(states3[:, 0:3, ds(n, 1)], xpad[:, TP:TP + HIST]).then_inc(tails_ready, 1)
                    v.tensor_copy(states3[:, 3:6, ds(n, 1)], xpad[:, XW - HIST:XW]).then_inc(tails_ready, 1)
                    prev = not (isinstance(n, int) and n == 0)
                    if prev:
                        recurrence(n - 1, 1 - b)
                    ahead(T_LRU, 4, i, 2 * b + 1)
                    if prev:
                        lower(n - 1)

            def recurrence(n, b):
                st = Steps(v, lru_s, LRU_STEPS * n)
                v.wait_ge(th_ready, 2 * n + 1)
                v.wait_ge(xc_ready, n + 1)
                st.link(v.tensor_scalar(t1[:, :], th[:, :], 1.0, None, ALU.add))
                st.step(v.reciprocal(rc[:, :], t1[:, :]))
                v.wait_ge(th_ready, 2 * n + 2)
                v.scalar_tensor_tensor(uu[:, :], ig[:, :], 1.0, xc[:, b, :], ALU.add, ALU.mult)\
                 .then_inc(uu_ready, 1)
                v.wait_ge(uu_ready, n + 1)
                st.step(v.tensor_scalar(aa[:, :], rc[:, :], 2.0, -1.0, ALU.mult, ALU.add))
                st.link(v.tensor_tensor(uu[:, :], uu[:, :], sq[:, :], ALU.mult))
                st.link(v.tensor_tensor(uu[:, :], uu[:, :], rc[:, :], ALU.mult))
                st.step(v.memset(aa[:, S0 - 1:S0], 0.0))
                st.link(v.tensor_copy(uu[:, S0 - 1:S0], prm2[:, ds(n + C_H0, 1)]))
                st.link(v.tensor_tensor_scan(hs[:, :], aa[:, :], uu[:, :], 0.0, ALU.mult, ALU.add))
                st.step(v.tensor_copy(states3[:, 6:7, ds(n, 1)], hs[:, TP - 1:TP]))
                st.step(v.tensor_copy(states3[:, 7:8, ds(n, 1)], hs[:, CW - 1:CW]))
                v.wait_ge(gy_ready, n + 1)
                st.step(v.tensor_tensor(ob[:, 0:TP], gy[:, 0:TP], hs[:, 0:TP], ALU.mult))
                st.link(v.tensor_tensor(ob[:, TP:T], gy[:, TP:T], hs[:, S0:CW], ALU.mult))
                v.sem_inc(go_ready, 1)
                assert st.n == LRU_STEPS, st.n

            def lower(n):
                v.wait_ge(oH_s, n + 1)
                v.tensor_tensor(oL[:, ds(n, 1), :], ob[:, :], oH[:, ds(n, 1), :].bitcast(F32), ALU.subtract)\
                 .then_inc(ob_ready, 1)

            peeled(v, KT // 2, lru)
            recurrence(KT - 1, 1)
            lower(KT - 1)

            def gated(base, m0, add):
                def body(i):
                    for b in range(2):
                        m = 2 * i + b
                        ahead(base, 4, i, 2 * b)
                        v.wait_ge(half_done, 2 * (base + 2 * m + 2))
                        v.wait_ge(sg_ready, m + m0 + 1)
                        if not add:
                            v.tensor_tensor(mixed[:, ds(m, 1), :], acc[1][:, 0:T], sg[:, :], ALU.mult)\
                             .then_inc(acc_used[1], 1)
                        else:
                            v.tensor_tensor(mx[:, :], acc[1][:, 0:T], sg[:, :], ALU.mult)\
                             .then_inc(acc_used[1], 1)
                        v.wait_ge(acc_used[1], base // 2 + m + 1)
                        if not add:
                            v.sem_inc(mix_ready, 1)
                        else:
                            v.tensor_tensor(mixed[:, ds(m, 1), :], mixed[:, ds(m, 1), :], mx[:, :], ALU.add)\
                             .then_inc(mix_ready, 1)
                        ahead(base, 4, i, 2 * b + 1)
                with v.Fori(0, KT // 2) as i:
                    body(i)

            gated(T_PB, 0, False)

            def att1(head):
                v.wait_ge(kc_ps, head + 1)
                need(v, zS_ready, head)
                v.tensor_copy(kcT[:, :], tr[0][:, :]).then_inc(kcT_ready, 1)
                v.wait_ge(sigP_ready, 2 * head + 2)
                v.tensor_tensor_scan(rP[:, 0:128][:, ::-1], kpP[:, 0:128][:, ::-1], kpP[:, 0:128][:, ::-1],
                                     1.0, ALU.mult, ALU.bypass).then_inc(scan_s, 1)
                v.tensor_tensor_scan(rP[:, 129:385][:, ::-1], kpP[:, 128:384][:, ::-1],
                                     kpP[:, 128:384][:, ::-1], 1.0, ALU.mult, ALU.bypass).then_inc(scan_s, 1)
                v.wait_ge(scan_s, 3 * head + 2)
                need(v, pt_ps, head)
                v.tensor_tensor(wP[:, 0:128], sgP[:, 0:128], rP[:, 1:129], ALU.mult).then_inc(mix_s, 1)
                v.tensor_tensor(wP[:, 128:384], sgP[:, 128:384], rP[:, 130:386], ALU.mult).then_inc(mix_s, 1)
                v.wait_ge(mix_s, 2 * head + 2)
                v.sem_inc(wP_ready, 1)
                v.wait_ge(sigS_ready, 4 * head + 4)
                n = PAST + TS
                v.tensor_tensor_scan(rS[:, 0:n][:, ::-1], kpS[:, :][:, ::-1], kpS[:, :][:, ::-1],
                                     1.0, ALU.mult, ALU.bypass).then_inc(scan_s, 1)
                v.wait_ge(scan_s, 3 * head + 3)
                need(v, ps_ps, head)
                v.tensor_tensor(wS[:, :], sgS[:, :], rS[:, 1:n + 1], ALU.mult).then_inc(wS_ready, 1)

            def att2(head):
                v.wait_ge(ps_ps, head + 1)
                need(v, ov_done, head)
                v.tensor_copy(pS[:, 0:128], tr[0][:, 0:128]).then_inc(pS_ready, 1)
                v.tensor_copy(pS[0:TS, 128:160], tr[0][0:TS, 128:160]).then_inc(pS_ready, 1)

            def att3(head):
                v.wait_ge(oaH_ready, head + 1)
                v.tensor_tensor(oL[:, ds(head, 1), :], ov[:, 0:T], oH[:, ds(head, 1), :].bitcast(F32),
                                ALU.subtract).then_inc(oa_ready, 1)

            def att(i):
                for j in range(4):
                    head = 4 * i + j
                    for c, step in enumerate((att1, att2, att3)):
                        ahead(T_ATT, 12, i, 3 * j + c)
                        if not (isinstance(head, int) and head == 0):
                            step(head - 1)

            v.wait_ge(consts, 15)
            peeled(v, H // 4, att)
            att1(H - 1)
            att2(H - 1)
            att3(H - 1)

            gated(T_PA, KT, True)

            for q in range(4):
                v.wait_ge(mixsplit_s, q + 1)
                c = slice(4 * q, 4 * q + 4)
                v.tensor_tensor(hL[:, c, :], mixed[:, c, :], hH[:, c, :].bitcast(F32), ALU.subtract)\
                 .then_inc(mixsplit_ready, 1)

            v.wait_ge(xr_in, 32)

            def residual(i, last=False):
                for j in range(4):
                    m = 4 * i + j - 1
                    if not (last and j >= 2):
                        ahead(T_WO, 4, i, j)
                    if not (isinstance(m, int) and m < 0):
                        add_tile(m, (j + 1) % 2)

            def add_tile(m, j):
                v.wait_ge(y_ps, m + 1)
                c = ds(m * P, P)
                v.tensor_tensor(x1[:, 0:2, c], tr[j][:, 0:256].rearrange("p (f d) -> p f d", f=2),
                                x1[:, 0:2, c], ALU.add).then_inc(mix_s, 1)
                v.tensor_tensor(x1[0:TS, 2, c], tr[j][0:TS, 256:384], x1[0:TS, 2, c], ALU.add)\
                 .then_inc(mix_s, 1)
                v.wait_ge(mix_s, 2 * H + 2 * m + 2)
                v.sem_inc(x1_ready, 1)

            residual(0)
            with v.Fori(1, KT // 4 - 1) as i:
                residual(i)
            residual(KT // 4 - 1, last=True)
            add_tile(KT - 1, 1)

            v.wait_ge(gain2_in, 16)
            norm(2, xn_ready, True, xn, x1)
            v.wait_ge(hT_ps, KT)
            for f in range(FT):
                v.wait_ge(xnH_ready, f + 1)
                v.tensor_tensor(xnL[0:ROWS[f], f, :], xn[0:ROWS[f], f, :], xnH[0:ROWS[f], f, :].bitcast(F32),
                                ALU.subtract).then_inc(xnL_ready, 1)

            for t, c in ((lg, 0.0), (pos, 0.0)):
                own.step(v.memset(t[:, :, :], c))
            own.settle()
            v.wait_ge(rw_in, 16 * 7)
            v.wait_ge(lg_ps, 1)
            for f in range(FT):
                own.step(v.tensor_tensor(lg[0:ROWS[f], f, :], bank[f][0:ROWS[f], 0:20], br[0:ROWS[f], :], ALU.add))
            own.settle()

            def bc(t, n=4):
                return t.to_broadcast([P, FT, n])

            f4 = first4[:, :].rearrange("p (a c) -> p a c", a=1).to_broadcast([P, FT, 4])

            def first_max(x, top, one, tmp):
                own.link(v.tensor_reduce(top, x, AX.X, ALU.max))
                own.link(v.tensor_tensor(tmp, x, bc(top), ALU.is_equal))
                own.link(v.tensor_tensor(tmp, tmp, f4, ALU.mult))
                own.link(v.tensor_reduce(r1[:, 5, :, :], tmp, AX.X, ALU.max))
                own.link(v.tensor_tensor(one, tmp, bc(r1[:, 5, :, :]), ALU.is_equal))

            oh = r4[:, 3, :, :]
            first_max(lg[:, :, 0:4], m1[:, :, :], oh, r4[:, 2, :, :])
            own.link(v.tensor_tensor(r4[:, 0, :, :], lg[:, :, 0:4], bc(m1[:, :, :]), ALU.subtract))
            v.sem_inc(lg_ready, 1)
            v.sem_inc(oh_ready, 1)
            own.link(v.tensor_tensor(psel[:, :, :, :], lg[:, :, 4:20].rearrange("p f (g e) -> p f g e", g=4),
                                     oh.rearrange("p f (g a) -> p f g a", a=1).to_broadcast([P, FT, 4, 4]),
                                     ALU.mult))
            sel, one1, one2, cut = r4[:, 4, :, :], r4[:, 5, :, :], r4[:, 6, :, :], r4[:, 7, :, :]
            own.link(v.tensor_reduce(sel, psel[:, :, :, :].rearrange("p f g e -> p f e g"), AX.X, ALU.add))
            first_max(sel, r1[:, 2, :, :], one1, r4[:, 2, :, :])
            own.link(v.scalar_tensor_tensor(cut, one1, NEG, sel, ALU.mult, ALU.add))
            first_max(cut, r1[:, 3, :, :], one2, r4[:, 2, :, :])
            own.link(v.tensor_tensor(r1[:, 0, :, :], r1[:, 3, :, :], r1[:, 2, :, :], ALU.subtract))
            v.sem_inc(dd_ready, 1)
            v.wait_ge(ge_ready, 1)
            own.link(v.tensor_reduce(pg[:, :, :], r4[:, 1, :, :], AX.X, ALU.add))
            own.link(v.reciprocal(pg[:, :, :], pg[:, :, :]))
            v.wait_ge(ed_ready, 1)
            own.link(v.tensor_scalar(r1[:, 2, :, :], r1[:, 1, :, :], 1.0, None, ALU.add))
            own.link(v.reciprocal(r1[:, 2, :, :], r1[:, 2, :, :]))
            own.link(v.tensor_tensor(r1[:, 2, :, :], r1[:, 2, :, :], pg[:, :, :], ALU.mult))
            own.link(v.tensor_tensor(r1[:, 3, :, :], r1[:, 2, :, :], r1[:, 1, :, :], ALU.mult))
            own.link(v.tensor_tensor(one1, one1, bc(r1[:, 2, :, :]), ALU.mult))
            own.link(v.tensor_tensor(one2, one2, bc(r1[:, 3, :, :]), ALU.mult))
            own.link(v.tensor_tensor(one1, one1, one2, ALU.add))
            own.link(v.tensor_tensor(comb[:, :, :].rearrange("p f (g e) -> p f g e", g=4),
                                     oh.rearrange("p f (g a) -> p f g a", a=1).to_broadcast([P, FT, 4, 4]),
                                     one1.rearrange("p f (a e) -> p f a e", a=1).to_broadcast([P, FT, 4, 4]),
                                     ALU.mult))
            v.wait_ge(pos_ps, 1)
            for f in range(FT):
                own.step(v.tensor_copy(pos[0:ROWS[f], f, 0:NG], bank[4 + f][0:ROWS[f], 0:NG]))
            own.link(v.tensor_scalar(r4[:, 8, :, :], oh, -1.0e6, 1.0e6, ALU.mult, ALU.add))
            own.link(v.tensor_tensor(pos[:, :, 0:NG], pos[:, :, 0:NG], r4[:, 8, :, :], ALU.add))
            own.link(v.tensor_reduce(cmax[:, :], bank[7][:, 0:NG], AX.X, ALU.max))
            v.tensor_copy(cnt_i[:, :], cmax[:, :]).then_inc(routed, 1)

            def split(gp, t):
                v.wait_ge(sH_ready, GH * gp + t + 1)
                v.tensor_tensor(sL[t % HALVES][:, :], raw[t // 2 % RAW][:, 1024 * (t % 2):1024 * (t % 2 + 1)],
                                sH[t % HALVES][:, :].bitcast(F32), ALU.subtract).then_inc(sL_ready, 1)

            def assign(g, c):
                for f in range(FT):
                    v.tensor_scalar(G[:, f, :], slots[:, c * CAP:(c + 1) * CAP], pos[:, f, ds(g, 1)], None,
                                    ALU.is_equal).then_inc(G_ready, 1)

            def add_part(u, done, count, out):
                f, nb = u // 4, u % 4
                c = slice(nb * 512, (nb + 1) * 512)
                v.wait_ge(done, count)
                v.tensor_tensor(x1[0:ROWS[f], f, c], out4[nb][0:ROWS[f], :], x1[0:ROWS[f], f, c], ALU.add)\
                 .then_inc(out, 1)

            def add(gp):
                for u in range(4 * FT):
                    add_part(u, sc_ps, 4 * FT * gp + u + 1, added)

            def group(g, c, first=False):
                gp = g + NG * c
                if not first:
                    add(gp - 1)
                for t in range(HALVES):
                    split(gp, t)
                v.wait_ge(cs_ps, gp + 1)
                v.tensor_copy(cs[:, :], bank[5][0:CAP, 0:EPG]).then_inc(cs_ready, 1)
                for q in range(4):
                    v.wait_ge(hgH_ready, 4 * gp + q + 1)
                    k = slice(4 * q, 4 * q + 4)
                    v.tensor_tensor(hgL[:, k, :],
                                    bank[HG_BANK[q]][:, 0:4 * CAP].rearrange("p (k c) -> p k c", k=4),
                                    hgH[:, k, :].bitcast(F32), ALU.subtract).then_inc(hgL_ready, 1)
                v.wait_ge(cs_ready, gp + 1)
                assign(g + 1, c)
                for t in range(HALVES, GH):
                    for j in range(EPG):
                        if t == TURNED[j] + HALVES - 1 + (j == EPG - 1):
                            v.wait_ge(atH_ready, EPG * gp + j + 1)
                            v.tensor_tensor(atL[:, :, :],
                                            pair[j % 2][0][:, 0:FM * CAP].rearrange("p (m c) -> p m c", m=FM),
                                            atH[:, :, :].bitcast(F32), ALU.subtract).then_inc(atL_ready, 1)
                        if t == GATED[j] + HALVES - 1:
                            v.wait_ge(silu_ready, EPG * gp + j + 1)
                            v.scalar_tensor_tensor(act[:, :], silu[:, :], cs[:, j:j + 1],
                                                   pair[j % 2][1][0:CAP, :], ALU.mult, ALU.mult)\
                             .then_inc(act_ready, 1)
                    split(gp, t)
                for nb in range(4):
                    v.wait_ge(ogH_ready, 4 * gp + nb + 1)
                    k = slice(nb * 512, (nb + 1) * 512)
                    v.tensor_tensor(ogL[:, k], out4[nb][0:CAP, :], ogH[:, k].bitcast(F32), ALU.subtract)\
                     .then_inc(ogL_ready, 1)

            def groups(c):
                assign(0, c)
                group(0, c, first=(c == 0))
                with v.Fori(1, NG) as g:
                    group(g, c)

            v.wait_ge(consts2, 5)
            v.wait_ge(routed, 1)
            n = v.value_load(cnt_i[0:1, 0:1], min_val=0, max_val=T)
            groups(0)
            with v.If(n > CAP):
                for c in range(1, CHUNKS):
                    groups(c)
                v.wait_ge(added, 4 * FT * (NG * CHUNKS - 1))
            v.wait_ge(added, 4 * FT * (NG - 1))
            for f in range(FT):
                for u in range(4 * f, 4 * f + 4):
                    add_part(u, last_ps, u + 1, last_added)
                v.wait_ge(last_added, 4 * f + 4)
                v.sem_inc(x1_final, 1)
                if f == 0:
                    v.wait_ge(gain_in, 16)
                else:
                    norm(3, yo_ready, True, xn, x1, (f - 1,))
            norm(3, yo_ready, True, xn, x1, (FT - 1,))


INS = ["x_prompt", "x_sample", "cache_k", "cache_v", "state_conv", "state_lru", "norm1_g", "w_in",
       "conv_w", "conv_b", "lru_wa", "lru_ba", "lru_wx", "lru_bx", "lru_lambda", "w_pa", "w_pb", "w_o",
       "norm2_g", "router_group_w", "router_group_b", "router_sub_w", "router_sub_b", "expert_w_up",
       "expert_w_down", "final_norm_g"]
OUTS = [(1, TP, D), (1, TS, D), (1, 1, TP, H, P), (1, 1, TP, H, P), (1, 1, HIST, D), (1, 1, D),
        (1, 1, TS, H, P), (1, 1, TS, H, P), (1, 1, HIST, D), (1, 1, D)]


def kernel(**inputs):
    import numpy as np
    import concourse.bacc as bacc
    from concourse.bass_utils import run_bass_kernel_spmd

    nc = bacc.Bacc("TRN2", target_bir_lowering=False, num_devices=1)
    arrays, args = {}, []
    for name in INS:
        a = np.ascontiguousarray(inputs[name])
        arrays[f"in_{name}"] = a
        args.append(nc.dram_tensor(f"in_{name}", a.shape, mybir.dt.from_np(a.dtype), kind="ExternalInput").ap())
    for i, shape in enumerate(OUTS):
        args.append(nc.dram_tensor(f"out_{i}", shape, F32, kind="ExternalOutput").ap())
    build(nc, *args)
    r = run_bass_kernel_spmd(nc, [arrays], core_ids=[0])
    return tuple(r.results[0][f"out_{i}"] for i in range(len(OUTS)))
```
